# Optimizing a Trainium2 kernel written in Bass

```python
import jax, jax.numpy as jnp
from jax import lax
import numpy as np
import math

D_MODEL = 1024
BATCH = 1
SEQ = 512
DEPTH = 2

GRID_W = 64
CTX_LEN = 256
W_CONV = D_MODEL
W_LRU = D_MODEL
W_EVEN = W_CONV + W_LRU
N_LRU_HEADS = 8
LRU_HEAD_DIM = W_LRU // N_LRU_HEADS
CONV_WIDTH = 31
CONV_PAD = (15, 15)
SHORT_CONV_WIDTH = 4
SHORT_CONV_PAD = (2, 1)
LRU_C = 8.0
W_POOL = 2 * D_MODEL
POOL_WINDOWS = (2, 4, 8, 16)
N_POOL_GROUPS = len(POOL_WINDOWS)
POOL_GROUP_DIM = W_POOL // N_POOL_GROUPS
N_EVEN = (DEPTH + 1) // 2
N_ODD = DEPTH // 2
RMS_EPS = 1e-6
LN_EPS = 1e-5


def rmsnorm(x, g):
    xf = x.astype(jnp.float32)
    y = xf * lax.rsqrt(jnp.mean(xf * xf, axis=-1, keepdims=True) + RMS_EPS)
    return (y * g.astype(jnp.float32)).astype(x.dtype)

def layernorm(x, g, b):
    xf = x.astype(jnp.float32)
    mu = jnp.mean(xf, axis=-1, keepdims=True)
    var = jnp.mean(jnp.square(xf - mu), axis=-1, keepdims=True)
    y = (xf - mu) * lax.rsqrt(var + LN_EPS) * g.astype(jnp.float32) + b.astype(jnp.float32)
    return y.astype(x.dtype)

def modulate(h, shift, scale):
    return h * (1 + scale) + shift

def depthwise_conv(u, w, b, pad):
    y = lax.conv_general_dilated(
        u, w[:, None, :].astype(u.dtype), window_strides=(1,), padding=(pad,),
        dimension_numbers=("NWC", "WIO", "NWC"), feature_group_count=u.shape[-1])
    return y + b.astype(u.dtype)

def conformer_conv(va, vg, p):
    u = va * jax.nn.sigmoid(vg)
    u = depthwise_conv(u, p["conv_w"], p["conv_b"], CONV_PAD)
    return jax.nn.silu(layernorm(u, p["ln_g"], p["ln_b"]))

def lru_coeffs(u2, p):
    bn, n = u2.shape[0], u2.shape[1]
    uf = u2.astype(jnp.float32)
    uh = uf.reshape(bn, n, 2, N_LRU_HEADS, LRU_HEAD_DIM)
    gr = jnp.einsum("bnkhi,khij->bnkhj", uh, p["w_r"].astype(jnp.float32)).reshape(bn, n, 2, W_LRU)
    gi = jnp.einsum("bnkhi,khij->bnkhj", uh, p["w_i"].astype(jnp.float32)).reshape(bn, n, 2, W_LRU)
    r = jax.nn.sigmoid(gr + p["b_r"].astype(jnp.float32))
    i = jax.nn.sigmoid(gi + p["b_i"].astype(jnp.float32))
    log_a = -LRU_C * r * jax.nn.softplus(-p["lam"].astype(jnp.float32))
    a = jnp.exp(log_a)
    bx = jnp.sqrt(-jnp.expm1(2.0 * log_a)) * (i * uf)
    return a, bx

def lru_scan(a, bx, h0, with_outputs):
    def step(h, ab):
        at, bt = ab
        h = at * h + bt
        return h, (h if with_outputs else None)
    hT, hs = lax.scan(step, h0, (jnp.swapaxes(a, 0, 1), jnp.swapaxes(bx, 0, 1)))
    return hT, hs

def rglru_branch(xb, p, h0, with_outputs):
    u = depthwise_conv(xb, p["sconv_w"], p["sconv_b"], SHORT_CONV_PAD)
    u2 = jnp.stack([u, u[:, ::-1]], axis=2)
    a, bx = lru_coeffs(u2, p)
    hT, hs = lru_scan(a, bx, h0, with_outputs)
    if not with_outputs:
        return None, hT
    y = hs[:, :, 0] + hs[::-1, :, 1]
    return jnp.swapaxes(y, 0, 1).astype(xb.dtype), hT

def even_mixer(h, h0, p):
    z = h @ p["w_in"]
    va, vg, ga, xb, gb = jnp.split(
        z, [W_CONV, 2 * W_CONV, 3 * W_CONV, 3 * W_CONV + W_LRU], axis=-1)
    y_a = conformer_conv(va, vg, p) * jax.nn.silu(ga)
    y_b, hT = rglru_branch(xb, p, h0, True)
    y_b = y_b * jax.nn.silu(gb)
    return jnp.concatenate([y_a, y_b], axis=-1) @ p["w_out"], hT

def multiscale_pool(u):
    n = u.shape[1]
    uf = u.astype(jnp.float32)
    s = jnp.pad(jnp.cumsum(uf, axis=1), ((0, 0), (1, 0), (0, 0)))
    t = jnp.arange(n)
    parts = []
    for g, w in enumerate(POOL_WINDOWS):
        lo = jnp.clip(t - w // 2, 0, n)
        hi = jnp.clip(t + w // 2, 0, n)
        sg = s[:, :, g * POOL_GROUP_DIM:(g + 1) * POOL_GROUP_DIM]
        cnt = (hi - lo).astype(jnp.float32)[None, :, None]
        parts.append((sg[:, hi] - sg[:, lo]) / cnt)
    return (jnp.concatenate(parts, axis=-1) - uf).astype(u.dtype)

def odd_mixer(h, p, on_grid):
    bn, n = h.shape[0], h.shape[1]
    z = h @ p["w_in"]
    u, g = jnp.split(z, [W_POOL], axis=-1)
    if on_grid:
        rows = n // GRID_W
        d = multiscale_pool(u.reshape(bn * rows, GRID_W, W_POOL)).reshape(bn, n, W_POOL)
    else:
        d = multiscale_pool(u)
    d = d.reshape(bn, n, N_POOL_GROUPS, POOL_GROUP_DIM)
    y = jnp.einsum("bngi,gij->bngj", d, p["w_grp"]).reshape(bn, n, W_POOL) * p["scale"]
    return (y * jax.nn.silu(g)) @ p["w_out"]

def first_inputs(seed: int = 0) -> dict:
    key = jax.random.key(seed)
    ks = jax.random.split(key, 32)
    f32 = jnp.float32

    def nrm(k, shape, s):
        return s * jax.random.normal(k, shape, f32)

    ua = jax.random.uniform(ks[20], (N_EVEN, 2, W_LRU), f32, 0.9, 0.999)
    pa = ua ** (1.0 / LRU_C)
    lam = jnp.log(pa) - jnp.log1p(-pa)
    return {
        "x": nrm(ks[0], (BATCH, SEQ, D_MODEL), 1.0),
        "c": nrm(ks[1], (BATCH, D_MODEL), 1.0),
        "ctx": nrm(ks[2], (BATCH, CTX_LEN, D_MODEL), 1.0),
        "c_ctx": nrm(ks[3], (D_MODEL,), 1.0),
        "norm_g": 1.0 + nrm(ks[4], (DEPTH, D_MODEL), 0.1),
        "mod_w": nrm(ks[5], (DEPTH, D_MODEL, 3 * D_MODEL), 0.5 * D_MODEL ** -0.5),
        "mod_b": nrm(ks[6], (DEPTH, 3 * D_MODEL), 0.02),
        "ev_w_in": nrm(ks[7], (N_EVEN, D_MODEL, 3 * W_CONV + 2 * W_LRU), D_MODEL ** -0.5),
        "ev_conv_w": nrm(ks[8], (N_EVEN, CONV_WIDTH, W_CONV), CONV_WIDTH ** -0.5),
        "ev_conv_b": nrm(ks[9], (N_EVEN, W_CONV), 0.02),
        "ev_ln_g": 1.0 + nrm(ks[10], (N_EVEN, W_CONV), 0.1),
        "ev_ln_b": nrm(ks[11], (N_EVEN, W_CONV), 0.02),
        "ev_sconv_w": nrm(ks[12], (N_EVEN, SHORT_CONV_WIDTH, W_LRU), SHORT_CONV_WIDTH ** -0.5),
        "ev_sconv_b": nrm(ks[13], (N_EVEN, W_LRU), 0.02),
        "ev_w_r": nrm(ks[14], (N_EVEN, 2, N_LRU_HEADS, LRU_HEAD_DIM, LRU_HEAD_DIM), LRU_HEAD_DIM ** -0.5),
        "ev_b_r": nrm(ks[15], (N_EVEN, 2, W_LRU), 0.02),
        "ev_w_i": nrm(ks[16], (N_EVEN, 2, N_LRU_HEADS, LRU_HEAD_DIM, LRU_HEAD_DIM), LRU_HEAD_DIM ** -0.5),
        "ev_b_i": nrm(ks[17], (N_EVEN, 2, W_LRU), 0.02),
        "ev_lam": lam,
        "ev_w_out": nrm(ks[18], (N_EVEN, W_EVEN, D_MODEL), W_EVEN ** -0.5),
        "od_w_in": nrm(ks[21], (N_ODD, D_MODEL, 2 * W_POOL), D_MODEL ** -0.5),
        "od_w_grp": nrm(ks[22], (N_ODD, N_POOL_GROUPS, POOL_GROUP_DIM, POOL_GROUP_DIM), POOL_GROUP_DIM ** -0.5),
        "od_scale": 1.0 + nrm(ks[23], (N_ODD, W_POOL), 0.1),
        "od_w_out": nrm(ks[24], (N_ODD, W_POOL, D_MODEL), W_POOL ** -0.5),
        "final_g": 1.0 + nrm(ks[25], (D_MODEL,), 0.1),
    }

def first_block(x, c, ctx, c_ctx, norm_g, mod_w, mod_b,
              ev_w_in, ev_conv_w, ev_conv_b, ev_ln_g, ev_ln_b, ev_sconv_w, ev_sconv_b,
              ev_w_r, ev_b_r, ev_w_i, ev_b_i, ev_lam, ev_w_out,
              od_w_in, od_w_grp, od_scale, od_w_out, final_g):
    bn = x.shape[0]
    sc = jax.nn.silu(c)
    scc = jax.nn.silu(c_ctx)
    for l in range(DEPTH):
        ctx_out_needed = any(j % 2 == 0 for j in range(l + 1, DEPTH))
        shift, scale, gate = jnp.split(sc @ mod_w[l] + mod_b[l], 3, axis=-1)
        hx = modulate(rmsnorm(x, norm_g[l]), shift[:, None], scale[:, None])
        if ctx_out_needed or l % 2 == 0:
            shift_c, scale_c, gate_c = jnp.split(scc @ mod_w[l] + mod_b[l], 3, axis=-1)
            hc = modulate(rmsnorm(ctx, norm_g[l]), shift_c, scale_c)
        j = l // 2
        if l % 2 == 0:
            pe = {"w_in": ev_w_in[j], "conv_w": ev_conv_w[j], "conv_b": ev_conv_b[j],
                  "ln_g": ev_ln_g[j], "ln_b": ev_ln_b[j], "sconv_w": ev_sconv_w[j],
                  "sconv_b": ev_sconv_b[j], "w_r": ev_w_r[j], "b_r": ev_b_r[j],
                  "w_i": ev_w_i[j], "b_i": ev_b_i[j], "lam": ev_lam[j], "w_out": ev_w_out[j]}
            h0 = jnp.zeros((bn, 2, W_LRU), jnp.float32)
            if ctx_out_needed:
                out_c, h_ctx = even_mixer(hc, h0, pe)
            else:
                xb_c = hc @ pe["w_in"][:, 3 * W_CONV:3 * W_CONV + W_LRU]
                _, h_ctx = rglru_branch(xb_c, pe, h0, False)
            out_x, _ = even_mixer(hx, h_ctx, pe)
        else:
            po = {"w_in": od_w_in[j], "w_grp": od_w_grp[j], "scale": od_scale[j], "w_out": od_w_out[j]}
            if ctx_out_needed:
                out_c = odd_mixer(hc, po, False)
            out_x = odd_mixer(hx, po, True)
        x = x + gate[:, None] * out_x
        if ctx_out_needed:
            ctx = ctx + gate_c * out_c
    return rmsnorm(x, final_g)


DEPTH_2 = 1

HEAD_DIM = 64
BRANCH_W = D_MODEL // 4
N_BRANCH = 4
N_HEADS = BRANCH_W // HEAD_DIM
SC_K = 3
SB_BLOCK = 128
SSM_GROUPS = 2
SSM_STATE = 64
SSM_CONV_K = 4
SSM_CHUNK = 256
SSM_CONV_DIM = BRANCH_W + 2 * SSM_GROUPS * SSM_STATE
MOBA_BLOCK = 256
MOBA_TOPK = 3
MOBA_QCHUNK = 128
SEQ_MULTIPLE = 256
FFN_HIDDEN = ((8 * D_MODEL + 3 * 256 - 1) // (3 * 256)) * 256

W_A_IN = 3 * BRANCH_W
W_B_IN = 3 * BRANCH_W
W_C_IN = BRANCH_W + SSM_CONV_DIM + N_HEADS
W_D_IN = 3 * BRANCH_W
W_G_IN = N_BRANCH * D_MODEL
IN_SPLITS = [W_A_IN, W_A_IN + W_B_IN, W_A_IN + W_B_IN + W_C_IN,
             W_A_IN + W_B_IN + W_C_IN + W_D_IN]
N_IN = W_A_IN + W_B_IN + W_C_IN + W_D_IN + W_G_IN


def rmsnorm_2(x, g):
    xf = x.astype(jnp.float32)
    y = xf * lax.rsqrt(jnp.mean(xf * xf, axis=-1, keepdims=True) + RMS_EPS)
    return (y * g.astype(jnp.float32)).astype(x.dtype)

def causal_depthwise_conv(x, w):
    k = w.shape[0]
    return lax.conv_general_dilated(
        x, w[:, None, :].astype(x.dtype), window_strides=(1,), padding=[(k - 1, 0)],
        dimension_numbers=("NWC", "WIO", "NWC"), feature_group_count=x.shape[-1])

def short_conv_mixer(u, conv_w):
    xa, b_gate, c_gate = jnp.split(u, 3, axis=-1)
    return b_gate * causal_depthwise_conv(c_gate * xa, conv_w)

def stick_breaking_attention(q, k, v):
    bsz, seq, nh, dh = q.shape
    nqb = seq // SB_BLOCK
    f32 = jnp.float32
    qs = q * (dh ** -0.5)
    within_mat = jnp.tril(jnp.ones((SB_BLOCK, SB_BLOCK), f32), -1)
    outs = []
    for c in range(nqb):
        nkb = c + 1
        kc = nkb * SB_BLOCK
        qi = qs[:, c * SB_BLOCK:(c + 1) * SB_BLOCK]
        z = jnp.einsum("bqhd,bkhd->bhqk", qi, k[:, :kc], preferred_element_type=f32)
        q_pos = c * SB_BLOCK + jnp.arange(SB_BLOCK)
        past = jnp.arange(kc)[None, :] < q_pos[:, None]
        z = jnp.where(past, z, -jnp.inf)
        sp = jax.nn.softplus(z)
        lk = sp.reshape(bsz, nh, SB_BLOCK, nkb, SB_BLOCK)
        within = jnp.einsum("bhqnj,js->bhqns", lk, within_mat)
        after_mat = jnp.tril(jnp.ones((nkb, nkb), f32), -1)
        after = jnp.einsum("bhqm,mn->bhqn", jnp.sum(lk, axis=-1), after_mat)
        between = (within + after[..., None]).reshape(bsz, nh, SB_BLOCK, kc)
        w = jnp.exp(z - sp - between)
        outs.append(jnp.einsum("bhqk,bkhd->bqhd", w.astype(v.dtype), v[:, :kc]))
    return jnp.concatenate(outs, axis=1).reshape(bsz, seq, nh * dh)

def ssd_chunked(x, a, b_in, c_in):
    bsz, seq, nh, hp = x.shape
    ng, ns = b_in.shape[2], b_in.shape[3]
    ne = nh // ng
    t = SSM_CHUNK
    nc = seq // t
    f32 = jnp.float32
    x = x.astype(f32).reshape(bsz, nc, t, ng, ne, hp)
    a = a.astype(f32).reshape(bsz, nc, t, ng, ne)
    bc = b_in.astype(f32).reshape(bsz, nc, t, ng, ns)
    cc = c_in.astype(f32).reshape(bsz, nc, t, ng, ns)
    a_cs = jnp.cumsum(a, axis=2)
    causal = jnp.tril(jnp.ones((t, t), dtype=bool))[:, :, None, None]
    seg = a_cs[:, :, :, None] - a_cs[:, :, None, :]
    decay = jnp.exp(jnp.where(causal, seg, -jnp.inf))
    cb = jnp.einsum("bclgn,bcsgn->bclsg", cc, bc)
    y_diag = jnp.einsum("bclsge,bcsgep->bclgep", cb[..., None] * decay, x)
    decay_to_end = jnp.exp(a_cs[:, :, -1:] - a_cs)
    chunk_states = jnp.einsum("bclgn,bclge,bclgep->bcgepn", bc, decay_to_end, x)
    chunk_decay = jnp.exp(a_cs[:, :, -1])

    def step(h, inp):
        s_c, d_c = inp
        return h * d_c[..., None, None] + s_c, h

    h0 = jnp.zeros((bsz, ng, ne, hp, ns), f32)
    _, h_enter = lax.scan(step, h0, (jnp.moveaxis(chunk_states, 1, 0),
                                     jnp.moveaxis(chunk_decay, 1, 0)))
    h_enter = jnp.moveaxis(h_enter, 0, 1)
    y_off = jnp.einsum("bclgn,bcgepn,bclge->bclgep", cc, h_enter, jnp.exp(a_cs))
    return (y_diag + y_off).reshape(bsz, seq, nh, hp)

def mamba2_mixer(u, conv_w, conv_b, dt_bias, a_log, d_skip, norm_g):
    bsz, seq, _ = u.shape
    z, xbc, dt = jnp.split(u, [BRANCH_W, BRANCH_W + SSM_CONV_DIM], axis=-1)
    xbc = jax.nn.silu(causal_depthwise_conv(xbc, conv_w) + conv_b)
    xs, b_in, c_in = jnp.split(xbc, [BRANCH_W, BRANCH_W + SSM_GROUPS * SSM_STATE], axis=-1)
    dt = jax.nn.softplus(dt.astype(jnp.float32) + dt_bias.astype(jnp.float32))
    a = -jnp.exp(a_log.astype(jnp.float32))
    xh = xs.reshape(bsz, seq, N_HEADS, HEAD_DIM)
    y = ssd_chunked(xh.astype(jnp.float32) * dt[..., None], dt * a,
                    b_in.reshape(bsz, seq, SSM_GROUPS, SSM_STATE),
                    c_in.reshape(bsz, seq, SSM_GROUPS, SSM_STATE))
    y = y.astype(u.dtype) + xh * d_skip[:, None]
    gsz = BRANCH_W // SSM_GROUPS
    gated = y.reshape(bsz, seq, SSM_GROUPS, gsz) * jax.nn.silu(z.reshape(bsz, seq, SSM_GROUPS, gsz))
    return rmsnorm_2(gated, norm_g.reshape(SSM_GROUPS, gsz)).reshape(bsz, seq, BRANCH_W)

def moba_head(q, k, v):
    seq, dh = q.shape
    nb = seq // MOBA_BLOCK
    ke = max(1, min(MOBA_TOPK, nb - 1))
    cq = MOBA_QCHUNK
    n_pairs = seq * ke
    n_chunks = -(-(n_pairs + (nb + 1) * (cq - 1)) // cq)
    scale = dh ** -0.5
    f32 = jnp.float32
    kblk = k.reshape(nb, MOBA_BLOCK, dh)
    vblk = v.reshape(nb, MOBA_BLOCK, dh)
    k_mean = jnp.mean(kblk.astype(f32), axis=1)
    gate = q.astype(f32) @ k_mean.T
    own = jnp.arange(seq) // MOBA_BLOCK
    gate = jnp.where(jnp.arange(nb)[None, :] < own[:, None], gate, -jnp.inf)
    _, sel = lax.top_k(gate, ke)
    valid = jnp.arange(ke)[None, :] < own[:, None]
    grp = jnp.where(valid, sel, nb).reshape(n_pairs)
    cnt = jnp.zeros((nb + 1,), jnp.int32).at[grp].add(1)
    padded = (cnt + cq - 1) // cq * cq
    pad_end = jnp.cumsum(padded)
    pad_start = pad_end - padded
    order = jnp.argsort(grp, stable=True)
    g_sorted = grp[order]
    rank = jnp.arange(n_pairs, dtype=jnp.int32) - (jnp.cumsum(cnt) - cnt)[g_sorted]
    dest = jnp.zeros((n_pairs,), jnp.int32).at[order].set(pad_start[g_sorted] + rank)
    slot_pair = jnp.full((n_chunks * cq,), -1, jnp.int32).at[dest].set(
        jnp.arange(n_pairs, dtype=jnp.int32)).reshape(n_chunks, cq)
    chunk_grp = jnp.searchsorted(pad_end, jnp.arange(n_chunks, dtype=jnp.int32) * cq, side="right")
    slot_ok = (slot_pair >= 0) & (chunk_grp < nb)[:, None]
    blk = jnp.minimum(chunk_grp, nb - 1)
    q_c = q[jnp.maximum(slot_pair, 0) // ke]
    k_c = kblk[blk]
    v_c = vblk[blk]
    s = jnp.einsum("cqd,ckd->cqk", q_c, k_c, preferred_element_type=f32) * scale
    s = jnp.where(slot_ok[..., None], s, -jnp.inf)
    m = jnp.where(slot_ok, jnp.max(s, axis=-1), 0.0)
    p = jnp.exp(s - m[..., None])
    l = jnp.sum(p, axis=-1)
    o = jnp.einsum("cqk,ckd->cqd", p.astype(v.dtype), v_c, preferred_element_type=f32)
    m_p = m.reshape(-1)[dest].reshape(seq, ke)
    l_p = l.reshape(-1)[dest].reshape(seq, ke)
    o_p = o.reshape(-1, dh)[dest].reshape(seq, ke, dh)
    s_own = jnp.einsum("nqd,nkd->nqk", q.reshape(nb, MOBA_BLOCK, dh), kblk,
                       preferred_element_type=f32) * scale
    s_own = jnp.where(jnp.tril(jnp.ones((MOBA_BLOCK, MOBA_BLOCK), dtype=bool)), s_own, -jnp.inf)
    m_own = jnp.max(s_own, axis=-1)
    p_own = jnp.exp(s_own - m_own[..., None])
    l_own = jnp.sum(p_own, axis=-1).reshape(seq)
    o_own = jnp.einsum("nqk,nkd->nqd", p_own.astype(v.dtype), vblk,
                       preferred_element_type=f32).reshape(seq, dh)
    m_own = m_own.reshape(seq)
    m_all = jnp.maximum(m_own, jnp.max(jnp.where(valid, m_p, -jnp.inf), axis=-1))
    w_p = jnp.where(valid, jnp.exp(m_p - m_all[:, None]), 0.0)
    w_own = jnp.exp(m_own - m_all)
    num = w_own[:, None] * o_own + jnp.einsum("sr,srd->sd", w_p, o_p)
    den = w_own * l_own + jnp.sum(w_p * l_p, axis=-1)
    return (num / den[:, None]).astype(q.dtype)

def moba_attention(q, k, v):
    bsz, seq, nh, dh = q.shape
    qt, kt, vt = [jnp.moveaxis(t, 2, 1) for t in (q, k, v)]
    out = lax.map(lambda a: jax.vmap(moba_head)(*a), (qt, kt, vt))
    return jnp.moveaxis(out, 1, 2).reshape(bsz, seq, nh * dh)

def hybrid_layer(x, norm1_g, w_in, conv_a_w, ssm_conv_w, ssm_conv_b, ssm_dt_bias,
                 ssm_a_log, ssm_d, ssm_norm_g, w_branch, w_o, norm2_g, w_gate_up, w_down):
    bsz, seq, _ = x.shape
    h = rmsnorm_2(x, norm1_g)
    u = h @ w_in
    u_a, u_b, u_c, u_d, u_g = jnp.split(u, IN_SPLITS, axis=-1)
    y_a = short_conv_mixer(u_a, conv_a_w)
    q_b, k_b, v_b = [t.reshape(bsz, seq, N_HEADS, HEAD_DIM) for t in jnp.split(u_b, 3, axis=-1)]
    y_b = stick_breaking_attention(q_b, k_b, v_b)
    y_c = mamba2_mixer(u_c, ssm_conv_w, ssm_conv_b, ssm_dt_bias, ssm_a_log, ssm_d, ssm_norm_g)
    q_d, k_d, v_d = [t.reshape(bsz, seq, N_HEADS, HEAD_DIM) for t in jnp.split(u_d, 3, axis=-1)]
    y_d = moba_attention(q_d, k_d, v_d)
    gates = jax.nn.sigmoid(u_g.reshape(bsz, seq, N_BRANCH, D_MODEL))
    branches = [y_a, y_b, y_c, y_d]
    merged = gates[:, :, 0] * (branches[0] @ w_branch[0])
    for i in range(1, N_BRANCH):
        merged = merged + gates[:, :, i] * (branches[i] @ w_branch[i])
    x = x + merged @ w_o
    h2 = rmsnorm_2(x, norm2_g)
    g_ff, up_ff = jnp.split(h2 @ w_gate_up, 2, axis=-1)
    return x + (jax.nn.silu(g_ff) * up_ff) @ w_down

def second_inputs(seed: int = 0) -> dict:
    key = jax.random.key(seed)
    ks = jax.random.split(key, 17)
    f32 = jnp.float32

    def nrm(k, shape, scale):
        return jax.random.normal(k, shape, f32) * scale

    dt0 = jnp.exp(jax.random.uniform(ks[6], (DEPTH_2, N_HEADS), f32, math.log(1e-3), math.log(1e-1)))
    return {
        "x": nrm(ks[0], (BATCH, SEQ, D_MODEL), 1.0),
        "norm1_g": 1.0 + nrm(ks[1], (DEPTH_2, D_MODEL), 0.02),
        "w_in": nrm(ks[2], (DEPTH_2, D_MODEL, N_IN), D_MODEL ** -0.5),
        "conv_a_w": nrm(ks[3], (DEPTH_2, SC_K, BRANCH_W), SC_K ** -0.5),
        "ssm_conv_w": nrm(ks[4], (DEPTH_2, SSM_CONV_K, SSM_CONV_DIM), SSM_CONV_K ** -0.5),
        "ssm_conv_b": nrm(ks[5], (DEPTH_2, SSM_CONV_DIM), 0.02),
        "ssm_dt_bias": dt0 + jnp.log(-jnp.expm1(-dt0)),
        "ssm_a_log": jnp.log(jax.random.uniform(ks[7], (DEPTH_2, N_HEADS), f32, 1.0, 16.0)),
        "ssm_d": 1.0 + nrm(ks[8], (DEPTH_2, N_HEADS), 0.1),
        "ssm_norm_g": 1.0 + nrm(ks[9], (DEPTH_2, BRANCH_W), 0.02),
        "w_branch": nrm(ks[10], (DEPTH_2, N_BRANCH, BRANCH_W, D_MODEL), BRANCH_W ** -0.5),
        "w_o": nrm(ks[11], (DEPTH_2, D_MODEL, D_MODEL), D_MODEL ** -0.5),
        "norm2_g": 1.0 + nrm(ks[12], (DEPTH_2, D_MODEL), 0.02),
        "w_gate_up": nrm(ks[13], (DEPTH_2, D_MODEL, 2 * FFN_HIDDEN), D_MODEL ** -0.5),
        "w_down": nrm(ks[14], (DEPTH_2, FFN_HIDDEN, D_MODEL), FFN_HIDDEN ** -0.5),
        "final_g": 1.0 + nrm(ks[15], (D_MODEL,), 0.02),
    }

def second_block(x, norm1_g, w_in, conv_a_w, ssm_conv_w, ssm_conv_b, ssm_dt_bias, ssm_a_log,
              ssm_d, ssm_norm_g, w_branch, w_o, norm2_g, w_gate_up, w_down, final_g):
    seq = x.shape[1]
    seq_pad = -(-seq // SEQ_MULTIPLE) * SEQ_MULTIPLE
    h = jnp.pad(x, ((0, 0), (0, seq_pad - seq), (0, 0)))
    for l in range(DEPTH_2):
        h = hybrid_layer(h, norm1_g[l], w_in[l], conv_a_w[l], ssm_conv_w[l], ssm_conv_b[l],
                         ssm_dt_bias[l], ssm_a_log[l], ssm_d[l], ssm_norm_g[l], w_branch[l],
                         w_o[l], norm2_g[l], w_gate_up[l], w_down[l])
    return rmsnorm_2(h, final_g)[:, :seq]


def setup_inputs(seed=0):
    out = dict(first_inputs(seed))
    for name, value in second_inputs(seed + 1).items():
        if name != "x":
            out[name + "_2"] = value
    return out


def reference(
    x, c, ctx, c_ctx, norm_g, mod_w, mod_b, ev_w_in, ev_conv_w, ev_conv_b, ev_ln_g, ev_ln_b,
    ev_sconv_w, ev_sconv_b, ev_w_r, ev_b_r, ev_w_i, ev_b_i, ev_lam, ev_w_out, od_w_in, od_w_grp,
    od_scale, od_w_out, final_g, norm1_g_2, w_in_2, conv_a_w_2, ssm_conv_w_2, ssm_conv_b_2,
    ssm_dt_bias_2, ssm_a_log_2, ssm_d_2, ssm_norm_g_2, w_branch_2, w_o_2, norm2_g_2,
    w_gate_up_2, w_down_2, final_g_2,
):
    x = first_block(
        x, c, ctx, c_ctx, norm_g, mod_w, mod_b, ev_w_in, ev_conv_w, ev_conv_b, ev_ln_g, ev_ln_b,
        ev_sconv_w, ev_sconv_b, ev_w_r, ev_b_r, ev_w_i, ev_b_i, ev_lam, ev_w_out, od_w_in,
        od_w_grp, od_scale, od_w_out, final_g,
    )
    return second_block(
        x, norm1_g_2, w_in_2, conv_a_w_2, ssm_conv_w_2, ssm_conv_b_2, ssm_dt_bias_2,
        ssm_a_log_2, ssm_d_2, ssm_norm_g_2, w_branch_2, w_o_2, norm2_g_2, w_gate_up_2, w_down_2,
        final_g_2,
    )


_drawn_inputs = setup_inputs


def setup_inputs(seed=0):
    import zlib

    import numpy as np

    out = dict(_drawn_inputs(seed))
    spreads = {}
    factors = {'ev_conv_b': 8.0,
     'ev_ln_g': 4.342,
     'ev_ln_b': 8.0,
     'ev_b_r': 8.0,
     'ev_b_i': 8.0,
     'ssm_conv_b_2': 5.173,
     'ssm_d_2': 8.0,
     'ssm_norm_g_2': 7.145,
     'norm2_g_2': 4.775,
     'final_g_2': 2.884}
    for name, (base, spread) in spreads.items():
        noise = np.random.default_rng([zlib.crc32(name.encode()), seed]).standard_normal(out[name].shape)
        drawn = base * np.exp(spread * noise) if base else spread * noise
        out[name] = __import__('jax').numpy.asarray(drawn.astype(out[name].dtype))
    for name, factor in factors.items():
        out[name] = (out[name] * factor).astype(out[name].dtype)
    return out
```

```python
import numpy as np
import concourse.bass as bass
from concourse import mybir
from contextlib import ExitStack, contextmanager

P = 128
D = 1024
T = 512
TC = 256
NT = D // P
NB = T // P
RING = 4
AHEAD = 3
KC = 8
CW = KC * P
CONV_K, SCONV_K, SSM_K, SHORT_K = 31, 4, 4, 3
HALO = CONV_K // 2
FFN_TILES = 22
HD = 64
NH = 4
ROW = 64
POOL_LEVELS = 4
F32, F32R = mybir.dt.float32, mybir.dt.float32r
ALU, ACT, AX = mybir.AluOpType, mybir.ActivationFunctionType, mybir.AxisListType

CAUSAL = NB * (NB + 1) // 2 * P
OFF = {0: 0, 1: 512, 3: 896, 2: 1024}


def vector_columns():
    at, cols = 0, {}
    for name, n in (
        ("c", NT), ("c_ctx", NT), ("norm_g", 2 * NT), ("mod_b", 2 * 3 * NT),
        ("conv_w", NT * CONV_K), ("conv_b", NT), ("ln_g", NT), ("ln_b", NT),
        ("sconv_w", NT * SCONV_K), ("sconv_b", NT), ("b_r", 2 * NT), ("b_i", 2 * NT), ("lam", 2 * NT),
        ("od_scale", 2 * NT), ("final_g", NT), ("norm1_g", NT), ("conv_a_w", 2 * SHORT_K),
        ("ssm_conv_w", 4 * SSM_K), ("ssm_conv_b", 4), ("dt_bias", NB * NH), ("a_log", NB * NH),
        ("ssm_d", 2), ("ssm_norm_g", 2), ("norm2_g", NT), ("final_g2", NT), ("w_dt", NT * NH),
    ):
        cols[name] = at
        at += n
    return cols, at


VC, NVEC = vector_columns()
LOOPS = {
    'va': {
        "per": {'v': 18, 'a': 13, 'mod': 1},
        "back": {'xp': ('a', 1), 'conv': ('v', 4), 'sig': ('a', 3), 'uu': ('v', 6), 'gates': ('mm', 4), 'gate_read': ('a', 9), 'scans': ('v', 16)},
    },
    'heads': {
        "per": {'v': 51, 'a': 15, 'mod': 3},
        "back": {'xp': ('a', 1), 'conv': ('v', 12), 'sgb': ('v', 22), 'sga': ('v', 23), 'gates': ('mm', 4), 'gate_read': ('a', 10), 'scans': ('v', 41), 'taps': ('v', 50), 'yb_lo': ('v', 51)},
    },
    'ev_out': {
        "per": {'v': 2},
        "back": {'res0': ('v', 1), 'res1': ('v', 2)},
    },
    'pool': {
        "per": {'v': 28, 'a': 8},
        "back": {'l0': ('a', 1), 'sub0': ('v', 6), 'l1': ('a', 3), 'sub1': ('v', 13), 'l2': ('a', 5), 'sub2': ('v', 20), 'l3': ('a', 7), 'sub3': ('v', 27)},
    },
    'group': {
        "per": {'v': 16, 'a': 16},
        "back": {'y0_0': ('v', 1), 'lo0_0': ('v', 2), 'y1_0': ('v', 3), 'lo1_0': ('v', 4), 'y2_0': ('v', 5), 'lo2_0': ('v', 6), 'y3_0': ('v', 7), 'lo3_0': ('v', 8), 'y0_1': ('v', 9), 'lo0_1': ('v', 10), 'y1_1': ('v', 11), 'lo1_1': ('v', 12), 'y2_1': ('v', 13), 'lo2_1': ('v', 14), 'y3_1': ('v', 15), 'lo3_1': ('v', 16)},
    },
    'od_out': {
        "per": {'v': 2},
        "back": {'res0': ('v', 1), 'res1': ('v', 2)},
    },
    'merge': {
        "per": {'v': 32, 'a': 20},
        "back": {'sg0_0': ('a', 1), 'pr0_0': ('v', 1), 'sg0_1': ('a', 2), 'pr0_1': ('v', 3), 'sg0_2': ('a', 3), 'pr0_2': ('v', 5), 'sg0_3': ('a', 4), 'pr0_3': ('v', 7), 'lo0': ('v', 8), 'sg1_0': ('a', 6), 'pr1_0': ('v', 9), 'sg1_1': ('a', 7), 'pr1_1': ('v', 11), 'sg1_2': ('a', 8), 'pr1_2': ('v', 13), 'sg1_3': ('a', 9), 'pr1_3': ('v', 15), 'lo1': ('v', 16), 'sg2_0': ('a', 11), 'pr2_0': ('v', 17), 'sg2_1': ('a', 12), 'pr2_1': ('v', 19), 'sg2_2': ('a', 13), 'pr2_2': ('v', 21), 'sg2_3': ('a', 14), 'pr2_3': ('v', 23), 'lo2': ('v', 24), 'sg3_0': ('a', 16), 'pr3_0': ('v', 25), 'sg3_1': ('a', 17), 'pr3_1': ('v', 27), 'sg3_2': ('a', 18), 'pr3_2': ('v', 29), 'sg3_3': ('a', 19), 'pr3_3': ('v', 31), 'lo3': ('v', 32)},
    },
    'w_o': {
        "per": {'v': 4},
        "back": {'res0': ('v', 1), 'res1': ('v', 2), 'res2': ('v', 3), 'res3': ('v', 4)},
    },
    'ffn_in': {
        "per": {'v': 4, 'a': 4},
        "back": {'up0': ('v', 1), 'flo0': ('v', 2), 'up1': ('v', 3), 'flo1': ('v', 4)},
    },
    'ffn_out': {
        "per": {'v': 4},
        "back": {'res0': ('v', 1), 'res1': ('v', 2), 'res2': ('v', 3), 'res3': ('v', 4)},
    },
}
CC = {"ident": 0, "ones": 128, "inv_cnt": 256, "tri_ones": 512, "after": 1024, "past": 1152, "neg": 1280}
NCONST = 1408
N_CHUNKS = 32 + 32 + 16 + 16 + 24 + 16 + 24 + 40 + 8 + 44 + 24


class Counter:

    def __init__(self, sem):
        self.sem, self.n, self.loop = sem, 0, None

    def lead(self, engine, n):
        engine.sem_inc(self.sem, n)
        self.n += n

    def on(self, instruction):
        instruction.then_inc(self.sem, 1)
        self.n += 1
        return Mark(self, self.n, self.loop)


class Mark:
    def __init__(self, counter, n, loop):
        self.counter, self.n, self.loop = counter, n, loop

    def prev(self):
        return Mark(self.counter, self.n - self.loop.per[self.counter], self.loop)

    def value(self):
        if self.loop is None:
            return self.n
        per = self.loop.per[self.counter]
        if self.loop.done:
            return self.n + per * (self.loop.count - 1)
        return self.n + self.loop.i * per


class Loop:

    def __init__(self, i, count, per, back, counters, starts):
        self.i, self.count, self.per, self.done = i, count, per, False
        self.back_at, self.counters, self.starts, self.noted = back, counters, starts, {}

    def back(self, name):
        if name not in self.back_at:
            return None
        which, k = self.back_at[name]
        c = self.counters[which]
        return Mark(c, self.starts[c] + k - self.per[c], self)

    def note(self, name, mark):
        which = next(k for k, c in self.counters.items() if c is mark.counter)
        self.noted[name] = (which, mark.n - self.starts[mark.counter])
        return mark


def program(nc, wts, modw, vecs, consts, x_in, ctx_in, out):
    ctx = ExitStack()
    base0 = (nc.sbuf_base + 31) // 32 * 32
    K = 1024

    def at(name, cols, off, dt=F32):
        return nc.alloc_sbuf_tensor_at(name, [P, cols], dt, offset=base0 + off)

    raw = at("raw", RING * CW, 0)
    w_hi = at("w_hi", RING * CW, 16 * K, F32R)
    w_lo = at("w_lo", RING * CW, 32 * K, F32R)
    X = at("X", NT * T, 48 * K)
    h_hi = at("h_hi", NT * T, 64 * K, F32R)
    h_lo = at("h_lo", NT * T, 80 * K, F32R)
    vec = at("vec", NVEC, 96 * K)
    o_small = 96 * K + (4 * NVEC + 31) // 32 * 32
    small = at("small", 384, o_small)
    o_cst = o_small + 4 * 384
    cst = at("cst", 512, o_cst)
    cst2 = at("cst2", NCONST - 512, o_cst + 2048)
    area = (o_cst + 2048 + 31) // 32 * 32
    area2 = area + 4 * (NCONST - 512)
    limit = nc.sbuf_usable_end - base0

    class Plan:

        def __init__(self, start):
            self.at = start

        def __call__(self, name, cols, dt=F32):
            t = at(name, cols, self.at, dt)
            self.at += (4 * cols + 31) // 32 * 32
            assert self.at <= limit, (name, self.at, limit)
            return t

    banks = ctx.enter_context(nc.psum_tensor("banks", [P, 8 * 512], F32))

    def bank(b, w=512, o=0):
        return banks[:, b * 512 + o:b * 512 + o + w]

    def sem(name):
        return ctx.enter_context(nc.semaphore(name))

    s_raw = [sem(f"s_raw{s}") for s in range(RING)]
    s_vec, s_x, s_ctx, s_cst = sem("s_vec"), sem("s_x"), sem("s_ctx"), sem("s_cst")
    s_cst2 = sem("s_cst2")
    s_mod0 = [sem(f"s_mod0_{j}") for j in range(4)]
    s_mraw = [sem(f"s_mraw{s}") for s in range(3)]
    s_out = sem("s_out")
    chunk_hi = Counter(sem("s_hi"))
    chunk_lo = Counter(sem("s_lo"))
    chunk_mm = Counter(sem("s_mm"))
    mod_mm = Counter(sem("s_mod_mm"))
    pe_done = Counter(sem("s_pe"))
    v_done = Counter(sem("s_v"))
    a_done = Counter(sem("s_a"))
    counters = (chunk_hi, chunk_lo, chunk_mm, mod_mm, pe_done, v_done, a_done)

    chunk_mm.lead(nc.tensor, RING)
    mod_mm.lead(nc.tensor, 3)

    state = {"loop": None, "chunk": 0, "split": 0}

    def after(engine, *marks):
        for m in marks:
            if m is not None:
                engine.wait_ge(m.counter.sem, m.value())

    def V(ins):
        return v_done.on(ins)

    def A(ins):
        return a_done.on(ins)

    vector, scalar, tensor = nc.vector, nc.scalar, nc.tensor

    def vop(fn, *args, needs=(), **kw):
        after(vector, *needs)
        return V(fn(*args, **kw))

    def aop(out_ap, in_ap, func, needs=(), **kw):
        after(scalar, *needs)
        return A(scalar.activation(out_ap, in_ap, func, **kw))

    def tt(o, a, b, op, needs=()):
        return vop(vector.tensor_tensor, o, a, b, op, needs=needs)

    def ts(o, a, s1, s2, op0, op1=None, needs=()):
        if op1 is None:
            return vop(vector.tensor_scalar, o, a, s1, None, op0, needs=needs)
        return vop(vector.tensor_scalar, o, a, s1, s2, op0, op1, needs=needs)

    def stt(o, a, s, b, op0, op1, needs=()):
        return vop(vector.scalar_tensor_tensor, o, a, s, b, op0, op1, needs=needs)

    named = {"pe": pe_done, "v": v_done, "a": a_done, "mod": mod_mm, "mm": chunk_mm}

    @contextmanager
    def loop(name, count, chunks=0):
        table = LOOPS.get(name, {"per": {}, "back": {}})
        rise = {c: 0 for c in counters}
        for c in (chunk_hi, chunk_lo, chunk_mm):
            rise[c] = chunks
        for k, n in table["per"].items():
            rise[named[k]] = n
        starts = {c: c.n for c in counters}
        c0, s0 = state["chunk"], state["split"]
        assert chunks % RING == 0
        v_all, a_all = Mark(v_done, v_done.n, None), Mark(a_done, a_done.n, None)
        after(tensor, v_all, a_all)
        after(scalar, v_all)
        after(vector, a_all)
        with nc.Fori(0, count) as i:
            lp = Loop(i, count, rise, table["back"], named, starts)
            state["loop"] = lp
            for c in counters:
                c.loop = lp
            yield lp
        found = {k: c.n - starts[c] for k, c in named.items() if k != "mm" and c.n > starts[c]}
        found = {"per": found, "back": lp.noted}
        assert found == table, f"LOOPS[{name!r}] = {found}"
        assert state["chunk"] - c0 == chunks and state["split"] - s0 == chunks
        lp.done = True
        state["loop"] = None
        for c in counters:
            c.loop = None
            c.n = starts[c] + count * rise[c]
        state["chunk"] = c0 + count * chunks
        state["split"] = s0 + count * chunks

    def moving(n, per_chunk=1):
        lp = state["loop"]
        if lp is None or not lp.per[chunk_mm]:
            return n
        return n + lp.i * (lp.per[chunk_mm] * per_chunk)

    def split_next():
        c = state["split"]
        last = c >= N_CHUNKS
        state["split"] += 1
        if last:
            return
        s = c % RING
        lp = state["loop"]
        turn = 16 * (c // RING + 1)
        if lp is not None:
            turn = turn + lp.i * (16 * lp.per[chunk_mm] // RING)
        scalar.wait_ge(s_raw[s], turn)
        if c >= RING:
            scalar.wait_ge(chunk_mm.sem, moving(c + 1))
        chunk_hi.on(scalar.activation(w_hi[:, s * CW:(s + 1) * CW], raw[:, s * CW:(s + 1) * CW], ACT.Copy))
        vector.wait_ge(chunk_hi.sem, moving(c + 1))
        chunk_lo.on(vector.tensor_tensor(w_lo[:, s * CW:(s + 1) * CW], raw[:, s * CW:(s + 1) * CW],
                                         w_hi[:, s * CW:(s + 1) * CW].bitcast(F32), ALU.subtract))

    def chunk(groups, needs=(), swap=False):
        split_next()
        c = state["chunk"]
        state["chunk"] += 1
        s = c % RING
        tensor.wait_ge(chunk_lo.sem, moving(c + 1))
        after(tensor, *needs)
        last = None
        for o, parts, start, stop in groups:
            for n, (b, r_hi, r_lo) in enumerate(parts):
                if swap:
                    hi = w_hi[:, s * CW + b * 256:s * CW + (b + 1) * 256]
                    lo = w_lo[:, s * CW + b * 256:s * CW + (b + 1) * 256]
                    passes = ((r_hi, hi), (r_hi, lo), (r_lo, hi))
                else:
                    hi = w_hi[:, s * CW + b * P:s * CW + (b + 1) * P]
                    lo = w_lo[:, s * CW + b * P:s * CW + (b + 1) * P]
                    passes = ((hi, r_hi), (hi, r_lo), (lo, r_hi))
                for j, (l, r) in enumerate(passes):
                    last = tensor.matmul(o, l, r, start=start and n == 0 and j == 0,
                                         stop=stop and n == len(parts) - 1 and j == 2)
        return chunk_mm.on(last)

    def parts(hi, lo, k0=0, n=KC, w=T, b0=0):
        return [(b0 + k, hi[:, (k0 + k) * w:(k0 + k + 1) * w], lo[:, (k0 + k) * w:(k0 + k + 1) * w]) for k in range(n)]

    def full(o, hi, lo, w=T):
        return [(o, parts(hi, lo, w=w), True, True)]

    def tile(t, f, w=T, stride=None, o=0):
        stride = w if stride is None else stride
        if isinstance(f, int):
            return t[:, f * stride + o:f * stride + o + w]
        return t[:, bass.ds(f * stride + o, w)]

    def col(name, k=0):
        k = VC[name] + k
        return vec[:, k:k + 1] if isinstance(k, int) else vec[:, bass.ds(k, 1)]

    ident, ones = cst[:, 0:P], cst[:, P:2 * P]

    nc.gpsimd.dma_start(vec[:, :], vecs).then_inc(s_vec, 16)
    scalar.dma_start(X[:, :], x_in).then_inc(s_x, 16)
    nc.gpsimd.dma_start(cst[:, :], consts[:, 0:512]).then_inc(s_cst, 16)

    p = Plan(area)
    U = p("U", (NT + 1) * (T + 2 * HALO))
    hc_hi = p("hc_hi", NT * TC, F32R)
    o_sga = p.at - 4 * NT * TC
    hc_lo = p("hc_lo", NT * TC, F32R)
    sga = at("sga", NT * T, o_sga)
    o_yb = p.at
    yb_hi = p("yb_hi", NT * T, F32R)
    yb_lo = p("yb_lo", NT * T, F32R)
    mraw = p("mraw", 3 * CW)
    xp = p("xp", T + SCONV_K)
    u = p("u", T)
    u_hi = p("u_hi", T, F32R)
    u_lo = p("u_lo", T, F32R)
    tr = [p(f"tr{k}", T) for k in range(2)]
    ti = [p(f"ti{k}", T) for k in range(2)]
    aa = [p(f"aa{k}", T) for k in range(2)]
    th = [p(f"th{k}", T) for k in range(2)]
    tg = p("tg", T)
    mod0 = at("mod0", 16 * CW, o_yb - 16 * K)
    ctx_x = at("ctx_x", NT * TC, area)
    sq = at("sq", T, area + 8 * K)
    sq2 = at("sq2", T, area + 10 * K)
    rstd = at("rstd", T, area + 12 * K)
    assert o_yb - 16 * K >= area + 14 * K and o_yb + 48 * K <= limit

    nc.gpsimd.dma_start(ctx_x[:, :], ctx_in).then_inc(s_ctx, 16)
    csil = small[:, 0:2 * NT]
    modv0 = small[:, 16:64]
    modv1 = small[:, 64:88]
    g0, g0c, g1 = small[:, 88:96], small[:, 96:104], small[:, 104:112]
    sp4, nsp4 = small[:, 112:128], small[:, 128:144]
    hb_r, hb_i = small[:, 144:160], small[:, 160:176]
    ctx_state = small[:, 176:192]
    tmp16 = [small[:, 192 + 16 * j:208 + 16 * j] for j in range(6)]
    wdt_hi = at("wdt_hi", NT * NH, o_small + 4 * 288, F32R)
    wdt_lo = at("wdt_lo", NT * NH, o_small + 4 * 320, F32R)
    eps_rms, eps_ln = small[:, 352:353], small[:, 353:354]

    for j in range(4):
        scalar.dma_start(mod0[:, j * 4 * CW:(j + 1) * 4 * CW].rearrange("p (a n) -> p a n", a=4),
                         modw[4 * j:4 * j + 4, :, :].rearrange("a p n -> p a n")).then_inc(s_mod0[j], 16)

    for s in range(RING):
        nc.sync.dma_start(raw[:, s * CW:(s + 1) * CW], wts[s, :, :]).then_inc(s_raw[s], 16)
    with nc.sync.Fori(0, N_CHUNKS // RING - 1) as it:
        for s in range(RING):
            nc.sync.wait_ge(chunk_lo.sem, it * RING + s + 1)
            nc.sync.dma_start(raw[:, s * CW:(s + 1) * CW],
                              wts[bass.ds(it * RING + s + RING, 1), :, :].rearrange("a p n -> p (a n)")).then_inc(s_raw[s], 16)

    m_z = vop(vector.memset, small[:, :], 0.0)
    m_e = vop(vector.memset, eps_rms, 1e-6, needs=(m_z,))
    m_e = vop(vector.memset, eps_ln, 1e-5, needs=(m_e,))
    scalar.wait_ge(s_vec, 16)
    vector.wait_ge(s_vec, 16)
    cs3 = csil.rearrange("p (k two) -> p k two", two=2)
    aop(cs3[:, :, 0:1], vec[:, VC["c"]:VC["c"] + NT].rearrange("p (k a) -> p k a", a=1), ACT.Silu, needs=(m_z,))
    m_c = aop(cs3[:, :, 1:2], vec[:, VC["c_ctx"]:VC["c_ctx"] + NT].rearrange("p (k a) -> p k a", a=1), ACT.Silu)

    def softplus16(dst, src, negate, needs):
        z, e, s, s2, acc, t = tmp16
        m = ts(z, src, -1.0 if negate else 1.0, None, ALU.mult, needs=needs)
        m = aop(e, z, ACT.Abs, needs=(m,))
        m_x = aop(e, e, ACT.Exp, scale=-1.0, needs=(m,))
        m = ts(t, e, 2.0, None, ALU.add, needs=(m_x,))
        m = vop(vector.reciprocal, t, t, needs=(m,))
        m = tt(s, e, t, ALU.mult, needs=(m,))
        m = tt(s2, s, s, ALU.mult, needs=(m,))
        m = ts(acc, s2, 1.0 / 15, None, ALU.mult, needs=(m,))
        for k in (13, 11, 9, 7, 5, 3):
            m = stt(acc, acc, 1.0 / k, s2, ALU.add, ALU.mult, needs=(m,))
        m = stt(acc, acc, 1.0, s, ALU.add, ALU.mult, needs=(m,))
        m = ts(z, z, 0.0, None, ALU.max, needs=(m,))
        return stt(dst, acc, 2.0, z, ALU.mult, ALU.add, needs=(m,))

    lam = vec[:, VC["lam"]:VC["lam"] + 16]
    m = softplus16(sp4, lam, True, (m_e,))
    m = ts(nsp4, sp4, -4.0, None, ALU.mult, needs=(m,))
    m = ts(sp4, sp4, 4.0, None, ALU.mult, needs=(m,))
    ts(hb_r, vec[:, VC["b_r"]:VC["b_r"] + 16], 0.5, None, ALU.mult)
    m_small = ts(hb_i, vec[:, VC["b_i"]:VC["b_i"] + 16], 0.5, None, ALU.mult, needs=(m,))
    wdt = vec[:, VC["w_dt"]:VC["w_dt"] + NT * NH]
    m = aop(wdt_hi[:, :], wdt, ACT.Copy)
    tt(wdt_lo[:, :], wdt, wdt_hi[:, :].bitcast(F32), ALU.subtract, needs=(m,))

    def square_sum(src, w, b, needs, n=NT, stride=None):
        bufs, used = (sq, sq2), [None, None]
        for k in range(n):
            m = aop(bufs[k % 2][:, 0:w], tile(src, k, w, stride), ACT.Square, needs=(*needs, used[k % 2]))
            after(tensor, m)
            used[k % 2] = m = pe_done.on(tensor.matmul(bank(b, w), ones, bufs[k % 2][:, 0:w], start=k == 0, stop=k == n - 1))
        return m

    def rms_rstd(dst, b, w, eps, n, needs):
        m = aop(dst, bank(b, w), ACT.Sqrt, bias=eps, scale=1.0 / n, needs=needs)
        return vop(vector.reciprocal, dst, dst, needs=(m,))

    tensor.wait_ge(s_cst, 16)
    scalar.wait_ge(s_x, 16)
    vector.wait_ge(s_x, 16)
    m = square_sum(X, T, 0, (m_e,))
    m_rx = rms_rstd(rstd[:, :], 0, T, eps_rms, D, (m,))
    scalar.wait_ge(s_ctx, 16)
    vector.wait_ge(s_ctx, 16)
    m = square_sum(ctx_x, TC, 1, ())
    rstd_c = tr[0]
    m_rc = rms_rstd(rstd_c[:, 0:TC], 1, TC, eps_rms, D, (m,))

    after(tensor, m_c)
    for j in range(16):
        if j % 4 == 0:
            tensor.wait_ge(s_mod0[j // 4], 16)
        for k in range(KC):
            last = tensor.matmul(bank(2, 2, 2 * j), mod0[:, j * CW + k * P:j * CW + (k + 1) * P],
                                 csil[:, 2 * k:2 * k + 2], start=k == 0, stop=k == KC - 1)
    m = pe_done.on(last)

    def bias_mod(tiles, t0, b, two, dst, layer, needs):
        mb = vec[:, VC["mod_b"] + 24 * layer + t0:VC["mod_b"] + 24 * layer + t0 + tiles].rearrange("p (k a) -> p k a", a=1)
        for j in range(two):
            d = dst[:, t0 * two:(t0 + tiles) * two].rearrange("p (k a) -> p k a", a=two)[:, :, j:j + 1]
            s = bank(b, tiles * 2, t0 * 2).rearrange("p (k a) -> p k a", a=2)[:, :, j:j + 1]
            m = tt(d, s, mb, ALU.add, needs=needs)
        return m

    m = bias_mod(16, 0, 2, 2, modv0, 0, (m, m_small))
    mv0 = modv0.rearrange("p (k two) -> p k two", two=2)
    ng = lambda l: vec[:, VC["norm_g"] + NT * l:VC["norm_g"] + NT * (l + 1)].rearrange("p (k a) -> p k a", a=1)
    stt(g0.rearrange("p (k a) -> p k a", a=1), mv0[:, 8:16, 0:1], 1.0, ng(0), ALU.add, ALU.mult, needs=(m,))
    m_g0 = stt(g0c.rearrange("p (k a) -> p k a", a=1), mv0[:, 8:16, 1:2], 1.0, ng(0), ALU.add, ALU.mult)

    def norm_split(src, w, r, gain, shift, hi, lo, tmps, needs, n=NT):
        used = [None, None]
        for k in range(n):
            t = tmps[k % 2]
            m1 = stt(t[:, 0:w], tile(src, k, w), gain(k), r, ALU.mult, ALU.mult, needs=(*needs, used[k % 2]))
            if shift is None:
                m2 = aop(tile(hi, k, w), t[:, 0:w], ACT.Copy, needs=(m1,))
                m3 = tt(tile(lo, k, w), t[:, 0:w], tile(hi, k, w).bitcast(F32), ALU.subtract, needs=(m2,))
            else:
                m2 = aop(tile(hi, k, w), t[:, 0:w], ACT.Identity, bias=shift(k), needs=(m1,))
                m3 = stt(tile(lo, k, w), t[:, 0:w], shift(k), tile(hi, k, w).bitcast(F32), ALU.add, ALU.subtract, needs=(m2,))
            used[k % 2] = m3
        return m3

    m_hc = norm_split(ctx_x, TC, rstd_c[:, 0:TC], lambda k: g0c[:, k:k + 1], lambda k: modv0[:, 2 * k + 1:2 * k + 2],
                      hc_hi, hc_lo, (u, tg), (m_g0,))
    m_h = norm_split(X, T, rstd[:, :], lambda k: g0[:, k:k + 1], lambda k: modv0[:, 2 * k:2 * k + 1],
                     h_hi, h_lo, (u, tg), ())

    UW = T + 2 * HALO
    vop(vector.memset, U[:, :], 0.0, needs=(m_h,))
    vop(vector.memset, xp[:, :], 0.0)
    m_zero = vop(vector.memset, ctx_state, 0.0)
    for _ in range(AHEAD):
        split_next()

    m_start = (m_zero, m_h, m_hc)

    def mod_chunk(slot, turn, o, needs=()):
        tensor.wait_ge(s_mraw[slot], turn)
        after(tensor, *needs)
        for k in range(KC):
            last = tensor.matmul(o, mraw[:, slot * CW + k * P:slot * CW + (k + 1) * P],
                                 csil[:, 2 * k:2 * k + 2], start=k == 0, stop=k == KC - 1)
        return mod_mm.on(last)

    def head_input(i, w, xb_bank, m_xb, lp):
        m_xp = lp.note("xp", aop(xp[:, 2:2 + w], xb_bank, ACT.Copy, needs=(m_xb, lp.back("conv"))))
        sw = lambda k: col("sconv_w", i * SCONV_K + k)
        m = ts(u[:, 0:w], xp[:, 0:w], sw(0), col("sconv_b", i), ALU.mult, ALU.add, needs=(m_xp,))
        for k in range(1, SCONV_K):
            m = stt(u[:, 0:w], xp[:, k:k + w], sw(k), u[:, 0:w], ALU.mult, ALU.add, needs=(m,))
        lp.note("conv", m)
        m = aop(u_hi[:, 0:w], u[:, 0:w], ACT.Copy, needs=(m, lp.back("gates")))
        return tt(u_lo[:, 0:w], u[:, 0:w], u_hi[:, 0:w].bitcast(F32), ALU.subtract, needs=(m,))

    def head_scan(i, w, m_gates, gates, init, lp):
        m_t, m_iu, res = [], [], []
        for k in range(2):
            c = i * 2 + k
            at_c = lambda o: small[:, bass.ds(o + c, 1)]
            m_r = aop(tr[k][:, 0:w], gates[2 * k], ACT.Tanh, bias=at_c(144), scale=0.5, needs=(m_gates, lp.back("scans")))
            m_i = aop(ti[k][:, 0:w], gates[2 * k + 1], ACT.Tanh, bias=at_c(160), scale=0.5)
            m_a = aop(aa[k][:, 0:w], tr[k][:, 0:w], ACT.Exp, bias=at_c(128), scale=at_c(128), needs=(m_r,))
            m_h = aop(th[k][:, 0:w], tr[k][:, 0:w], ACT.Tanh, bias=at_c(112), scale=at_c(112))
            m_t.append((m_i, m_h))
        lp.note("gate_read", m_i)
        for k in range(2):
            m_i, m_h = m_t[k]
            m = tt(tr[k][:, 0:w], aa[k][:, 0:w], aa[k][:, 0:w], ALU.mult, needs=(m_h,))
            m_v = stt(th[k][:, 0:w], tr[k][:, 0:w], 1.0, th[k][:, 0:w], ALU.add, ALU.mult, needs=(m,))
            m = stt(ti[k][:, 0:w], ti[k][:, 0:w], 1.0, u[:, 0:w], ALU.add, ALU.mult)
            m_iu.append((m_v, m))
        for k in range(2):
            m_s = aop(th[k][:, 0:w], th[k][:, 0:w], ACT.Sqrt, scale=0.25, needs=(m_iu[k][0],))
            m = tt(ti[k][:, 0:w], ti[k][:, 0:w], th[k][:, 0:w], ALU.mult, needs=(m_s, m_iu[k][1]))
            o, d0, d1 = (t[:, 0:w] if k == 0 else t[:, 0:w][:, ::-1] for t in (tr[k], aa[k], ti[k]))
            res.append(vop(vector.tensor_tensor_scan, o, d0, d1, init(k), ALU.mult, ALU.add, needs=(m,)))
        lp.note("scans", res[-1])
        return res

    nc.gpsimd.wait_ge(pe_done.sem, pe_done.n)
    nc.gpsimd.wait_ge(v_done.sem, v_done.n)
    after(tensor, *m_start)
    with loop("va", NT, chunks=4) as lp:
        i = lp.i
        nc.gpsimd.wait_ge(mod_mm.sem, i + 3)
        nc.gpsimd.dma_start(mraw[:, 0:CW], modw[bass.ds(i + 16, 1), :, :].rearrange("a p n -> p (a n)")).then_inc(s_mraw[0], 16)
        m_xb = chunk(full(bank(4, TC), hc_hi, hc_lo, w=TC), needs=(lp.back("xp"),))
        m_u = head_input(i, TC, bank(4, TC), m_xb, lp)
        m_vg = chunk(full(bank(1), h_hi, h_lo), needs=(lp.back("sig"),))
        m_sig = lp.note("sig", aop(tg[:, :], bank(1), ACT.Sigmoid, needs=(m_vg, lp.back("uu"))))
        m_va = chunk(full(bank(0), h_hi, h_lo), needs=(lp.back("uu"),))
        lp.note("uu", tt(tile(U, i, T, UW, UW + HALO), bank(0), tg[:, :], ALU.mult, needs=(m_va, m_sig)))
        gates = [bank(5, TC), bank(5, TC, TC), bank(6, TC), bank(6, TC, TC)]
        m_gt = lp.note("gates", chunk([(o, [(b, u_hi[:, 0:TC], u_lo[:, 0:TC])], True, True) for b, o in enumerate(gates)],
                                      needs=(m_u, lp.back("gate_read"))))
        mod_chunk(0, 16 * (i + 1), banks[:, bass.ds(2 * 512 + 32 + 2 * i, 2)])
        res = head_scan(i, TC, m_gt, gates, lambda k: 0.0, lp)
        for k in range(2):
            vop(vector.tensor_copy, small[:, bass.ds(176 + i * 2 + k, 1)], tr[k][:, (TC - 1, 0)[k]:(TC, 1)[k]], needs=(res[k],))

    m = vop(vector.memset, xp[:, :], 0.0)
    after(scalar, m)
    m_prev = v_done.n
    nc.gpsimd.wait_ge(mod_mm.sem, NT + 3)
    with loop("heads", NT, chunks=4) as lp:
        i = lp.i
        for j in range(3):
            nc.gpsimd.wait_ge(mod_mm.sem, i * 3 + NT + j + 1)
            nc.gpsimd.dma_start(mraw[:, j * CW:(j + 1) * CW],
                                modw[bass.ds(i * 3 + 24 + j, 1), :, :].rearrange("a p n -> p (a n)")).then_inc(s_mraw[j], 16)

        def taps(k0, k1):
            acc = tile(U, i, T, UW)
            for k in range(k0, k1):
                src, w = tile(U, i, T, UW, UW + k), col("conv_w", i * CONV_K + k)
                if k == 0:
                    m = ts(acc, src, w, col("conv_b", i), ALU.mult, ALU.add, needs=(lp.back("taps"),))
                else:
                    m = stt(acc, src, w, acc, ALU.mult, ALU.add, needs=(Mark(v_done, v_done.n, lp),))
            return m

        m_xb = chunk(full(bank(0), h_hi, h_lo), needs=(lp.back("xp"),))
        taps(0, 8)
        m_u = head_input(i, T, bank(0), m_xb, lp)
        m_gb = chunk(full(bank(1), h_hi, h_lo), needs=(lp.back("sgb"),))
        taps(8, 16)
        m = aop(tg[:, :], bank(1), ACT.Tanh, scale=0.5, needs=(m_gb, lp.back("yb_lo")))
        m_sgb = lp.note("sgb", stt(tg[:, :], tg[:, :], 1.0, bank(1), ALU.add, ALU.mult, needs=(m,)))
        m_ga = chunk(full(bank(3), h_hi, h_lo), needs=(lp.back("sga"),))
        m = aop(tile(sga, i), bank(3), ACT.Tanh, scale=0.5, needs=(m_ga,))
        lp.note("sga", stt(tile(sga, i), tile(sga, i), 1.0, bank(3), ALU.add, ALU.mult, needs=(m,)))
        gates = [bank(4), bank(5), bank(6), bank(7)]
        m_gt = lp.note("gates", chunk([(o, [(b, u_hi[:, :], u_lo[:, :])], True, True) for b, o in enumerate(gates)],
                                      needs=(m_u, lp.back("gate_read"))))
        for j in range(3):
            turn = 16 * (NT + i + 1) if j == 0 else 16 * (i + 1)
            mod_chunk(j, turn, banks[:, bass.ds(2 * 512 + 64 + 6 * i + 2 * j, 2)])
        taps(16, 24)
        res = head_scan(i, T, m_gt, gates, lambda k: small[:, bass.ds(176 + i * 2 + k, 1)], lp)
        m = tt(u[:, :], tr[0][:, :], tr[1][:, :], ALU.add, needs=res)
        m = stt(u[:, :], u[:, :], 0.5, tg[:, :], ALU.mult, ALU.mult, needs=(m, m_sgb))
        m = aop(tile(yb_hi, i), u[:, :], ACT.Copy, needs=(m,))
        m_taps = lp.note("taps", taps(24, CONV_K))
        m_yb = lp.note("yb_lo", tt(tile(yb_lo, i), u[:, :], tile(yb_hi, i).bitcast(F32), ALU.subtract, needs=(m,)))

    after(vector, Mark(mod_mm, mod_mm.n, None))
    bias_mod(8, 16, 2, 2, modv0, 0, ())
    mb1 = vec[:, VC["mod_b"] + 24:VC["mod_b"] + 48].rearrange("p (k a) -> p k a", a=1)
    m = tt(modv1.rearrange("p (k a) -> p k a", a=1), bank(2, 48, 64).rearrange("p (k two) -> p k two", two=2)[:, :, 0:1], mb1, ALU.add)
    m = stt(g1, modv1[:, 8:16], 1.0, vec[:, VC["norm_g"] + NT:VC["norm_g"] + 2 * NT], ALU.add, ALU.mult, needs=(m,))
    mu, rs, s_a, s_b = aa[0], aa[1], (tr[0], tr[1]), (th[0], th[1])
    after(tensor, m_taps, m)
    for k in range(NT):
        last = tensor.matmul(bank(0), ones, tile(U, k, T, UW), start=k == 0, stop=k == NT - 1)
    m_sum = pe_done.on(last)
    m_mu = ts(mu[:, :], bank(0), 1.0 / D, None, ALU.mult, needs=(m_sum,))
    m_sq = [None, None]
    for k in range(NT):
        m = tt(tile(U, k, T, UW), tile(U, k, T, UW), mu[:, :], ALU.subtract, needs=(m_mu,))
        m = aop(s_a[k % 2][:, :], tile(U, k, T, UW), ACT.Square, needs=(m, m_sq[k % 2]))
        after(tensor, m)
        m_sq[k % 2] = m = pe_done.on(tensor.matmul(bank(1), ones, s_a[k % 2][:, :], start=k == 0, stop=k == NT - 1))
    m_rs = rms_rstd(rs[:, :], 1, T, eps_ln, D, (m,))
    used = [None, None]
    for k in range(NT):
        t = s_b[k % 2]
        m = stt(t[:, :], tile(U, k, T, UW), col("ln_g", k), rs[:, :], ALU.mult, ALU.mult, needs=(m_rs, used[k % 2]))
        m = aop(ti[k % 2][:, :], t[:, :], ACT.Silu, bias=col("ln_b", k), needs=(m,))
        m = stt(t[:, :], ti[k % 2][:, :], 0.5, tile(sga, k), ALU.mult, ALU.mult, needs=(m,))
        m = aop(tile(h_hi, k), t[:, :], ACT.Copy, needs=(m,))
        m_ya = used[k % 2] = tt(tile(h_lo, k), t[:, :], tile(h_hi, k).bitcast(F32), ALU.subtract, needs=(m,))

    after(tensor, m_ya, m_yb)
    with loop("ev_out", NT // 2, chunks=4) as lp:
        for j in range(2):
            chunk([(bank(j), parts(yb_hi, yb_lo), True, False)], needs=(lp.back(f"res{j}"),))
            m = chunk([(bank(j), parts(h_hi, h_lo), False, True)])
            f = lp.i * 2 + j
            m_x = lp.note(f"res{j}", stt(tile(X, f), bank(j), small[:, bass.ds(16 + 32 + 2 * f, 1)], tile(X, f), ALU.mult, ALU.add, needs=(m,)))

    p = Plan(area)
    d_hi = p("d_hi", 2 * NT * T, F32R)
    d_lo = p("d_lo", 2 * NT * T, F32R)
    LW = 88
    lev0 = [p(f"lev0_{k}", 8 * LW) for k in range(2)]
    lev = p("lev", POOL_LEVELS * 8 * LW)
    pt = [p(f"pt{k}", T) for k in range(2)]
    sq, sq2, rstd = pt[0], pt[1], lev0[0][:, 0:T]
    nt_ = (lev[:, 0:T], lev[:, T:2 * T])

    def norm_into_h(gain, shift, needs):
        m = square_sum(X, T, 7, needs)
        m = rms_rstd(rstd, 7, T, eps_rms, D, (m,))
        return norm_split(X, T, rstd, gain, shift, h_hi, h_lo, nt_, (m,))

    after(scalar, m_x)
    after(scalar, Mark(chunk_mm, chunk_mm.n, None))
    m_h = norm_into_h(lambda k: g1[:, k:k + 1], lambda k: modv1[:, k:k + 1], (m_x,))
    vop(vector.memset, lev0[0][:, :], 0.0, needs=(m_h,))
    m = vop(vector.memset, lev0[1][:, :], 0.0)
    m = vop(vector.memset, lev[:, :], 0.0)
    after(scalar, m)

    rows = lambda ap, w: ap.rearrange("p (r w) -> p r w", w=w)
    PADL = 8
    after(tensor, m_h)
    with loop("pool", POOL_LEVELS, chunks=4) as lp:
        for j in range(4):
            m = chunk(full(bank(j), h_hi, h_lo), needs=(lp.back(f"l{j}"),))
            l0 = rows(lev0[j % 2][:, :], LW)
            pr = [None] * 4
            free = lp.back(f"sub{j + 2}") if j < 2 else prev_sub[j - 2]
            m_l = lp.note(f"l{j}", aop(l0[:, :, PADL:PADL + ROW], rows(bank(j), ROW), ACT.Copy, needs=(m, free)))
            if j == 0:
                prev_sub = []
            below, m, shift0 = l0, m_l, 0
            for g in range(POOL_LEVELS):
                w = 2 << g
                n = PADL + ROW + PADL - w + 1
                dst = rows(lev[:, g * 8 * LW:(g + 1) * 8 * LW], LW)[:, :, w // 2:w // 2 + n]
                a = below[:, :, shift0:shift0 + n]
                b = below[:, :, shift0 + w // 2:shift0 + w // 2 + n]
                m = tt(dst, a, b, ALU.add, needs=(m,))
                below, shift0 = rows(lev[:, g * 8 * LW:(g + 1) * 8 * LW], LW), w // 2
            sums = rows(lev[:, bass.ds(lp.i * (8 * LW), 8 * LW)], LW)[:, :, PADL:PADL + ROW]
            inv = cst[:, bass.ds(lp.i * ROW + 2 * P, ROW)].rearrange("p (a w) -> p a w", a=1).to_broadcast([P, 8, ROW])
            t = pt[j % 2]
            m = tt(rows(t[:, :], ROW), sums, inv, ALU.mult, needs=(m,))
            m = tt(rows(t[:, :], ROW), rows(t[:, :], ROW), l0[:, :, PADL:PADL + ROW], ALU.subtract, needs=(m,))
            prev_sub.append(lp.note(f"sub{j}", m))
            f = lp.i * 4 + j
            m = aop(tile(d_hi, f), t[:, :], ACT.Copy, needs=(m,))
            m_d = tt(tile(d_lo, f), t[:, :], tile(d_hi, f).bitcast(F32), ALU.subtract, needs=(m,))

    after(tensor, m_d)
    sg = [p.at and at(f"sg{k}", T, area + 2 * 2 * NT * T * 4 + 4 * T * k) for k in range(4)]
    after(scalar, m_d)
    with loop("group", 2, chunks=12) as lp:
        for gg in range(2):
            def d_parts(b0):
                return [(b0 + k, tile(d_hi, lp.i * 8 + gg * 4 + k), tile(d_lo, lp.i * 8 + gg * 4 + k)) for k in range(4)]
            for half in range(2):
                m_grp = chunk([(bank(2 * half + e), d_parts(4 * e), True, True) for e in range(2)],
                              needs=(lp.back("y3_1"),) if gg == 0 else (m_y,))
            for j in range(4):
                b = 4 + j
                m = chunk(full(bank(b), h_hi, h_lo))
                m = aop(sg[j][:, :], bank(b), ACT.Silu, needs=(m, lp.back(f"lo{j}_1") if gg == 0 else m_lo[j]))
                if j == 0:
                    m_los = []
                f = lp.i * 8 + gg * 4 + j
                m_y = lp.note(f"y{j}_{gg}", stt(sg[j][:, :], bank(j), col("od_scale", f), sg[j][:, :], ALU.mult, ALU.mult, needs=(m, m_grp)))
                m = aop(tile(d_hi, f), sg[j][:, :], ACT.Copy, needs=(m_y,))
                m_los.append(lp.note(f"lo{j}_{gg}", tt(tile(d_lo, f), sg[j][:, :], tile(d_hi, f).bitcast(F32), ALU.subtract, needs=(m,))))
            m_lo = m_los

    after(tensor, m_lo[3])
    with loop("od_out", NT // 2, chunks=4) as lp:
        for j in range(2):
            chunk([(bank(j), parts(d_hi, d_lo), True, False)], needs=(lp.back(f"res{j}"),))
            m = chunk([(bank(j), parts(d_hi, d_lo, k0=KC), False, True)] if False else
                      [(bank(j), [(k, tile(d_hi, KC + k), tile(d_lo, KC + k)) for k in range(KC)], False, True)])
            f = lp.i * 2 + j
            m_x = lp.note(f"res{j}", stt(tile(X, f), bank(j), small[:, bass.ds(64 + 16 + f, 1)], tile(X, f), ALU.mult, ALU.add, needs=(m,)))

    p = Plan(area2)
    y_hi = p("y_hi", 8 * T, F32R)
    y_lo = p("y_lo", 8 * T, F32R)
    o_m = p.at
    sq, sq2, rs_ = p("bsq", T), p("bsq2", T), p("brs", T)
    rstd = rs_[:, :]
    nt2 = (p("bn0", T), p("bn1", T))
    nt_ = (nt2[0][:, :], nt2[1][:, :])
    m_mm = Mark(chunk_mm, chunk_mm.n, None)
    after(vector, m_mm)
    after(scalar, m_x, m_mm)
    after(nc.gpsimd, m_x, m_mm)
    nc.gpsimd.dma_start(cst2[:, :], consts[:, 512:NCONST]).then_inc(s_cst2, 16)
    ident2 = ident
    tri_ones, after_m = cst2[:, 0:512], cst2[:, 512:640]
    past, neg = cst2[:, 640:768], cst2[:, 768:896]
    tri = tri_ones[:, 0:P]

    def norm_in_place(name, b, needs):
        m = square_sum(X, T, b, needs)
        m = rms_rstd(rstd, b, T, eps_rms, D, (m,))
        for k in range(NT):
            m_ = stt(tile(X, k), tile(X, k), col(name, k), rstd, ALU.mult, ALU.mult, needs=(m,))
        return m_

    m_x = norm_in_place("final_g", 7, (m_x,))
    m = square_sum(X, T, 6, (m_x,))
    m = rms_rstd(rstd, 6, T, eps_rms, D, (m,))
    m_h = norm_split(X, T, rstd, lambda k: col("norm1_g", k), None, h_hi, h_lo, nt_, (m,))

    p = Plan(o_m)
    qk = [p(f"qk{n}", 4 * T) for n in range(2)]
    vv = [p(f"vv{n}", NB * 256) for n in range(2)]
    zs = p("zs", 2 * T)
    bc = p("bc", 4 * T)
    dtv, av, acs = p("dtv", 16), p("av", 16), p("acs", 16)
    o_w = p.at
    XW = T + SSM_K
    cpad = [p(f"cpad{k}", XW) for k in range(2)]
    ct = [p(f"ct{k}", T) for k in range(2)]
    csb = p("csb", T)
    after(vector, m_h)
    after(scalar, m_h)
    m = vop(vector.memset, cpad[0][:, :], 0.0)
    m_pad = vop(vector.memset, cpad[1][:, :], 0.0)
    after(scalar, m_pad)
    after(tensor, m_h)
    m_free, m_y = None, None
    for t in range(2):
        m_xa = chunk(full(bank(0), h_hi, h_lo), needs=(m_free,))
        m_c = chunk(full(bank(1), h_hi, h_lo))
        m_b = chunk(full(bank(2), h_hi, h_lo))
        m = aop(csb[:, :], bank(0), ACT.Copy, needs=(m_xa, m_y))
        m = tt(cpad[t][:, SSM_K - 1:SSM_K - 1 + T], bank(1), csb[:, :], ALU.mult, needs=(m, m_c))
        for k in range(SHORT_K):
            src = cpad[t][:, 1 + k:1 + k + T]
            w = col("conv_a_w", t * SHORT_K + k)
            if k == 0:
                m = ts(ct[t][:, :], src, w, None, ALU.mult, needs=(m,))
            else:
                m = stt(ct[t][:, :], src, w, ct[t][:, :], ALU.mult, ALU.add, needs=(m,))
        m_y = m_free = tt(ct[t][:, :], bank(2), ct[t][:, :], ALU.mult, needs=(m, m_b))
        m = aop(tile(y_hi, t), ct[t][:, :], ACT.Copy, needs=(m_y,))
        m_y = tt(tile(y_lo, t), ct[t][:, :], tile(y_hi, t).bitcast(F32), ALU.subtract, needs=(m,))
    m_bank = {0: m_free, 1: m_free, 2: m_free, 3: None}
    n_b = 3

    def next_bank():
        nonlocal n_b
        n_b = (n_b + 1) % 4
        return n_b

    for n in range(2):
        for t in range(4):
            b = next_bank()
            m = chunk(full(bank(b), h_hi, h_lo), needs=(m_bank[b],))
            m_bank[b] = m_qk = aop(tile(qk[n], t), bank(b), ACT.Copy, needs=(m,))
        for half in range(2):
            for tb in range(NB):
                pass
            groups = []
            for tb in range(NB):
                pr = [(k, h_hi[:, (4 * half + k) * T + tb * P:(4 * half + k) * T + (tb + 1) * P],
                       h_lo[:, (4 * half + k) * T + tb * P:(4 * half + k) * T + (tb + 1) * P]) for k in range(4)]
                groups.append((bank(4 + tb, 256), pr, half == 0, half == 1))
            m = chunk(groups, needs=(m_vv,) if n and not half else (), swap=True)
        for tb in range(NB):
            m_vv = aop(vv[n][:, tb * 256:(tb + 1) * 256], bank(4 + tb, 256), ACT.Copy, needs=(m,))
    for t in range(2):
        b = next_bank()
        m = chunk(full(bank(b), h_hi, h_lo), needs=(m_bank[b],))
        m_bank[b] = m_z = aop(tile(zs, t), bank(b), ACT.Silu, needs=(m,))
    m_pad = [m_y, m_y]
    for t in range(4):
        b = next_bank()
        m = chunk(full(bank(b), h_hi, h_lo), needs=(m_bank[b],))
        m_bank[b] = m = aop(cpad[t % 2][:, SSM_K - 1:SSM_K - 1 + T], bank(b), ACT.Copy, needs=(m, m_pad[t % 2]))
        for k in range(SSM_K):
            src, w = cpad[t % 2][:, k:k + T], col("ssm_conv_w", t * SSM_K + k)
            if k == 0:
                m = ts(ct[t % 2][:, :], src, w, None, ALU.mult, needs=(m,) if t < 2 else (m, m_s[t % 2]))
            else:
                m = stt(ct[t % 2][:, :], src, w, ct[t % 2][:, :], ALU.mult, ALU.add, needs=(m,))
        m_pad[t % 2] = m
        if t == 0:
            m_s = [None, None]
        m_s[t % 2] = m_bc = aop(tile(bc, t), ct[t % 2][:, :], ACT.Silu, bias=col("ssm_conv_b", t), needs=(m,))
    after(tensor, m_vv)
    for tb in range(NB):
        for k in range(NT):
            hh, hl = (h[:, k * T + tb * P:k * T + (tb + 1) * P] for h in (h_hi, h_lo))
            wh, wl = (w[:, k * NH:(k + 1) * NH] for w in (wdt_hi, wdt_lo))
            for j, (l, r) in enumerate(((hh, wh), (hh, wl), (hl, wh))):
                last = tensor.matmul(bank(4, NH, tb * NH), l, r, start=k == 0 and j == 0, stop=k == NT - 1 and j == 2)
    m = pe_done.on(last)
    m = tt(av[:, :], bank(4, 16), vec[:, VC["dt_bias"]:VC["dt_bias"] + 16], ALU.add, needs=(m,))
    m = softplus16(dtv[:, :], av[:, :], False, (m,))
    m_e = aop(av[:, :], vec[:, VC["a_log"]:VC["a_log"] + 16], ACT.Exp, needs=(m,))
    m_a = stt(av[:, :], av[:, :], -1.0, dtv[:, :], ALU.mult, ALU.mult, needs=(m_e,))

    p = Plan(o_w)
    after(vector, m_y, m_bc)
    after(scalar, m_y, m_bc, m_a)
    vector.wait_ge(s_cst2, 16)
    tensor.wait_ge(s_cst2, 16)
    scalar.wait_ge(s_cst2, 16)

    def split_y(f, src, needs):
        m = aop(tile(y_hi, f), src, ACT.Copy, needs=needs)
        return tt(tile(y_lo, f), src, tile(y_hi, f).bitcast(F32), ALU.subtract, needs=(m,))

    def blk(t, n, w=None):
        return t[:, OFF[n]:OFF[n] + (T - P * n if w is None else w)]

    def pblk(b, n, w=None, o=0):
        s = b * 512 + OFF[n] + o
        return banks[:, s:s + (T - P * n if w is None else w)]

    wide = lambda b: banks[:, b * 512:b * 512 + CAUSAL]
    ew = [p(f"ew{k}", CAUSAL) for k in range(5)]
    xd = p("xd", NB * 256)
    mx, nl = p("mx", NB), p("nl", NB)

    scale = HD ** -0.5
    sp_, zz, ww, e_, l_ = ew
    m_w_free = m_y_b = m_pv = m_mid = None
    after(tensor, m_qk, m_vv, m_a)
    m_out = [None, None]
    for h in range(NH):
        t, p0 = h // 2, HD * (h % 2)
        q = qk[0][p0:p0 + HD, t * T:(t + 1) * T]
        kk = qk[0][p0:p0 + HD, (2 + t) * T:(3 + t) * T]
        after(tensor, m_mid)
        for n in range(NB):
            last = tensor.matmul(pblk(0, n), kk[:, n * P:(n + 1) * P], q[:, n * P:T], start=True, stop=True)
        m = pe_done.on(last)
        m_1 = aop(e_[:, :], wide(0), ACT.Abs, scale=scale, needs=(m, m_mid))
        m_abs = m_1
        m_1 = aop(l_[:, :], e_[:, :], ACT.Exp, scale=-1.0, needs=(m_1,))
        m_1 = aop(e_[:, :], l_[:, :], ACT.Ln, bias=1.0, needs=(m_1,))
        m = ts(sp_[:, :], wide(0), scale, 0.0, ALU.mult, ALU.max, needs=(m_abs,))
        m = tt(sp_[:, :], sp_[:, :], e_[:, :], ALU.add, needs=(m, m_1))
        m_mid = m = stt(zz[:, :], wide(0), scale, sp_[:, :], ALU.mult, ALU.subtract, needs=(m,))
        for n in range(NB):
            m = tt(blk(sp_, n, P), blk(sp_, n, P), past, ALU.mult, needs=(m_mid,))
        after(tensor, m)
        for n in range(NB):
            for k in range(n, NB):
                last = tensor.matmul(pblk(3, n, T - P * k, P * (k - n)), after_m if k == n else ones, blk(sp_, k),
                                     start=k == n, stop=k == NB - 1)
        m_bt = pe_done.on(last)
        m = tt(zz[:, :], zz[:, :], wide(3), ALU.subtract, needs=(m_bt,))
        m_mid = m = aop(ww[:, :], zz[:, :], ACT.Exp, needs=(m, m_pv))
        for n in range(NB):
            m = tt(blk(ww, n, P), blk(ww, n, P), past, ALU.mult, needs=(m_mid,))
        after(tensor, m, m_out[t] if h % 2 == 0 else None)
        for n in range(NB):
            last = tensor.matmul(banks[p0:p0 + HD, (6 + t) * 512 + n * P:(7 + t) * 512],
                                 vv[0][:, n * 256 + h * HD:n * 256 + (h + 1) * HD], blk(ww, n), start=n == 0, stop=n == NB - 1)
        m_pv = pe_done.on(last)
        if h % 2:
            m = aop(e_[:, 0:T], bank(6 + t), ACT.Copy, needs=(m_pv,))
            m_mid = m_out[t] = split_y(2 + t, e_[:, 0:T], (m,))

    after(tensor, *m_out)
    pm, pT = ew[0], ew[1]
    m_p = m_pt = m_pv = None
    m_pend = [None, None]
    for h in range(NH):
        t, p0 = h // 2, HD * (h % 2)
        q = qk[1][p0:p0 + HD, t * T:(t + 1) * T]
        kk = qk[1][p0:p0 + HD, (2 + t) * T:(3 + t) * T]
        after(tensor, m_p)
        for b in range(NB):
            last = tensor.matmul(pblk(0, NB - 1 - b, (b + 1) * P), q[:, b * P:(b + 1) * P], kk[:, 0:(b + 1) * P], start=True, stop=True)
        m = pe_done.on(last)
        for b in range(NB):
            dg = pblk(0, NB - 1 - b, P, b * P)
            m_1 = tt(dg, dg, neg, ALU.add, needs=(m,))
            m_1 = vop(vector.reduce_max, mx[:, b:b + 1], pblk(0, NB - 1 - b, (b + 1) * P), AX.X, needs=(m_1,))
        m_1 = ts(mx[:, :], mx[:, :], -scale, None, ALU.mult, needs=(m_1,))
        for b in range(NB):
            m_p = aop(blk(pm, NB - 1 - b, (b + 1) * P), pblk(0, NB - 1 - b, (b + 1) * P), ACT.Exp, bias=mx[:, b:b + 1],
                      scale=scale, accum_out=nl[:, b:b + 1], needs=(m_1, m_pt))
        m = vop(vector.reciprocal, nl[:, :], nl[:, :], needs=(m_p,))
        for b in range(NB):
            m_n = ts(blk(pm, NB - 1 - b, (b + 1) * P), blk(pm, NB - 1 - b, (b + 1) * P), nl[:, b:b + 1], None, ALU.mult, needs=(m,))
        after(tensor, m_n)
        for b in range(NB):
            for k in range(b + 1):
                src = pm[:, OFF[NB - 1 - b] + k * P:OFF[NB - 1 - b] + (k + 1) * P]
                last = tensor.transpose(pblk(3, k, P, (b - k) * P), src, ident2)
        m_pt = pe_done.on(last)
        m = aop(pT[:, :], wide(3), ACT.Copy, needs=(m_pt, m_pv))
        after(tensor, m, m_pend[t] if h % 2 == 0 else None)
        for n in range(NB):
            last = tensor.matmul(banks[p0:p0 + HD, (6 + t) * 512 + n * P:(7 + t) * 512],
                                 vv[1][:, n * 256 + h * HD:n * 256 + (h + 1) * HD], blk(pT, n), start=n == 0, stop=n == NB - 1)
        m_pv = pe_done.on(last)
        if h % 2:
            m = aop(ew[2][:, t * T:(t + 1) * T], bank(6 + t), ACT.Copy, needs=(m_pv,))
            m_pend[t] = split_y(6 + t, ew[2][:, t * T:(t + 1) * T], (m,))

    after(tensor, *m_pend)
    for n in range(NB):
        for k in range(n + 1):
            last = tensor.matmul(bank(6, NH, n * NH), tri if k == n else ones, av[:, k * NH:(k + 1) * NH], start=k == 0, stop=k == n)
    m = pe_done.on(last)
    m_acs = vop(vector.tensor_copy, acs[:, :], bank(6, 16), needs=(m,))
    for t in range(2):
        for n in range(NB):
            last = tensor.transpose(banks[:, 4 * 512 + n * 256 + t * P:4 * 512 + n * 256 + (t + 1) * P],
                                    bc[:, t * T + n * P:t * T + (n + 1) * P], ident2)
    m = pe_done.on(last)
    m_xd = tt(xd[:, :].rearrange("p (n d) -> p n d", d=HD), banks[:, 4 * 512:6 * 512].rearrange("p (n d) -> p n d", d=HD),
              dtv[:, :].rearrange("p (n a) -> p n a", a=1).to_broadcast([P, 16, HD]), ALU.mult, needs=(m,))
    gm = [ew[3], ew[4]]
    m_cp = None
    for g in range(2):
        bm = bc[g * HD:(g + 1) * HD, 2 * T:3 * T]
        cm = bc[g * HD:(g + 1) * HD, 3 * T:4 * T]
        after(tensor, m_cp)
        for n in range(NB):
            last = tensor.matmul(pblk(0, n), bm[:, n * P:(n + 1) * P], cm[:, n * P:T], start=True, stop=True)
        m = pe_done.on(last)
        m_cp = aop(gm[g][:, :], wide(0), ACT.Copy, needs=(m,))
        for n in range(NB):
            m_gm = tt(blk(gm[g], n, P), blk(gm[g], n, P), tri, ALU.mult, needs=(m_cp,))
    dk = [ew[0], ew[1]]
    abc = ew[2]
    after(tensor, m_xd, m_gm)
    m_ab = m_ar = None
    m_dk = [None, None]
    m_row = [None, None]
    for h in range(NH):
        g, p0, d_ = h // 2, HD * (h % 2), dk[h % 2]
        m = vop(vector.tensor_copy, abc[:, (h % 2) * 512:(h % 2) * 512 + 512].rearrange("p (n c) -> p n c", c=P),
                av[:, :].rearrange("p (n h) -> p n h", h=NH)[:, :, h:h + 1].to_broadcast([P, NB, P]), needs=(m_row[h % 2],))
        after(tensor, m, m_dk[h % 2])
        for n in range(NB):
            last = tensor.matmul(bank(3 + h % 2, T - P * n, P * n), abc[:, (h % 2) * 512 + n * P:(h % 2) * 512 + (n + 1) * P],
                                 tri_ones[:, 0:T - P * n], start=n == 0, stop=n == NB - 1)
        m_row[h % 2] = m = pe_done.on(last)
        after(vector, m, m_ar)
        for n in range(NB):
            m = ts(blk(d_, n), bank(3 + h % 2, T - P * n, P * n), acs[:, n * NH + h:n * NH + h + 1], 0.0, ALU.subtract, ALU.min,
                   needs=(m_acs,))
        m_dk[h % 2] = m
        m = aop(d_[:, :], d_[:, :], ACT.Exp, needs=(m,))
        m = tt(d_[:, :], d_[:, :], gm[g][:, :], ALU.mult, needs=(m, m_gm))
        after(tensor, m)
        for n in range(NB):
            last = tensor.matmul(banks[p0:p0 + HD, (6 + g) * 512 + n * P:(7 + g) * 512],
                                 xd[:, n * 256 + h * HD:n * 256 + (h + 1) * HD], blk(d_, n), start=n == 0, stop=n == NB - 1)
        m_py = pe_done.on(last)
        m_ar = m_ar2 = m_py if h else m_py
        if h % 2 == 0:
            m_ar = None
            m_keep = m_py
        else:
            m_ar = m_py
    yt = [abc[:, 0:T], abc[:, T:2 * T]]
    for g in range(2):
        m = stt(yt[g], tile(bc, g), col("ssm_d", g), bank(6 + g), ALU.mult, ALU.add, needs=(m_py,))
        m = tt(yt[g], yt[g], tile(zs, g), ALU.mult, needs=(m,))
        m_1 = aop(dk[0][:, g * T:(g + 1) * T], yt[g], ACT.Square, needs=(m,))
        after(tensor, m_1)
        m = pe_done.on(tensor.matmul(bank(g), ones, dk[0][:, g * T:(g + 1) * T], start=True, stop=True))
        m = rms_rstd(dk[1][:, g * T:(g + 1) * T], g, T, eps_rms, P, (m,))
        m = stt(yt[g], yt[g], col("ssm_norm_g", g), dk[1][:, g * T:(g + 1) * T], ALU.mult, ALU.mult, needs=(m,))
        m_yc = split_y(4 + g, yt[g], (m,))

    p = Plan(o_m)
    m_hi, m_lo_ = p("m_hi", NT * T, F32R), p("m_lo", NT * T, F32R)
    gs = [p(f"gs{k}", T) for k in range(4)]
    after(scalar, m_yc)
    after(tensor, m_yc)
    with loop("merge", 2, chunks=20) as lp:
        for j in range(4):
            f = lp.i * 4 + j
            free = lp.back("pr3_3") if j == 0 else m_pr[3]
            m_br = chunk([(bank(4 + b), [(2 * b + k, tile(y_hi, 2 * b + k), tile(y_lo, 2 * b + k)) for k in range(2)], True, True)
                          for b in range(4)], needs=(free,))
            m_acc, new = None, []
            for b in range(4):
                mf = lp.back(f"sg3_{b}") if j == 0 else m_sg[b]
                m = chunk(full(bank(b), h_hi, h_lo), needs=(mf,))
                gf = lp.back(f"pr3_{b}") if j == 0 else m_pr[b]
                gf2 = (lp.back("lo3"),) if j == 0 else (m_last,)
                if b == 0:
                    m_sg_new, m_pr_new = [], []
                m = lp.note(f"sg{j}_{b}", aop(gs[b][:, :], bank(b), ACT.Sigmoid, needs=(m, *(gf2 if b == 0 else ()), gf)))
                m_sg_new.append(m)
                m = lp.note(f"pr{j}_{b}", tt(gs[b][:, :], bank(4 + b), gs[b][:, :], ALU.mult, needs=(m, m_br)))
                m_pr_new.append(m)
                if b:
                    m_pr_new[b] = m_acc = tt(gs[0][:, :], gs[0][:, :], gs[b][:, :], ALU.add, needs=(m,))
                    lp.note(f"pr{j}_{b}", m_acc)
            m_sg, m_pr = m_sg_new, m_pr_new
            m = aop(tile(m_hi, f), gs[0][:, :], ACT.Copy, needs=(m_acc,))
            m_last = lp.note(f"lo{j}", tt(tile(m_lo_, f), gs[0][:, :], tile(m_hi, f).bitcast(F32), ALU.subtract, needs=(m,)))

    after(tensor, m_last)
    with loop("w_o", 2, chunks=4) as lp:
        for j in range(4):
            m = chunk(full(bank(j), m_hi, m_lo_), needs=(lp.back(f"res{j}"),))
            f = lp.i * 4 + j
            m_x = lp.note(f"res{j}", tt(tile(X, f), bank(j), tile(X, f), ALU.add, needs=(m,)))

    p = Plan(area)
    f_hi, f_lo = p("f_hi", FFN_TILES * T, F32R), p("f_lo", FFN_TILES * T, F32R)
    fs = [p(f"fs{k}", T) for k in range(2)]
    sq, sq2 = fs
    rstd = f_hi[:, 0:T].bitcast(F32)
    rstd_b = at("rstd_b", T, area + 4 * T * 30)
    rstd = rstd_b[:, :]
    n0, n1 = at("n0b", T, area + 4 * T * 32), at("n1b", T, area + 4 * T * 34)
    nt_ = (n0[:, :], n1[:, :])
    m_mm = Mark(chunk_mm, chunk_mm.n, None)
    after(scalar, m_x, m_mm)
    after(vector, m_mm)
    m_h = norm_into_h(lambda k: col("norm2_g", k), None, (m_x,))
    after(tensor, m_h)
    after(scalar, m_h)
    with loop("ffn_in", FFN_TILES // 2, chunks=4) as lp:
        for j in range(2):
            m_g = chunk(full(bank(2 * j), h_hi, h_lo), needs=(lp.back(f"up{j}"),))
            m_u = chunk(full(bank(2 * j + 1), h_hi, h_lo))
            f = lp.i * 2 + j
            m = aop(fs[j][:, :], bank(2 * j), ACT.Silu, needs=(m_g, lp.back(f"flo{j}")))
            m = lp.note(f"up{j}", tt(fs[j][:, :], bank(2 * j + 1), fs[j][:, :], ALU.mult, needs=(m, m_u)))
            m = aop(tile(f_hi, f), fs[j][:, :], ACT.Copy, needs=(m,))
            m_f = lp.note(f"flo{j}", tt(tile(f_lo, f), fs[j][:, :], tile(f_hi, f).bitcast(F32), ALU.subtract, needs=(m,)))
    after(tensor, m_f)
    m_res = [None] * 4
    for f in range(NT):
        for k0, n in ((0, 8), (8, 8), (16, FFN_TILES - 16)):
            m = chunk([(bank(f % 4), [(k, tile(f_hi, k0 + k), tile(f_lo, k0 + k)) for k in range(n)], k0 == 0, k0 == 16)],
                      needs=(m_res[f % 4],) if k0 == 0 else ())
        m_x = m_res[f % 4] = tt(tile(X, f), bank(f % 4), tile(X, f), ALU.add, needs=(m,))

    after(scalar, m_x)
    m_x = norm_in_place("final_g2", 7, (m_x,))
    nc.sync.wait_ge(v_done.sem, m_x.value())
    nc.sync.dma_start(out, X[:, :]).then_inc(s_out, 16)
    nc.sync.wait_ge(s_out, 16)
    assert state["chunk"] == N_CHUNKS, state["chunk"]
    ctx.close()


def constants():
    c = np.zeros((P, NCONST), np.float32)
    r, q = np.arange(P)[:, None], np.arange(P)[None, :]
    c[:, CC["ident"]:CC["ident"] + P] = r == q
    c[:, CC["ones"]:CC["ones"] + P] = 1
    t = np.arange(ROW)
    for g in range(POOL_LEVELS):
        w = 2 << g
        cnt = np.clip(t + w // 2, 0, ROW) - np.clip(t - w // 2, 0, ROW)
        c[:, CC["inv_cnt"] + g * ROW:CC["inv_cnt"] + (g + 1) * ROW] = np.float32(1) / cnt.astype(np.float32)
    c[:, CC["tri_ones"]:CC["tri_ones"] + P] = r <= q
    c[:, CC["tri_ones"] + P:CC["tri_ones"] + 512] = 1
    c[:, CC["after"]:CC["after"] + P] = r > q
    c[:, CC["past"]:CC["past"] + P] = r < q
    c[:, CC["neg"]:CC["neg"] + P] = np.where(q <= r, 0, -1e30)
    return c


def tiles_of(w):
    k, n = w.shape
    return w.reshape(k // P, P, n // P, P).transpose(2, 1, 0, 3).reshape(n // P, P, k)


def lay_out(a):
    ev, od = a["ev_w_in"][0], a["od_w_in"][0]
    evt = tiles_of(ev)
    zero = np.zeros((P, CW - 4 * P), np.float32)
    gates = [np.concatenate([a["ev_w_r"][0, 0, h], a["ev_w_i"][0, 0, h], a["ev_w_r"][0, 1, h], a["ev_w_i"][0, 1, h], zero], 1)
             for h in range(8)]
    s = []
    for i in range(NT):
        s += [evt[24 + i], evt[8 + i], evt[i], gates[i]]
    for i in range(NT):
        s += [evt[24 + i], evt[32 + i], evt[16 + i], gates[i]]
    wo = tiles_of(a["ev_w_out"][0])
    for f in range(NT):
        s += [wo[f][:, CW:], wo[f][:, :CW]]
    odt = tiles_of(od)
    s += list(odt[:16])
    for g in range(POOL_LEVELS):
        wg = tiles_of(a["od_w_grp"][0, g])
        s += [np.concatenate([wg[0], wg[1]], 1), np.concatenate([wg[2], wg[3]], 1)]
        s += list(odt[16 + 4 * g:20 + 4 * g])
    wo = tiles_of(a["od_w_out"][0])
    for f in range(NT):
        s += [wo[f][:, :CW], wo[f][:, CW:]]
    w = a["w_in_2"][0]
    A = tiles_of(w[:, 0:768])
    for t in range(2):
        s += [A[t], A[4 + t], A[2 + t]]
    c0 = 768 + 768
    d0 = c0 + 772
    for base in (768, d0):
        s += list(tiles_of(w[:, base:base + 512]))
        v = w[:, base + 512:base + 768].reshape(2, 4, P, 256).transpose(0, 2, 1, 3).reshape(2, P, CW)
        s += [v[0], v[1]]
    s += list(tiles_of(w[:, c0:c0 + 768]))
    wdt = w[:, c0 + 768:c0 + 772]
    G = tiles_of(w[:, d0 + 768:])
    wb = a["w_branch_2"][0]
    br = [tiles_of(wb[b]) for b in range(4)]
    for f in range(NT):
        s.append(np.concatenate([br[b][f] for b in range(4)], 1))
        s += [G[b * NT + f] for b in range(4)]
    s += list(tiles_of(a["w_o_2"][0]))
    gu = tiles_of(a["w_gate_up_2"][0])
    for f in range(FFN_TILES):
        s += [gu[f], gu[FFN_TILES + f]]
    wd = tiles_of(a["w_down_2"][0])
    for f in range(NT):
        last = np.concatenate([wd[f][:, 2 * CW:], np.zeros((P, 3 * CW - FFN_TILES * P), np.float32)], 1)
        s += [wd[f][:, :CW], wd[f][:, CW:2 * CW], last]
    weights = np.stack(s)
    assert weights.shape == (N_CHUNKS, P, CW), weights.shape
    modw = np.concatenate([tiles_of(a["mod_w"][0]), tiles_of(a["mod_w"][1])])

    f = lambda v: np.asarray(v).reshape(-1, P).T
    k_ = lambda v: v.reshape(v.shape[0], -1, P).transpose(2, 1, 0).reshape(P, -1)
    rep = lambda v: np.broadcast_to(np.tile(v, NB)[None, :], (P, NB * NH))
    vals = {
        "c": f(a["c"]), "c_ctx": f(a["c_ctx"]), "norm_g": f(a["norm_g"]), "mod_b": f(a["mod_b"]),
        "conv_w": k_(a["ev_conv_w"][0]), "conv_b": f(a["ev_conv_b"]), "ln_g": f(a["ev_ln_g"]), "ln_b": f(a["ev_ln_b"]),
        "sconv_w": k_(a["ev_sconv_w"][0]), "sconv_b": f(a["ev_sconv_b"]),
        "b_r": k_(a["ev_b_r"][0]), "b_i": k_(a["ev_b_i"][0]), "lam": k_(a["ev_lam"][0]),
        "od_scale": f(a["od_scale"]), "final_g": f(a["final_g"]), "norm1_g": f(a["norm1_g_2"]),
        "conv_a_w": k_(a["conv_a_w_2"][0]), "ssm_conv_w": k_(a["ssm_conv_w_2"][0]), "ssm_conv_b": f(a["ssm_conv_b_2"]),
        "dt_bias": rep(a["ssm_dt_bias_2"][0]), "a_log": rep(a["ssm_a_log_2"][0]),
        "ssm_d": f(np.repeat(a["ssm_d_2"][0], HD)), "ssm_norm_g": f(a["ssm_norm_g_2"]),
        "norm2_g": f(a["norm2_g_2"]), "final_g2": f(a["final_g_2"]),
        "w_dt": wdt.reshape(NT, P, NH).transpose(1, 0, 2).reshape(P, NT * NH),
    }
    order = sorted(VC, key=VC.get)
    vecs = np.ascontiguousarray(np.concatenate([vals[n] for n in order], 1))
    assert vecs.shape == (P, NVEC), vecs.shape
    xt = lambda x, t: np.ascontiguousarray(x[0].reshape(t, NT, P).transpose(2, 1, 0).reshape(P, NT * t))
    return {"weights": weights, "modw": np.ascontiguousarray(modw), "vecs": vecs, "consts": constants(),
            "x_in": xt(a["x"], T), "ctx_in": xt(a["ctx"], TC)}


def kernel(**inputs):
    import concourse.bacc as bacc
    from concourse.bass_utils import run_bass_kernel_spmd

    arrays = lay_out({k: np.asarray(v) for k, v in inputs.items()})
    nc = bacc.Bacc("TRN2", target_bir_lowering=False, num_devices=1)
    args = [nc.dram_tensor(n, v.shape, F32, kind="ExternalInput").ap() for n, v in arrays.items()]
    out = nc.dram_tensor("out", (P, NT * T), F32, kind="ExternalOutput").ap()
    program(nc, *args, out)
    r = run_bass_kernel_spmd(nc, [arrays], core_ids=[0])
    y = r.results[0]["out"]
    return y.reshape(P, NT, T).transpose(2, 1, 0).reshape(1, T, D)
```

```python
import numpy as np
import concourse.bass as bass
from concourse import mybir
from contextlib import ExitStack, contextmanager

P = 128
D = 1024
T = 512
TC = 256
NT = D // P
NB = T // P
MOD_RING = 2
RING = 4
AHEAD = 3
KC = 8
CW = KC * P
CONV_K, SCONV_K, SSM_K, SHORT_K = 31, 4, 4, 3
HALO = CONV_K // 2
PE_TAPS = 16
FFN_TILES = 22
HD = 64
NH = 4
ROW = 64
POOL_LEVELS = 4
F32, F32R = mybir.dt.float32, mybir.dt.float32r
ALU, ACT, AX = mybir.AluOpType, mybir.ActivationFunctionType, mybir.AxisListType

CAUSAL = NB * (NB + 1) // 2 * P
OFF = {0: 0, 1: 512, 3: 896, 2: 1024}


def vector_columns():
    at, cols = 0, {}
    for name, n in (
        ("c", NT), ("c_ctx", NT), ("norm_g", 2 * NT), ("mod_b", 2 * 3 * NT),
        ("conv_w", NT * CONV_K), ("conv_b", NT), ("ln_g", NT), ("ln_b", NT),
        ("sconv_w", NT * SCONV_K), ("sconv_b", NT), ("b_r", 2 * NT), ("b_i", 2 * NT), ("lam", 2 * NT),
        ("od_scale", 2 * NT), ("final_g", NT), ("norm1_g", NT), ("conv_a_w", 2 * SHORT_K),
        ("ssm_conv_w", 4 * SSM_K), ("ssm_conv_b", 4), ("dt_bias", NB * NH), ("a_log", NB * NH),
        ("ssm_d", 2), ("ssm_norm_g", 2), ("norm2_g", NT), ("final_g2", NT), ("w_dt", NT * NH),
    ):
        cols[name] = at
        at += n
    return cols, at


VC, NVEC = vector_columns()
LOOPS = {
    'va': {
        "per": {'v': 16, 'a': 15, 'mod': 1},
        "back": {'xp': ('a', 1), 'conv': ('v', 4), 'sig': ('a', 3), 'uu': ('v', 6), 'gates': ('mm', 4), 'gate_read': ('a', 10), 'th_read': ('v', 11), 'scans': ('v', 14)},
    },
    'heads': {
        "per": {'v': 72, 'a': 36, 'mod': 6},
        "back": {'xp0': ('a', 2), 'conv0': ('v', 5), 'sgb0': ('v', 11), 'gates0': ('mm', 3), 'gate_read0': ('a', 11), 'conv_pe0': ('mm', 6), 'sga0': ('v', 16), 'th_read0': ('v', 23), 'scans0': ('v', 26), 'taps0': ('v', 33), 'conv_sum0': ('v', 34), 'yb_lo0': ('v', 36), 'xp1': ('a', 20), 'conv1': ('v', 41), 'sgb1': ('v', 47), 'gates1': ('mm', 9), 'gate_read1': ('a', 29), 'conv_pe1': ('mm', 12), 'sga1': ('v', 52), 'th_read1': ('v', 59), 'scans1': ('v', 62), 'taps1': ('v', 69), 'conv_sum1': ('v', 70), 'yb_lo1': ('v', 72)},
    },
    'ev_out': {
        "per": {'v': 2},
        "back": {'res0': ('v', 1), 'res1': ('v', 2)},
    },
    'pool': {
        "per": {'v': 28, 'a': 8},
        "back": {'l0': ('a', 1), 'sub0': ('v', 6), 'l1': ('a', 3), 'sub1': ('v', 13), 'l2': ('a', 5), 'sub2': ('v', 20), 'l3': ('a', 7), 'sub3': ('v', 27)},
    },
    'group': {
        "per": {'v': 16, 'a': 16},
        "back": {'y0_0': ('v', 1), 'lo0_0': ('v', 2), 'y1_0': ('v', 3), 'lo1_0': ('v', 4), 'y2_0': ('v', 5), 'lo2_0': ('v', 6), 'y3_0': ('v', 7), 'lo3_0': ('v', 8), 'y0_1': ('v', 9), 'lo0_1': ('v', 10), 'y1_1': ('v', 11), 'lo1_1': ('v', 12), 'y2_1': ('v', 13), 'lo2_1': ('v', 14), 'y3_1': ('v', 15), 'lo3_1': ('v', 16)},
    },
    'od_out': {
        "per": {'v': 6, 'a': 4},
        "back": {'res0': ('v', 1), 's10': ('v', 2), 's20': ('v', 3), 'res1': ('v', 4), 's11': ('v', 5), 's21': ('v', 6)},
    },
    'merge': {
        "per": {'v': 32, 'a': 20},
        "back": {'sg0_0': ('a', 1), 'pr0_0': ('v', 1), 'sg0_1': ('a', 2), 'pr0_1': ('v', 3), 'sg0_2': ('a', 3), 'pr0_2': ('v', 5), 'sg0_3': ('a', 4), 'pr0_3': ('v', 7), 'lo0': ('v', 8), 'sg1_0': ('a', 6), 'pr1_0': ('v', 9), 'sg1_1': ('a', 7), 'pr1_1': ('v', 11), 'sg1_2': ('a', 8), 'pr1_2': ('v', 13), 'sg1_3': ('a', 9), 'pr1_3': ('v', 15), 'lo1': ('v', 16), 'sg2_0': ('a', 11), 'pr2_0': ('v', 17), 'sg2_1': ('a', 12), 'pr2_1': ('v', 19), 'sg2_2': ('a', 13), 'pr2_2': ('v', 21), 'sg2_3': ('a', 14), 'pr2_3': ('v', 23), 'lo2': ('v', 24), 'sg3_0': ('a', 16), 'pr3_0': ('v', 25), 'sg3_1': ('a', 17), 'pr3_1': ('v', 27), 'sg3_2': ('a', 18), 'pr3_2': ('v', 29), 'sg3_3': ('a', 19), 'pr3_3': ('v', 31), 'lo3': ('v', 32)},
    },
    'w_o': {
        "per": {'v': 8, 'a': 4},
        "back": {'res0': ('v', 1), 's10': ('v', 2), 'res1': ('v', 3), 's11': ('v', 4), 'res2': ('v', 5), 's12': ('v', 6), 'res3': ('v', 7), 's13': ('v', 8)},
    },
    'ffn_in': {
        "per": {'v': 4, 'a': 4},
        "back": {'up0': ('v', 1), 'flo0': ('v', 2), 'up1': ('v', 3), 'flo1': ('v', 4)},
    },
    'ffn_out': {
        "per": {'v': 4},
        "back": {'res0': ('v', 1), 'res1': ('v', 2), 'res2': ('v', 3), 'res3': ('v', 4)},
    },
    'odd': {
        "per": {'v': 68, 'a': 32},
        "back": {'l00': ('a', 1), 'l10': ('a', 3), 'dlo00': ('v', 9), 'l20': ('a', 5), 'dlo10': ('v', 15), 'l30': ('a', 7), 'dlo20': ('v', 21), 'sil00': ('a', 9), 'dlo30': ('v', 24), 'sil10': ('a', 10), 'y00': ('v', 25), 'ylo00': ('v', 26), 'y10': ('v', 27), 'ylo10': ('v', 28), 'sil20': ('a', 13), 'sil30': ('a', 14), 'y20': ('v', 29), 'ylo20': ('v', 30), 'y30': ('v', 31), 'ylo30': ('v', 32), 'grp0': ('mm', 10), 'l01': ('a', 17), 'l11': ('a', 19), 'dlo01': ('v', 43), 'l21': ('a', 21), 'dlo11': ('v', 50), 'l31': ('a', 23), 'dlo21': ('v', 57), 'sil01': ('a', 25), 'dlo31': ('v', 60), 'sil11': ('a', 26), 'y01': ('v', 61), 'ylo01': ('v', 62), 'y11': ('v', 63), 'ylo11': ('v', 64), 'sil21': ('a', 29), 'sil31': ('a', 30), 'y21': ('v', 65), 'ylo21': ('v', 66), 'y31': ('v', 67), 'ylo31': ('v', 68), 'grp1': ('mm', 20)},
    },
}
CC = {"ident": 0, "ones": 128, "inv_cnt": 256, "tri_ones": 512, "after": 1024, "past": 1152, "neg": 1280}
NCONST = 1408
N_CHUNKS = 32 + 48 + 16 + 40 + 16 + 24 + 40 + 8 + 44 + 24


class Counter:

    def __init__(self, sem):
        self.sem, self.n, self.loop = sem, 0, None

    def lead(self, engine, n):
        engine.sem_inc(self.sem, n)
        self.n += n

    def on(self, instruction):
        instruction.then_inc(self.sem, 1)
        self.n += 1
        return Mark(self, self.n, self.loop)


class Mark:
    def __init__(self, counter, n, loop):
        self.counter, self.n, self.loop = counter, n, loop

    def prev(self):
        return Mark(self.counter, self.n - self.loop.per[self.counter], self.loop)

    def value(self):
        if self.loop is None:
            return self.n
        per = self.loop.per[self.counter]
        if self.loop.done:
            return self.n + per * (self.loop.count - 1)
        return self.n + self.loop.i * per


class Turns:

    def __init__(self, loop, n):
        self.loop, self.n, self.e, self.last = loop, n, 0, {}

    def at(self, e):
        self.e = e
        return self

    def back(self, name):
        return self.loop.back(f"{name}{self.n - 1}") if self.e == 0 else self.last[name, self.e - 1]

    def note(self, name, mark):
        self.last[name, self.e] = mark
        return self.loop.note(f"{name}{self.e}", mark)


class Loop:

    def __init__(self, i, count, per, back, counters, starts):
        self.i, self.count, self.per, self.done = i, count, per, False
        self.back_at, self.counters, self.starts, self.noted = back, counters, starts, {}

    def back(self, name):
        if name not in self.back_at:
            return None
        which, k = self.back_at[name]
        c = self.counters[which]
        return Mark(c, self.starts[c] + k - self.per[c], self)

    def note(self, name, mark):
        which = next(k for k, c in self.counters.items() if c is mark.counter)
        self.noted[name] = (which, mark.n - self.starts[mark.counter])
        return mark


def program(nc, wts, modw, vecs, consts, x_in, ctx_in, out):
    ctx = ExitStack()
    base0 = (nc.sbuf_base + 31) // 32 * 32
    K = 1024

    def at(name, cols, off, dt=F32):
        return nc.alloc_sbuf_tensor_at(name, [P, cols], dt, offset=base0 + off)

    raw = at("raw", RING * CW, 0)
    w_hi = at("w_hi", RING * CW, 16 * K, F32R)
    w_lo = at("w_lo", RING * CW, 32 * K, F32R)
    X = at("X", NT * T, 48 * K)
    h_hi = at("h_hi", NT * T, 64 * K, F32R)
    h_lo = at("h_lo", NT * T, 80 * K, F32R)
    vec = at("vec", NVEC, 96 * K)
    o_small = 96 * K + (4 * NVEC + 31) // 32 * 32
    small = at("small", 392, o_small)
    o_cst = o_small + 4 * 392
    cst = at("cst", 512, o_cst)
    cst2 = at("cst2", NCONST - 512, o_cst + 2048)
    area = (o_cst + 2048 + 31) // 32 * 32
    area2 = area + 4 * (NCONST - 512)
    limit = nc.sbuf_usable_end - base0

    class Plan:

        def __init__(self, start):
            self.at = start

        def __call__(self, name, cols, dt=F32):
            t = at(name, cols, self.at, dt)
            self.at += (4 * cols + 31) // 32 * 32
            assert self.at <= limit, (name, self.at, limit)
            return t

    banks = ctx.enter_context(nc.psum_tensor("banks", [P, 8 * 512], F32))

    def bank(b, w=512, o=0):
        return banks[:, b * 512 + o:b * 512 + o + w]

    def sem(name):
        return ctx.enter_context(nc.semaphore(name))

    s_raw = [sem(f"s_raw{s}") for s in range(RING)]
    s_vec, s_x, s_ctx, s_cst = sem("s_vec"), sem("s_x"), sem("s_ctx"), sem("s_cst")
    s_cst2 = sem("s_cst2")
    s_mod0 = [sem(f"s_mod0_{j}") for j in range(4)]
    s_mraw = [sem(f"s_mraw{s}") for s in range(MOD_RING)]
    s_out = sem("s_out")
    chunk_hi = Counter(sem("s_hi"))
    chunk_lo = Counter(sem("s_lo"))
    chunk_mm = Counter(sem("s_mm"))
    mod_mm = Counter(sem("s_mod_mm"))
    pe_done = Counter(sem("s_pe"))
    v_done = Counter(sem("s_v"))
    a_done = Counter(sem("s_a"))
    counters = (chunk_hi, chunk_lo, chunk_mm, mod_mm, pe_done, v_done, a_done)

    chunk_mm.lead(nc.tensor, RING)
    mod_mm.lead(nc.tensor, 3)

    state = {"loop": None, "chunk": 0, "split": 0}

    def after(engine, *marks):
        for m in marks:
            if m is not None:
                engine.wait_ge(m.counter.sem, m.value())

    def V(ins):
        return v_done.on(ins)

    def A(ins):
        return a_done.on(ins)

    vector, scalar, tensor = nc.vector, nc.scalar, nc.tensor

    def vop(fn, *args, needs=(), **kw):
        after(vector, *needs)
        return V(fn(*args, **kw))

    def aop(out_ap, in_ap, func, needs=(), **kw):
        after(scalar, *needs)
        return A(scalar.activation(out_ap, in_ap, func, **kw))

    def tt(o, a, b, op, needs=()):
        return vop(vector.tensor_tensor, o, a, b, op, needs=needs)

    def ts(o, a, s1, s2, op0, op1=None, needs=()):
        if op1 is None:
            return vop(vector.tensor_scalar, o, a, s1, None, op0, needs=needs)
        return vop(vector.tensor_scalar, o, a, s1, s2, op0, op1, needs=needs)

    def stt(o, a, s, b, op0, op1, needs=()):
        return vop(vector.scalar_tensor_tensor, o, a, s, b, op0, op1, needs=needs)

    named = {"pe": pe_done, "v": v_done, "a": a_done, "mod": mod_mm, "mm": chunk_mm}

    @contextmanager
    def loop(name, count, chunks=0, banks_free=None):
        table = LOOPS.get(name, {"per": {}, "back": {}})
        rise = {c: 0 for c in counters}
        for c in (chunk_hi, chunk_lo, chunk_mm):
            rise[c] = chunks
        for k, n in table["per"].items():
            rise[named[k]] = n
        starts = {c: c.n for c in counters}
        c0, s0 = state["chunk"], state["split"]
        assert chunks % RING == 0
        v_all, a_all = Mark(v_done, v_done.n, None), Mark(a_done, a_done.n, None)
        after(tensor, *((v_all, a_all) if banks_free is None else banks_free))
        after(scalar, v_all)
        after(vector, a_all)
        with nc.Fori(0, count) as i:
            lp = Loop(i, count, rise, table["back"], named, starts)
            state["loop"] = lp
            for c in counters:
                c.loop = lp
            yield lp
        found = {k: c.n - starts[c] for k, c in named.items() if k != "mm" and c.n > starts[c]}
        found = {"per": found, "back": lp.noted}
        assert found == table, f"LOOPS[{name!r}] = {found}"
        assert state["chunk"] - c0 == chunks and state["split"] - s0 == chunks
        lp.done = True
        state["loop"] = None
        for c in counters:
            c.loop = None
            c.n = starts[c] + count * rise[c]
        state["chunk"] = c0 + count * chunks
        state["split"] = s0 + count * chunks

    def moving(n, per_chunk=1):
        lp = state["loop"]
        if lp is None or not lp.per[chunk_mm]:
            return n
        return n + lp.i * (lp.per[chunk_mm] * per_chunk)

    def split_next():
        c = state["split"]
        last = c >= N_CHUNKS
        state["split"] += 1
        if last:
            return
        s = c % RING
        lp = state["loop"]
        turn = 16 * (c // RING + 1)
        if lp is not None:
            turn = turn + lp.i * (16 * lp.per[chunk_mm] // RING)
        scalar.wait_ge(s_raw[s], turn)
        if c >= RING:
            scalar.wait_ge(chunk_mm.sem, moving(c + 1))
        chunk_hi.on(scalar.activation(w_hi[:, s * CW:(s + 1) * CW], raw[:, s * CW:(s + 1) * CW], ACT.Copy))
        vector.wait_ge(chunk_hi.sem, moving(c + 1))
        chunk_lo.on(vector.tensor_tensor(w_lo[:, s * CW:(s + 1) * CW], raw[:, s * CW:(s + 1) * CW],
                                         w_hi[:, s * CW:(s + 1) * CW].bitcast(F32), ALU.subtract))

    def chunk(groups, needs=(), swap=False, by_part=None):
        split_next()
        c = state["chunk"]
        state["chunk"] += 1
        s = c % RING
        tensor.wait_ge(chunk_lo.sem, moving(c + 1))
        after(tensor, *needs)
        last = None
        for o, parts, start, stop in groups:
            for n, (b, r_hi, r_lo) in enumerate(parts):
                if by_part is not None and last is None or by_part is not None and o is groups[0][0]:
                    after(tensor, by_part[n])
                if swap:
                    hi = w_hi[:, s * CW + b * 256:s * CW + (b + 1) * 256]
                    lo = w_lo[:, s * CW + b * 256:s * CW + (b + 1) * 256]
                    passes = ((r_hi, hi), (r_hi, lo), (r_lo, hi))
                else:
                    hi = w_hi[:, s * CW + b * P:s * CW + (b + 1) * P]
                    lo = w_lo[:, s * CW + b * P:s * CW + (b + 1) * P]
                    passes = ((hi, r_hi), (hi, r_lo), (lo, r_hi))
                for j, (l, r) in enumerate(passes):
                    last = tensor.matmul(o, l, r, start=start and n == 0 and j == 0,
                                         stop=stop and n == len(parts) - 1 and j == 2)
        return chunk_mm.on(last)

    def parts(hi, lo, k0=0, n=KC, w=T, b0=0):
        return [(b0 + k, hi[:, (k0 + k) * w:(k0 + k + 1) * w], lo[:, (k0 + k) * w:(k0 + k + 1) * w]) for k in range(n)]

    def full(o, hi, lo, w=T):
        return [(o, parts(hi, lo, w=w), True, True)]

    def tile(t, f, w=T, stride=None, o=0):
        stride = w if stride is None else stride
        if isinstance(f, int):
            return t[:, f * stride + o:f * stride + o + w]
        return t[:, bass.ds(f * stride + o, w)]

    def col(name, k=0):
        k = VC[name] + k
        return vec[:, k:k + 1] if isinstance(k, int) else vec[:, bass.ds(k, 1)]

    ident, ones = cst[:, 0:P], cst[:, P:2 * P]

    nc.gpsimd.dma_start(vec[:, :], vecs).then_inc(s_vec, 16)
    scalar.dma_start(X[:, :], x_in).then_inc(s_x, 16)
    nc.gpsimd.dma_start(cst[:, :], consts[:, 0:512]).then_inc(s_cst, 16)

    p = Plan(area)
    U = p("U", (NT + 1) * (T + 2 * HALO))
    o_sga = p.at
    hc_hi = p("hc_hi", NT * TC, F32R)
    hc_lo = p("hc_lo", NT * TC, F32R)
    sga = at("sga", NT * T, o_sga)
    o_yb = p.at
    yb_hi = p("yb_hi", NT * T, F32R)
    yb_lo = p("yb_lo", NT * T, F32R)
    mraw = p("mraw", MOD_RING * CW)
    us_hi = p("us_hi", T + 2 * HALO, F32R)
    us_lo = p("us_lo", T + 2 * HALO, F32R)
    csum = p("csum", T)
    u = p("u", T)
    u_hi = p("u_hi", T, F32R)
    u_lo = p("u_lo", T, F32R)
    o_tr = p.at
    tr = [p(f"tr{k}", T) for k in range(2)]
    ti = [p(f"ti{k}", T) for k in range(2)]
    aa = [p(f"aa{k}", T) for k in range(2)]
    xp = p("xp", T + SCONV_K)
    th = [xp[:, SCONV_K // 2:SCONV_K // 2 + T], p("th1", T)]
    tg = p("tg", T)
    mod0 = at("mod0", 16 * CW, o_sga)
    ctx_x = at("ctx_x", NT * TC, o_tr)
    sq, sq2, rstd, rstd_c, ssum = aa[0], aa[1], th[0], th[1], tg
    n_t = [at(f"n_t{k}", T, area + 2 * K * k) for k in range(3)]
    assert o_sga + 64 * K <= o_tr

    nc.gpsimd.dma_start(ctx_x[:, :], ctx_in).then_inc(s_ctx, 16)
    csil = small[:, 0:2 * NT]
    modv0 = small[:, 16:64]
    modv1 = small[:, 64:88]
    g0, g0c, g1 = small[:, 88:96], small[:, 96:104], small[:, 104:112]
    sp4, nsp4 = small[:, 112:128], small[:, 128:144]
    hb_r, hb_i = small[:, 144:160], small[:, 160:176]
    ctx_state = small[:, 176:192]
    tmp16 = [small[:, 192 + 16 * j:208 + 16 * j] for j in range(6)]
    wdt_hi = at("wdt_hi", NT * NH, o_small + 4 * 288, F32R)
    wdt_lo = at("wdt_lo", NT * NH, o_small + 4 * 320, F32R)
    eps_rms, eps_ln = small[:, 352:353], small[:, 353:354]
    cb2, gn, nsp8 = small[:, 354:362], small[:, 362:370], small[:, 370:386]

    for j in range(4):
        scalar.dma_start(mod0[:, j * 4 * CW:(j + 1) * 4 * CW].rearrange("p (a n) -> p a n", a=4),
                         modw[4 * j:4 * j + 4, :, :].rearrange("a p n -> p a n")).then_inc(s_mod0[j], 16)

    for s in range(RING):
        nc.sync.dma_start(raw[:, s * CW:(s + 1) * CW], wts[s, :, :]).then_inc(s_raw[s], 16)
    with nc.sync.Fori(0, N_CHUNKS // RING - 1) as it:
        for s in range(RING):
            nc.sync.wait_ge(chunk_lo.sem, it * RING + s + 1)
            nc.sync.dma_start(raw[:, s * CW:(s + 1) * CW],
                              wts[bass.ds(it * RING + s + RING, 1), :, :].rearrange("a p n -> p (a n)")).then_inc(s_raw[s], 16)

    m_z = vop(vector.memset, small[:, :], 0.0)
    m_e = vop(vector.memset, eps_rms, 1e-6, needs=(m_z,))
    m_e = vop(vector.memset, eps_ln, 4e-5, needs=(m_e,))
    scalar.wait_ge(s_vec, 16)
    vector.wait_ge(s_vec, 16)
    cs3 = csil.rearrange("p (k two) -> p k two", two=2)
    aop(cs3[:, :, 0:1], vec[:, VC["c"]:VC["c"] + NT].rearrange("p (k a) -> p k a", a=1), ACT.Silu, needs=(m_z,))
    m_c = aop(cs3[:, :, 1:2], vec[:, VC["c_ctx"]:VC["c_ctx"] + NT].rearrange("p (k a) -> p k a", a=1), ACT.Silu)

    def softplus16(dst, src, negate, needs):
        z, e, s, s2, acc, t = tmp16
        m = ts(z, src, -1.0 if negate else 1.0, None, ALU.mult, needs=needs)
        m = aop(e, z, ACT.Abs, needs=(m,))
        m_x = aop(e, e, ACT.Exp, scale=-1.0, needs=(m,))
        m = ts(t, e, 2.0, None, ALU.add, needs=(m_x,))
        m = vop(vector.reciprocal, t, t, needs=(m,))
        m = tt(s, e, t, ALU.mult, needs=(m,))
        m = tt(s2, s, s, ALU.mult, needs=(m,))
        m = ts(acc, s2, 1.0 / 15, None, ALU.mult, needs=(m,))
        for k in (13, 11, 9, 7, 5, 3):
            m = stt(acc, acc, 1.0 / k, s2, ALU.add, ALU.mult, needs=(m,))
        m = stt(acc, acc, 1.0, s, ALU.add, ALU.mult, needs=(m,))
        m = ts(z, z, 0.0, None, ALU.max, needs=(m,))
        return stt(dst, acc, 2.0, z, ALU.mult, ALU.add, needs=(m,))

    lam = vec[:, VC["lam"]:VC["lam"] + 16]
    m = softplus16(sp4, lam, True, (m_e,))
    m = ts(nsp4, sp4, -4.0, None, ALU.mult, needs=(m,))
    m = ts(sp4, sp4, 4.0, None, ALU.mult, needs=(m,))
    ts(hb_r, vec[:, VC["b_r"]:VC["b_r"] + 16], 0.5, None, ALU.mult)
    ts(cb2, vec[:, VC["conv_b"]:VC["conv_b"] + NT], 2.0, None, ALU.mult)
    tt(gn, vec[:, VC["final_g"]:VC["final_g"] + NT], vec[:, VC["norm1_g"]:VC["norm1_g"] + NT], ALU.mult)
    ts(nsp8, nsp4, 2.0, None, ALU.mult, needs=(m,))
    m_small = ts(hb_i, vec[:, VC["b_i"]:VC["b_i"] + 16], 0.5, None, ALU.mult, needs=(m,))
    wdt = vec[:, VC["w_dt"]:VC["w_dt"] + NT * NH]
    m = aop(wdt_hi[:, :], wdt, ACT.Copy)
    tt(wdt_lo[:, :], wdt, wdt_hi[:, :].bitcast(F32), ALU.subtract, needs=(m,))

    def add_square(total, src, tmp, needs, gain=1.0, first=False):
        if first:
            return aop(total, src, ACT.Square, scale=gain, needs=needs)
        m = aop(tmp, src, ACT.Square, scale=gain, needs=needs)
        return tt(total, total, tmp, ALU.add, needs=(m,))

    def feature_sum(b, total, w, needs):
        after(tensor, *needs)
        return pe_done.on(tensor.matmul(bank(b, w), ones, total, start=True, stop=True))

    def rms_rstd(dst, src, eps, n, needs):
        m = aop(dst, src, ACT.Sqrt, bias=eps, scale=1.0 / n, needs=needs)
        return vop(vector.reciprocal, dst, dst, needs=(m,))

    tensor.wait_ge(s_cst, 16)
    scalar.wait_ge(s_x, 16)
    vector.wait_ge(s_x, 16)
    m = m_e
    for k in range(NT):
        m = add_square(ssum[:, :], tile(X, k), (sq, sq2)[k % 2][:, :], (m,) if k < 2 else (m2, m), first=k == 0)
        m2 = m
    m = feature_sum(0, ssum[:, :], T, (m,))
    m_rx = rms_rstd(rstd[:, :], bank(0), eps_rms, D, (m,))
    scalar.wait_ge(s_ctx, 16)
    vector.wait_ge(s_ctx, 16)
    for k in range(NT):
        m = add_square(ssum[:, 0:TC], tile(ctx_x, k, TC), (sq, sq2)[k % 2][:, 0:TC], (m,), first=k == 0)
    m = feature_sum(1, ssum[:, 0:TC], TC, (m,))
    m_rc = rms_rstd(rstd_c[:, 0:TC], bank(1, TC), eps_rms, D, (m,))

    after(tensor, m_c)
    for j in range(16):
        if j % 4 == 0:
            tensor.wait_ge(s_mod0[j // 4], 16)
        for k in range(KC):
            last = tensor.matmul(bank(2, 2, 2 * j), mod0[:, j * CW + k * P:j * CW + (k + 1) * P],
                                 csil[:, 2 * k:2 * k + 2], start=k == 0, stop=k == KC - 1)
    m = pe_done.on(last)

    def bias_mod(tiles, t0, b, two, dst, layer, needs):
        mb = vec[:, VC["mod_b"] + 24 * layer + t0:VC["mod_b"] + 24 * layer + t0 + tiles].rearrange("p (k a) -> p k a", a=1)
        for j in range(two):
            d = dst[:, t0 * two:(t0 + tiles) * two].rearrange("p (k a) -> p k a", a=two)[:, :, j:j + 1]
            s = bank(b, tiles * 2, t0 * 2).rearrange("p (k a) -> p k a", a=2)[:, :, j:j + 1]
            m = tt(d, s, mb, ALU.add, needs=needs)
        return m

    m = bias_mod(16, 0, 2, 2, modv0, 0, (m, m_small))
    mv0 = modv0.rearrange("p (k two) -> p k two", two=2)
    ng = lambda l: vec[:, VC["norm_g"] + NT * l:VC["norm_g"] + NT * (l + 1)].rearrange("p (k a) -> p k a", a=1)
    stt(g0.rearrange("p (k a) -> p k a", a=1), mv0[:, 8:16, 0:1], 1.0, ng(0), ALU.add, ALU.mult, needs=(m,))
    m_g0 = stt(g0c.rearrange("p (k a) -> p k a", a=1), mv0[:, 8:16, 1:2], 1.0, ng(0), ALU.add, ALU.mult)

    def norm_split(src, w, r, gain, shift, hi, lo, tmps, needs, n=NT, also=None):
        marks, pend = [], None
        used = [None] * len(tmps)

        def finish(k, t, m2):
            if shift is None:
                m = tt(tile(lo, k, w), t, tile(hi, k, w).bitcast(F32), ALU.subtract, needs=(m2,))
            else:
                m = stt(tile(lo, k, w), t, shift(k), tile(hi, k, w).bitcast(F32), ALU.add, ALU.subtract, needs=(m2,))
            used[k % len(tmps)] = m
            marks.append(m)

        for k in range(n):
            t = tmps[k % len(tmps)][:, 0:w]
            m1 = stt(t, tile(src, k, w), gain(k), r, ALU.mult, ALU.mult, needs=(*needs, used[k % len(tmps)]))
            if shift is None:
                m2 = aop(tile(hi, k, w), t, ACT.Copy, needs=(m1,))
            else:
                m2 = aop(tile(hi, k, w), t, ACT.Identity, bias=shift(k), needs=(m1,))
            if also is not None:
                also(k, m1)
            if pend is not None:
                finish(*pend)
            pend = (k, t, m2)
        finish(*pend)
        return marks

    for _ in range(AHEAD):
        split_next()
    m_hc = norm_split(ctx_x, TC, rstd_c[:, 0:TC], lambda k: g0c[:, k:k + 1], lambda k: modv0[:, 2 * k + 1:2 * k + 2],
                      hc_hi, hc_lo, n_t, (m_g0, m_rc))
    m_h = norm_split(X, T, rstd[:, :], lambda k: g0[:, k:k + 1], lambda k: modv0[:, 2 * k:2 * k + 1],
                     h_hi, h_lo, n_t, (m_rx, m_hc[-1]))

    UW = T + 2 * HALO
    u3 = U[:, :].rearrange("p (f w) -> p f w", w=UW)
    vop(vector.memset, u3[:, :, 0:HALO], 0.0, needs=(m_h[-1],))
    vop(vector.memset, u3[:, :, HALO + T:UW], 0.0)
    vop(vector.memset, xp[:, :], 0.0)
    m_zero = vop(vector.memset, ctx_state, 0.0)


    def mod_chunk(slot, turn, o, needs=()):
        tensor.wait_ge(s_mraw[slot], turn)
        after(tensor, *needs)
        for k in range(KC):
            last = tensor.matmul(o, mraw[:, slot * CW + k * P:slot * CW + (k + 1) * P],
                                 csil[:, 2 * k:2 * k + 2], start=k == 0, stop=k == KC - 1)
        return mod_mm.on(last)

    def head_input(i, w, xb_bank, m_xb, lp, u_read=None):
        m_xp = lp.note("xp", aop(xp[:, 2:2 + w], xb_bank, ACT.Copy, needs=(m_xb, lp.back("conv"), lp.back("th_read"))))
        sw = lambda k: col("sconv_w", i * SCONV_K + k)
        m = ts(u[:, 0:w], xp[:, 0:w], sw(0), col("sconv_b", i), ALU.mult, ALU.add, needs=(m_xp, u_read))
        for k in range(1, SCONV_K):
            m = stt(u[:, 0:w], xp[:, k:k + w], sw(k), u[:, 0:w], ALU.mult, ALU.add, needs=(m,))
        lp.note("conv", m)
        m = aop(u_hi[:, 0:w], u[:, 0:w], ACT.Copy, needs=(m, lp.back("gates")))
        return tt(u_lo[:, 0:w], u[:, 0:w], u_hi[:, 0:w].bitcast(F32), ALU.subtract, needs=(m,))

    def head_scan(i, w, m_gates, gates, init, lp, part=None, got=None):
        m_t, m_iu, res = [], [], []
        if part == 1:
            return head_scan_end(w, got, init, lp)
        for k in range(2):
            c = i * 2 + k
            at_c = lambda o: small[:, bass.ds(o + c, 1)]
            m_r = aop(tr[k][:, 0:w], gates[2 * k], ACT.Tanh, bias=at_c(144), scale=0.5, needs=(m_gates, lp.back("scans")))
            m_i = aop(ti[k][:, 0:w], gates[2 * k + 1], ACT.Tanh, bias=at_c(160), scale=0.5)
            aop(aa[k][:, 0:w], tr[k][:, 0:w], ACT.Exp, bias=at_c(128), scale=at_c(128), needs=(m_r,))
            m_h = aop(th[k][:, 0:w], tr[k][:, 0:w], ACT.Tanh, bias=at_c(112), scale=at_c(112))
            m_2 = aop(tr[k][:, 0:w], tr[k][:, 0:w], ACT.Exp, bias=at_c(370), scale=at_c(370))
            m_t.append((m_i, m_2))
        lp.note("gate_read", m_i)
        for k in range(2):
            m_i, m_h = m_t[k]
            m_v = stt(th[k][:, 0:w], tr[k][:, 0:w], 1.0, th[k][:, 0:w], ALU.add, ALU.mult, needs=(m_h,))
            m = stt(ti[k][:, 0:w], ti[k][:, 0:w], 1.0, u[:, 0:w], ALU.add, ALU.mult)
            m_iu.append((m_v, m))
        return m_iu if part == 0 else head_scan_end(w, m_iu, init, lp)

    def head_scan_end(w, m_iu, init, lp):
        res = []
        for k in range(2):
            m_s = aop(th[k][:, 0:w], th[k][:, 0:w], ACT.Sqrt, scale=0.25, needs=(m_iu[k][0],))
            m = tt(ti[k][:, 0:w], ti[k][:, 0:w], th[k][:, 0:w], ALU.mult, needs=(m_s, m_iu[k][1]))
            if k == 0:
                lp.note("th_read", m)
            o, d0, d1 = (t[:, 0:w] if k == 0 else t[:, 0:w][:, ::-1] for t in (tr[k], aa[k], ti[k]))
            res.append(vop(vector.tensor_tensor_scan, o, d0, d1, init(k), ALU.mult, ALU.add, needs=(m,)))
        lp.note("scans", res[-1])
        return res

    nc.gpsimd.wait_ge(pe_done.sem, pe_done.n)
    nc.gpsimd.wait_ge(v_done.sem, v_done.n)
    with loop("va", NT, chunks=4, banks_free=(m_e,)) as lp:
        i = lp.i
        nc.gpsimd.wait_ge(mod_mm.sem, i + 3)
        nc.gpsimd.dma_start(mraw[:, 0:CW], modw[bass.ds(i + 16, 1), :, :].rearrange("a p n -> p (a n)")).then_inc(s_mraw[0], 16)
        m_xb = chunk(full(bank(4, TC), hc_hi, hc_lo, w=TC), needs=(lp.back("xp"),), by_part=m_hc)
        m_u = head_input(i, TC, bank(4, TC), m_xb, lp)
        m_vg = chunk(full(bank(1), h_hi, h_lo), needs=(lp.back("sig"),), by_part=m_h)
        m_sig = lp.note("sig", aop(tg[:, :], bank(1), ACT.Tanh, scale=0.5, needs=(m_vg, lp.back("uu"))))
        m_va = chunk(full(bank(0), h_hi, h_lo), needs=(lp.back("uu"),))
        lp.note("uu", stt(tile(U, i, T, UW, UW + HALO), tg[:, :], 1.0, bank(0), ALU.add, ALU.mult, needs=(m_va, m_sig)))
        gates = [bank(5, TC), bank(5, TC, TC), bank(6, TC), bank(6, TC, TC)]
        m_gt = lp.note("gates", chunk([(o, [(b, u_hi[:, 0:TC], u_lo[:, 0:TC])], True, True) for b, o in enumerate(gates)],
                                      needs=(m_u, lp.back("gate_read"))))
        mod_chunk(0, 16 * (i + 1), banks[:, bass.ds(2 * 512 + 32 + 2 * i, 2)])
        res = head_scan(i, TC, m_gt, gates, lambda k: 0.0, lp)
        for k in range(2):
            vop(vector.tensor_copy, small[:, bass.ds(176 + i * 2 + k, 1)], tr[k][:, (TC - 1, 0)[k]:(TC, 1)[k]], needs=(res[k],))

    m = vop(vector.memset, xp[:, :], 0.0)
    after(scalar, m)
    vop(vector.memset, csum[:, :], 0.0)
    nc.gpsimd.wait_ge(mod_mm.sem, NT + 3)
    with loop("heads", NT // 2, chunks=12) as lp:
        turns = Turns(lp, 2)
        for e in range(2):
            i, tn = lp.i * 2 + e, turns.at(e)
            for j in range(3):
                n = 3 * e + j
                nc.gpsimd.wait_ge(mod_mm.sem, lp.i * 6 + n + NT + 3 + 1 - MOD_RING)
                nc.gpsimd.dma_start(mraw[:, n % 2 * CW:(n % 2 + 1) * CW],
                                    modw[bass.ds(lp.i * 6 + n + 24, 1), :, :].rearrange("a p n -> p (a n)")).then_inc(s_mraw[n % 2], 16)

            def taps(k0, k1):
                acc = tile(U, i, T, UW)
                for k in range(k0, k1):
                    src, w = tile(U, i, T, UW, UW + k), col("conv_w", i * CONV_K + k)
                    if k == PE_TAPS:
                        m = ts(acc, src, w, small[:, bass.ds(354 + i, 1)], ALU.mult, ALU.add, needs=(tn.back("taps"),))
                    else:
                        m = stt(acc, src, w, acc, ALU.mult, ALU.add, needs=(Mark(v_done, v_done.n, lp),))
                return m

            m_xb = chunk(full(bank(0), h_hi, h_lo), needs=(tn.back("sga"),))
            m = aop(us_hi[:, :], tile(U, i, UW, UW, UW), ACT.Copy, needs=(tn.back("conv_pe"),))
            m_us = tt(us_lo[:, :], tile(U, i, UW, UW, UW), us_hi[:, :].bitcast(F32), ALU.subtract, needs=(m,))
            m_u = head_input(i, T, bank(0), m_xb, tn, tn.back("yb_lo"))
            m_gb = chunk(full(bank(1), h_hi, h_lo), needs=(tn.back("sgb"),))
            taps(PE_TAPS, 20)
            m = aop(tg[:, :], bank(1), ACT.Tanh, scale=0.5, needs=(m_gb, tn.back("yb_lo")))
            m_sgb = tn.note("sgb", stt(tg[:, :], tg[:, :], 1.0, bank(1), ALU.add, ALU.mult, needs=(m,)))
            gates = [bank(4), bank(5), bank(6), bank(7)]
            m_gt = tn.note("gates", chunk([(o, [(b, u_hi[:, :], u_lo[:, :])], True, True) for b, o in enumerate(gates)],
                                          needs=(m_u, tn.back("gate_read"))))
            m_ga = chunk(full(bank(0), h_hi, h_lo), needs=(tn.last["xp", e],))
            res_v = head_scan(i, T, m_gt, gates, lambda k: small[:, bass.ds(176 + i * 2 + k, 1)], tn, part=0)
            for half in range(2):
                m_cv = chunk([(bank(3), [(b, us_hi[:, 8 * half + b:8 * half + b + T], us_lo[:, 8 * half + b:8 * half + b + T])
                                         for b in range(KC)], half == 0, half == 1)],
                             needs=(m_us, tn.back("conv_sum")) if half == 0 else ())
            tn.note("conv_pe", m_cv)
            for j in range(3):
                n = 3 * e + j
                mod_chunk(n % 2, lp.i * 48 + 16 * ((NT if n % 2 == 0 else 0) + n // 2 + 1), banks[:, bass.ds(2 * 512 + 64 + 6 * i + 2 * j, 2)])
            m = aop(tile(sga, i), bank(0), ACT.Tanh, scale=0.5, needs=(m_ga,))
            tn.note("sga", stt(tile(sga, i), tile(sga, i), 1.0, bank(0), ALU.add, ALU.mult, needs=(m,)))
            taps(20, 26)
            res = head_scan(i, T, m_gt, gates, lambda k: small[:, bass.ds(176 + i * 2 + k, 1)], tn, part=1, got=res_v)
            m = tt(u[:, :], tr[0][:, :], tr[1][:, :], ALU.add, needs=res)
            m = stt(u[:, :], u[:, :], 0.5, tg[:, :], ALU.mult, ALU.mult, needs=(m, m_sgb))
            m = aop(tile(yb_hi, i), u[:, :], ACT.Copy, needs=(m,))
            m_1 = tn.note("taps", taps(26, CONV_K))
            m_1 = tn.note("conv_sum", tt(tile(U, i, T, UW), bank(3), tile(U, i, T, UW), ALU.add, needs=(m_1, m_cv)))
            m_taps = tt(csum[:, :], csum[:, :], tile(U, i, T, UW), ALU.add, needs=(m_1,))
            m_yb = tn.note("yb_lo", tt(tile(yb_lo, i), u[:, :], tile(yb_hi, i).bitcast(F32), ALU.subtract, needs=(m,)))

    after(vector, Mark(mod_mm, mod_mm.n, None))
    bias_mod(8, 16, 2, 2, modv0, 0, ())
    mb1 = vec[:, VC["mod_b"] + 24:VC["mod_b"] + 48].rearrange("p (k a) -> p k a", a=1)
    m = tt(modv1.rearrange("p (k a) -> p k a", a=1), bank(2, 48, 64).rearrange("p (k two) -> p k two", two=2)[:, :, 0:1], mb1, ALU.add)
    m = stt(g1, modv1[:, 8:16], 1.0, vec[:, VC["norm_g"] + NT:VC["norm_g"] + 2 * NT], ALU.add, ALU.mult, needs=(m,))
    mu, rs, s_a, ssq = aa[0], aa[1], (tr[0], tr[1]), ti[0]
    s_b, s_c = (th[0], th[1], u), (ti[1], tg, tr[0])
    m_sum = feature_sum(0, csum[:, :], T, (m_taps, m))
    m_bank = [None] * 4
    after(tensor, m_yb)
    for f in range(4):
        chunk([(bank(4 + f), parts(yb_hi, yb_lo), True, False)])
    m_mu = ts(mu[:, :], bank(0), 1.0 / D, None, ALU.mult, needs=(m_sum,))
    pend, m_sq = None, [None, None]
    for k in range(NT + 1):
        if k < NT:
            m1 = tt(tile(U, k, T, UW), tile(U, k, T, UW), mu[:, :], ALU.subtract, needs=(m_mu,))
            m1 = aop(ssq[:, :] if k == 0 else s_a[k % 2][:, :], tile(U, k, T, UW), ACT.Square, needs=(m1, m_sq[k % 2]))
        if k > 1:
            m_sq[(k - 1) % 2] = m = tt(ssq[:, :], ssq[:, :], s_a[(k - 1) % 2][:, :], ALU.add, needs=(pend, m_sq[k % 2]))
        pend = m1
    m = feature_sum(1, ssq[:, :], T, (m,))
    m_rs = rms_rstd(rs[:, :], bank(1), eps_ln, D, (m,))
    m_ya, pend1, pend2, m_hi2, used = [], None, None, None, [None] * 3
    for k in range(NT + 2):
        if k < NT:
            m = stt(s_b[k % 3][:, :], tile(U, k, T, UW), col("ln_g", k), rs[:, :], ALU.mult, ALU.mult, needs=(m_rs, used[k % 3]))
            m_si = aop(s_c[k % 3][:, :], s_b[k % 3][:, :], ACT.Silu, bias=col("ln_b", k), needs=(m,))
        if 0 < k <= NT:
            j = k - 1
            m = stt(s_b[j % 3][:, :], s_c[j % 3][:, :], 0.5, tile(sga, j), ALU.mult, ALU.mult, needs=(pend1,))
            m_hi2 = aop(tile(h_hi, j), s_b[j % 3][:, :], ACT.Copy, needs=(m,))
        if k > 1:
            j = k - 2
            m = used[j % 3] = tt(tile(h_lo, j), s_b[j % 3][:, :], tile(h_hi, j).bitcast(F32), ALU.subtract, needs=(pend2,))
            m_ya.append(m)
        pend1, pend2 = m_si, m_hi2

    p = Plan(area)
    d_hi = p("d_hi", 2 * NT * T, F32R)
    d_lo = p("d_lo", 2 * NT * T, F32R)
    o_o = p.at
    s1, s2, sqa, sqb = (at(f"s_{n}", T, limit // 32 * 32 - 2 * K * (n + 1)) for n in range(4))
    after(scalar, m_ya[-1])
    after(vector, m_ya[-1])

    def residual(f, b, gate, needs, note=lambda m: m, total=None, first=False):
        if gate is None:
            m = note(tt(tile(X, f), bank(b), tile(X, f), ALU.add, needs=needs))
        else:
            m = note(stt(tile(X, f), bank(b), gate, tile(X, f), ALU.mult, ALU.add, needs=needs))
        return m

    m_sqf = None
    for half in range(2):
        for j in range(4):
            f = 4 * half + j
            if half:
                chunk([(bank(4 + j), parts(yb_hi, yb_lo), True, False)], needs=(m_bank[j],))
        for j in range(4):
            f = 4 * half + j
            m = chunk([(bank(4 + j), parts(h_hi, h_lo), False, True)], by_part=m_ya if f == 0 else None)
            m_bank[j] = residual(f, 4 + j, modv0[:, 32 + 2 * f:33 + 2 * f], (m,))
            m_sqf = add_square(s1[:, :], tile(X, f), sqa[:, :], (m_bank[j], m_sqf), first=f == 0)
    m_x = m_sqf

    p = Plan(area)
    y1_hi = p("y1_hi", 2 * NT * T, F32R)
    y1_lo = p("y1_lo", 2 * NT * T, F32R)
    d_hi = p("d_hi", 4 * T, F32R)
    d_lo = p("d_lo", 4 * T, F32R)
    LW = 88
    lev0 = [p(f"lev0_{k}", 8 * LW) for k in range(2)]
    lev = p("lev", POOL_LEVELS * 8 * LW)
    sg = [p(f"sg{k}", T) for k in range(2)]
    rstd, nt_ = lev0[0][:, 0:T], [lev[:, T * k:T * (k + 1)] for k in range(3)]

    m_free = Mark(chunk_mm, chunk_mm.n, None)
    after(scalar, m_free)
    after(vector, m_free)
    m = feature_sum(7, s1[:, :], T, (m_x,))
    m = rms_rstd(rstd, bank(7), eps_rms, D, (m,))
    m_hk = norm_split(X, T, rstd, lambda k: g1[:, k:k + 1], lambda k: modv1[:, k:k + 1], h_hi, h_lo, nt_, (m,))
    m = vop(vector.memset, lev0[0][:, :], 0.0, needs=(m_hk[-1],))
    vop(vector.memset, lev0[1][:, :], 0.0)
    vop(vector.memset, lev[:, :], 0.0)

    rows = lambda ap, w: ap.rearrange("p (r w) -> p r w", w=w)
    PADL = 8
    with loop("odd", 2, chunks=20, banks_free=(m_x,)) as lp:
        turns = Turns(lp, 2)
        for gg in range(2):
            tn, group = turns.at(gg), lp.i * 2 + gg
            m_l, m_sub, m_dhi, m_dlo = [], [], [], []

            def d_low(j):
                c = rows(lev0[j % 2][:, :], LW)[:, :, PADL:PADL + ROW]
                m_dlo.append(tn.note(f"dlo{j}", tt(rows(tile(d_lo, j), ROW), c, rows(tile(d_hi, j).bitcast(F32), ROW),
                                                   ALU.subtract, needs=(m_dhi[j],))))

            for j in range(4):
                m = chunk(full(bank(j % 2), h_hi, h_lo), needs=(m_l[j - 2] if j > 1 else tn.back(f"l{j + 2}"),),
                          by_part=m_hk if gg == 0 and j == 0 else None)
                l0 = rows(lev0[j % 2][:, :], LW)
                c0 = l0[:, :, PADL:PADL + ROW]
                m_l.append(tn.note(f"l{j}", aop(c0, rows(bank(j % 2), ROW), ACT.Copy,
                                                needs=(m, m_dlo[j - 2] if j > 1 else tn.back(f"dlo{j + 2}")))))
                below, m, shift0 = l0, m_l[j], 0
                for g in range(POOL_LEVELS - 1 + gg):
                    w = 2 << g
                    n = PADL + ROW + PADL - w + 1
                    here = rows(lev[:, g * 8 * LW:(g + 1) * 8 * LW], LW)
                    m = tt(here[:, :, w // 2:w // 2 + n], below[:, :, shift0:shift0 + n],
                           below[:, :, shift0 + w // 2:shift0 + w // 2 + n], ALU.add, needs=(m,))
                    below, shift0 = here, w // 2
                if j:
                    d_low(j - 1)
                sums = rows(lev[:, bass.ds(group * (8 * LW), 8 * LW)], LW)[:, :, PADL:PADL + ROW]
                inv = cst[:, bass.ds(group * ROW + 2 * P, ROW)].rearrange("p (a w) -> p a w", a=1).to_broadcast([P, 8, ROW])
                m = tt(sums, sums, inv, ALU.mult, needs=(m,))
                m = tt(c0, sums, c0, ALU.subtract, needs=(m,))
                m_dhi.append(aop(rows(tile(d_hi, j), ROW), c0, ACT.Copy, needs=(m, tn.back("grp"))))
            for half in range(2):
                m_s = []
                for e in range(2):
                    t = 2 * half + e
                    m = chunk(full(bank(2 + e), h_hi, h_lo), needs=(m_sil[e] if half else tn.back(f"sil{2 + e}"),))
                    free = m_ylo[e] if half else tn.back(f"ylo{2 + e}")
                    m_s.append(tn.note(f"sil{t}", aop(sg[e][:, :], bank(2 + e), ACT.Silu, needs=(m, free))))
                    if t == 0:
                        d_low(3)
                m_sil = m_s
                dp = [[(4 * e + k, tile(d_hi, k), tile(d_lo, k)) for k in range(4)] for e in range(2)]
                m_g = chunk([(bank(4 + 2 * half + e), dp[e], True, True) for e in range(2)],
                            needs=(m_dlo[3], tn.back(f"y{2 * half + 1}")))
                m_yl = []
                for e in range(2):
                    t = 2 * half + e
                    f = group * 4 + t
                    m = tn.note(f"y{t}", stt(sg[e][:, :], bank(4 + t), col("od_scale", f), sg[e][:, :], ALU.mult, ALU.mult,
                                             needs=(m_g, m_sil[e])))
                    m = aop(tile(y1_hi, f), sg[e][:, :], ACT.Copy, needs=(m,))
                    m_yl.append(tn.note(f"ylo{t}", tt(tile(y1_lo, f), sg[e][:, :], tile(y1_hi, f).bitcast(F32), ALU.subtract, needs=(m,))))
                m_ylo = m_yl
            tn.note("grp", m_g)

    m = vop(vector.memset, s1[:, :], 0.0, needs=(m_ylo[1],))
    m = vop(vector.memset, s2[:, :], 0.0)
    with loop("od_out", NT // 2, chunks=4) as lp:
        turns = Turns(lp, 2)
        for j in range(2):
            tn = turns.at(j)
            f = lp.i * 2 + j
            chunk([(bank(j), parts(y1_hi, y1_lo), True, False)], needs=(lp.back(f"res{j}"),))
            m = chunk([(bank(j), [(k, tile(y1_hi, KC + k), tile(y1_lo, KC + k)) for k in range(KC)], False, True)])
            m_x = tn.note("res", stt(tile(X, f), bank(j), small[:, bass.ds(64 + 16 + f, 1)], tile(X, f), ALU.mult, ALU.add, needs=(m,)))
            tn.note("s1", add_square(s1[:, :], tile(X, f), sqa[:, :], (m_x, tn.back("s1"))))
            m_s2 = tn.note("s2", add_square(s2[:, :], tile(X, f), sqb[:, :], (m_x, tn.back("s2")), gain=col("final_g", f)))

    p = Plan(area2)
    y_hi = p("y_hi", 8 * T, F32R)
    y_lo = p("y_lo", 8 * T, F32R)
    o_m = p.at
    qk0 = p("qk0", 4 * T)
    vv0 = p("vv0", NB * 256)
    XW = T + SSM_K
    cpad = [p(f"cpad{k}", XW) for k in range(2)]
    ct = [p(f"ct{k}", T) for k in range(2)]
    M = at("M", NT * T, o_m)
    gs = [at("gs0", T, o_m + 16 * K), at("gs1", T, o_m + 18 * K)]
    assert o_m + 20 * K <= p.at
    o_2 = p.at
    qk1 = p("qk1", 4 * T)
    vv1 = p("vv1", NB * 256)
    zs = p("zs", 2 * T)
    bc = p("bc", 4 * T)
    ew = [p(f"ew{k}", CAUSAL) for k in range(3)]
    xd = p("xd", NB * 256)
    abc = p("abc", T)
    dtv, av, acs, mx, nl = p("dtv", 16), p("av", 16), p("acs", 16), p("mx", NB), p("nl", NB)
    gs += [p("gs2", T), p("gs3", T)]
    m_hi = at("m_hi", NT * T, o_2, F32R)
    m_lo_ = at("m_lo", NT * T, o_2 + 16 * K, F32R)
    yt = [at(f"yt{k}", T, o_2 + 2 * K * k) for k in range(2)]

    rstd, r2, nt_ = zs[:, 0:T], zs[:, T:2 * T], [bc[:, T * k:T * (k + 1)] for k in range(3)]
    m_mm = Mark(chunk_mm, chunk_mm.n, None)
    after(vector, m_mm, m_s2)
    after(scalar, m_mm, m_s2)
    after(nc.gpsimd, m_s2, m_mm)
    nc.gpsimd.dma_start(cst2[:, :], consts[:, 512:NCONST]).then_inc(s_cst2, 16)
    tri_ones, after_m = cst2[:, 0:512], cst2[:, 512:640]
    past, neg = cst2[:, 640:768], cst2[:, 768:896]
    tri = tri_ones[:, 0:P]

    m = feature_sum(6, s1[:, :], T, (m_s2,))
    m_q = feature_sum(7, s2[:, :], T, ())
    m = rms_rstd(rstd, bank(6), eps_rms, D, (m,))
    m = tt(r2, bank(7), rstd, ALU.mult, needs=(m, m_q))
    m = tt(r2, r2, rstd, ALU.mult, needs=(m,))
    m = rms_rstd(r2, r2, eps_rms, D, (m,))
    m = tt(r2, r2, rstd, ALU.mult, needs=(m,))

    def first_norm(k, m_read):
        if k:
            stt(tile(X, k - 1), tile(X, k - 1), col("final_g", k - 1), rstd, ALU.mult, ALU.mult)

    m_hk = norm_split(X, T, r2, lambda k: gn[:, k:k + 1], None, h_hi, h_lo, nt_, (m,), also=first_norm)
    m_h = stt(tile(X, NT - 1), tile(X, NT - 1), col("final_g", NT - 1), rstd, ALU.mult, ALU.mult, needs=(m_hk[-1],))

    after(scalar, m_h)
    vop(vector.memset, cpad[0][:, :], 0.0)
    m_pad = vop(vector.memset, cpad[1][:, :], 0.0)
    bank_free = {b: m_s2 for b in range(4, 8)}
    turn_b = [0]

    def next_bank():
        turn_b[0] = (turn_b[0] + 1) % 4
        return 4 + turn_b[0]

    def split_y(f, src, needs):
        m = aop(tile(y_hi, f), src, ACT.Copy, needs=needs)
        return tt(tile(y_lo, f), src, tile(y_hi, f).bitcast(F32), ALU.subtract, needs=(m,))

    done = {}

    def taps_of(dst, src, name, t, n, first, needs):
        for k in range(n):
            a, w = src[:, first + k:first + k + T], col(name, t * n + k)
            if k == 0:
                m = ts(dst, a, w, None, ALU.mult, needs=needs)
            else:
                m = stt(dst, a, w, dst, ALU.mult, ALU.add, needs=(m,))
        return m

    def inputs_a():
        m_y = None
        for t in range(2):
            marks, bs = [], []
            for n in range(3):
                b = next_bank()
                bs.append(b)
                marks.append(chunk(full(bank(b), h_hi, h_lo), needs=(bank_free[b],), by_part=m_hk if t + n == 0 else None))
                if n == 0:
                    bank_free[b] = m = aop(ct[t][:, :], bank(b), ACT.Copy, needs=(marks[0], m_pad))
                if n == 1:
                    bank_free[b] = m = tt(cpad[t][:, SSM_K - 1:SSM_K - 1 + T], bank(b), ct[t][:, :], ALU.mult, needs=(m, marks[1]))
                    m = taps_of(ct[t][:, :], cpad[t], "conv_a_w", t, SHORT_K, 1, (m,))
                if n == 2:
                    bank_free[b] = m = tt(ct[t][:, :], bank(b), ct[t][:, :], ALU.mult, needs=(m, marks[2]))
                    done["ya"] = split_y(t, ct[t][:, :], (m,))
                yield

    def inputs_qkv(n, qk, vv):
        for t in range(4):
            b = next_bank()
            m = chunk(full(bank(b), h_hi, h_lo), needs=(bank_free[b],))
            bank_free[b] = done["qk", n] = aop(tile(qk, t), bank(b), ACT.Copy, needs=(m,))
            yield
        for half in range(2):
            groups = []
            for tb in range(NB):
                pr = [(k, h_hi[:, (4 * half + k) * T + tb * P:(4 * half + k) * T + (tb + 1) * P],
                       h_lo[:, (4 * half + k) * T + tb * P:(4 * half + k) * T + (tb + 1) * P]) for k in range(4)]
                groups.append((bank(4 + tb, 256), pr, half == 0, half == 1))
            m = chunk(groups, needs=[bank_free[4 + tb] for tb in range(NB)] if half == 0 else (), swap=True)
            if half == 0:
                yield
        for tb in range(NB):
            bank_free[4 + tb] = done["v", n] = aop(vv[:, tb * 256:(tb + 1) * 256], bank(4 + tb, 256), ACT.Copy, needs=(m,))
        yield

    def inputs_c():
        for t in range(2):
            b = next_bank()
            m = chunk(full(bank(b), h_hi, h_lo), needs=(bank_free[b],))
            bank_free[b] = aop(tile(zs, t), bank(b), ACT.Silu, needs=(m,))
            yield
        m_tap, m_act = [done["ya"]] * 2, [None, None]
        for t in range(4):
            b = next_bank()
            m = chunk(full(bank(b), h_hi, h_lo), needs=(bank_free[b],))
            bank_free[b] = m = aop(cpad[t % 2][:, SSM_K - 1:SSM_K - 1 + T], bank(b), ACT.Copy, needs=(m, m_tap[t % 2]))
            m_tap[t % 2] = m = taps_of(ct[t % 2][:, :], cpad[t % 2], "ssm_conv_w", t, SSM_K, 0, (m, m_act[t % 2]))
            done["bc"] = m_act[t % 2] = aop(tile(bc, t), ct[t % 2][:, :], ACT.Silu, bias=col("ssm_conv_b", t), needs=(m,))
            if t == 3:
                b = next_bank()
                after(tensor, bank_free[b])
                for tb in range(NB):
                    for k in range(NT):
                        hh, hl = (h[:, k * T + tb * P:k * T + (tb + 1) * P] for h in (h_hi, h_lo))
                        wh, wl = (w[:, k * NH:(k + 1) * NH] for w in (wdt_hi, wdt_lo))
                        for j, (l, r) in enumerate(((hh, wh), (hh, wl), (hl, wh))):
                            last = tensor.matmul(bank(b, NH, tb * NH), l, r, start=k == 0 and j == 0, stop=k == NT - 1 and j == 2)
                m = pe_done.on(last)
                bank_free[b] = m = tt(av[:, :], bank(b, 16), vec[:, VC["dt_bias"]:VC["dt_bias"] + 16], ALU.add, needs=(m,))
                m = softplus16(dtv[:, :], av[:, :], False, (m,))
                m_e = aop(av[:, :], vec[:, VC["a_log"]:VC["a_log"] + 16], ACT.Exp, needs=(m,))
                done["a"] = stt(av[:, :], av[:, :], -1.0, dtv[:, :], ALU.mult, ALU.mult, needs=(m_e,))
            yield

    m_gs = [None] * 4

    def merge(n, br, first, last):
        for half in range(2):
            bs, m_s = [], []
            for j in range(4):
                b = 4 + j
                m = chunk(full(bank(b), h_hi, h_lo), needs=(bank_free[b],))
                bank_free[b] = m = aop(gs[j][:, :], bank(b), ACT.Sigmoid, needs=(m, m_gs[j], done["gs"]))
                m_s.append(m)
                yield
            m = chunk([(bank(4 + j), [(2 * j + k, tile(y_hi, 2 * br + k), tile(y_lo, 2 * br + k)) for k in range(2)], True, True)
                       for j in range(4)], needs=(*m_s, done[n]))
            for j in range(4):
                f = 4 * half + j
                if first:
                    bank_free[4 + j] = m_gs[j] = tt(tile(M, f), bank(4 + j), gs[j][:, :], ALU.mult, needs=(m, m_s[j]))
                    continue
                bank_free[4 + j] = m1 = tt(gs[j][:, :], bank(4 + j), gs[j][:, :], ALU.mult, needs=(m, m_s[j]))
                m_gs[j] = m1 = tt(tile(M, f), gs[j][:, :], tile(M, f), ALU.add, needs=(m1,))
                if last:
                    m1 = aop(tile(m_hi, f), tile(M, f), ACT.Copy, needs=(m1,))
                    done["m", f] = tt(tile(m_lo_, f), tile(M, f), tile(m_hi, f).bitcast(F32), ALU.subtract, needs=(m1,))
            yield

    def blk(t, n, w=None):
        return t[:, OFF[n]:OFF[n] + (T - P * n if w is None else w)]

    def pblk(b, n, w=None, o=0):
        s = b * 512 + OFF[n] + o
        return banks[:, s:s + (T - P * n if w is None else w)]

    wide = lambda b: banks[:, b * 512:b * 512 + CAUSAL]
    scale = HD ** -0.5
    OUT = 3

    def weighted_values(h, vv, w):
        p0 = HD * (h % 2)
        for n in range(NB):
            last = tensor.matmul(banks[p0:p0 + HD, OUT * 512 + n * P:(OUT + 1) * 512],
                                 vv[:, n * 256 + h * HD:n * 256 + (h + 1) * HD], blk(w, n), start=n == 0, stop=n == NB - 1)
        return pe_done.on(last)

    def stick():
        sp_, zz, ww = ew
        after(tensor, done["qk", 0], done["v", 0])
        m_zb = m_pv = m_out = None
        for h in range(NH):
            t, p0 = h // 2, HD * (h % 2)
            q = qk0[p0:p0 + HD, t * T:(t + 1) * T]
            kk = qk0[p0:p0 + HD, (2 + t) * T:(3 + t) * T]
            after(tensor, m_zb)
            for n in range(NB):
                last = tensor.matmul(pblk(0, n), kk[:, n * P:(n + 1) * P], q[:, n * P:T], start=True, stop=True)
            m = pe_done.on(last)
            m_abs = aop(ww[:, :], wide(0), ACT.Abs, scale=scale, needs=(m, m_pv, m_out))
            m_1 = aop(zz[:, :], ww[:, :], ACT.Exp, scale=-1.0, needs=(m_abs, m_zb))
            m_1 = aop(ww[:, :], zz[:, :], ACT.Ln, bias=1.0, needs=(m_1,))
            m = ts(sp_[:, :], wide(0), scale, 0.0, ALU.mult, ALU.max, needs=(m_abs,))
            m = tt(sp_[:, :], sp_[:, :], ww[:, :], ALU.add, needs=(m, m_1))
            m_z = stt(zz[:, :], wide(0), scale, sp_[:, :], ALU.mult, ALU.subtract, needs=(m,))
            for n in range(NB):
                m = tt(blk(sp_, n, P), blk(sp_, n, P), past, ALU.mult, needs=(m_z,))
            yield
            after(tensor, m)
            for n in range(NB):
                for k in range(n, NB):
                    last = tensor.matmul(pblk(0, n, T - P * k, P * (k - n)), after_m if k == n else ones, blk(sp_, k),
                                         start=k == n, stop=k == NB - 1)
            m = pe_done.on(last)
            m_zb = m = tt(zz[:, :], zz[:, :], wide(0), ALU.subtract, needs=(m,))
            m_w = aop(ww[:, :], zz[:, :], ACT.Exp, needs=(m,))
            for n in range(NB):
                m = tt(blk(ww, n, P), blk(ww, n, P), past, ALU.mult, needs=(m_w,))
            yield
            after(tensor, m, m_out)
            m_pv = weighted_values(h, vv0, ww)
            if h % 2:
                m = aop(sp_[:, 0:T], bank(OUT), ACT.Copy, needs=(m_pv,))
                m_out = done["yb"] = split_y(2 + t, sp_[:, 0:T], (m,))
            yield

    def moba():
        pm, pT, o = ew
        after(tensor, done["qk", 1], done["v", 1], done["yb"])
        after(scalar, done["yb"])
        m_pt = m_pv = m_out = m_cp = None
        for h in range(NH):
            t, p0 = h // 2, HD * (h % 2)
            q = qk1[p0:p0 + HD, t * T:(t + 1) * T]
            kk = qk1[p0:p0 + HD, (2 + t) * T:(3 + t) * T]
            after(tensor, m_cp)
            for b in range(NB):
                last = tensor.matmul(pblk(0, NB - 1 - b, (b + 1) * P), q[:, b * P:(b + 1) * P], kk[:, 0:(b + 1) * P], start=True, stop=True)
            m = pe_done.on(last)
            for b in range(NB):
                dg = pblk(0, NB - 1 - b, P, b * P)
                m_1 = tt(dg, dg, neg, ALU.add, needs=(m,))
                m_1 = vop(vector.reduce_max, mx[:, b:b + 1], pblk(0, NB - 1 - b, (b + 1) * P), AX.X, needs=(m_1,))
            m_1 = ts(mx[:, :], mx[:, :], -scale, None, ALU.mult, needs=(m_1,))
            for b in range(NB):
                m_p = aop(blk(pm, NB - 1 - b, (b + 1) * P), pblk(0, NB - 1 - b, (b + 1) * P), ACT.Exp, bias=mx[:, b:b + 1],
                          scale=scale, accum_out=nl[:, b:b + 1], needs=(m_1, m_pt))
            m = vop(vector.reciprocal, nl[:, :], nl[:, :], needs=(m_p,))
            for b in range(NB):
                m_n = ts(blk(pm, NB - 1 - b, (b + 1) * P), blk(pm, NB - 1 - b, (b + 1) * P), nl[:, b:b + 1], None, ALU.mult, needs=(m,))
            yield
            after(tensor, m_n)
            for b in range(NB):
                for k in range(b + 1):
                    src = pm[:, OFF[NB - 1 - b] + k * P:OFF[NB - 1 - b] + (k + 1) * P]
                    last = tensor.transpose(pblk(0, k, P, (b - k) * P), src, ident)
            m_pt = pe_done.on(last)
            m_cp = m = aop(pT[:, :], wide(0), ACT.Copy, needs=(m_pt, m_pv))
            yield
            after(tensor, m, m_out)
            m_pv = weighted_values(h, vv1, pT)
            if h % 2:
                m = aop(o[:, t * T:(t + 1) * T], bank(OUT), ACT.Copy, needs=(m_pv,))
                m_out = done["yd"] = split_y(6 + t, o[:, t * T:(t + 1) * T], (m,))
            yield

    def mamba():
        gm, dk = ew[0], (ew[1], ew[2])
        after(tensor, done["a"], done["bc"], done["yd"])
        after(vector, done["yd"])
        for n in range(NB):
            for k in range(n + 1):
                last = tensor.matmul(bank(OUT, NH, n * NH), tri if k == n else ones, av[:, k * NH:(k + 1) * NH], start=k == 0, stop=k == n)
        m = pe_done.on(last)
        m_acs = vop(vector.tensor_copy, acs[:, :], bank(OUT, 16), needs=(m, done["a"]))
        for t in range(2):
            for n in range(NB):
                last = tensor.transpose(banks[:, n * 256 + t * P:n * 256 + (t + 1) * P],
                                        bc[:, t * T + n * P:t * T + (n + 1) * P], ident)
        m = pe_done.on(last)
        m_free = m_xd = tt(xd[:, :].rearrange("p (n d) -> p n d", d=HD), banks[:, 0:2 * 512].rearrange("p (n d) -> p n d", d=HD),
                           dtv[:, :].rearrange("p (n a) -> p n a", a=1).to_broadcast([P, 16, HD]), ALU.mult, needs=(m,))
        yield
        m_row, m_y, m_used = None, [None, None], None
        for g in range(2):
            bm = bc[g * HD:(g + 1) * HD, 2 * T:3 * T]
            cm = bc[g * HD:(g + 1) * HD, 3 * T:4 * T]
            after(tensor, m_free)
            for n in range(NB):
                last = tensor.matmul(pblk(0, n), bm[:, n * P:(n + 1) * P], cm[:, n * P:T], start=True, stop=True)
            m = pe_done.on(last)
            m_cp = aop(gm[:, :], wide(0), ACT.Copy, needs=(m, m_used))
            for n in range(NB):
                m_gm = tt(blk(gm, n, P), blk(gm, n, P), tri, ALU.mult, needs=(m_cp,))
            yield
            for e in range(2):
                h, p0, d_ = 2 * g + e, HD * e, dk[e]
                m = vop(vector.tensor_copy, abc[:, :].rearrange("p (n c) -> p n c", c=P),
                        av[:, :].rearrange("p (n h) -> p n h", h=NH)[:, :, h:h + 1].to_broadcast([P, NB, P]), needs=(m_row,))
                after(tensor, m, m_gm)
                for n in range(NB):
                    last = tensor.matmul(bank(e, T - P * n, P * n), abc[:, n * P:(n + 1) * P], tri_ones[:, 0:T - P * n],
                                         start=n == 0, stop=n == NB - 1)
                m_row = pe_done.on(last)
                for n in range(NB):
                    m = ts(blk(d_, n), bank(e, T - P * n, P * n), acs[:, n * NH + h:n * NH + h + 1], 0.0, ALU.subtract, ALU.min,
                           needs=(m_row, m_y[e], m_acs))
                m_free = m
                m = aop(d_[:, :], d_[:, :], ACT.Exp, needs=(m,))
                m_used = m = tt(d_[:, :], d_[:, :], gm[:, :], ALU.mult, needs=(m,))
                yield
                after(tensor, m, done.get("yc"))
                m_y[e] = weighted_values(h, xd, d_)
                yield
            m = m_y[1]
            m = stt(yt[g][:, :], tile(bc, g), col("ssm_d", g), bank(OUT), ALU.mult, ALU.add, needs=(m,))
            m = tt(yt[g][:, :], yt[g][:, :], tile(zs, g), ALU.mult, needs=(m,))
            m_s = aop(dk[0][:, 0:T], yt[g][:, :], ACT.Square, needs=(m,))
            m = feature_sum(2, dk[0][:, 0:T], T, (m_s, m_free))
            m_y[0] = m_y[1] = m = rms_rstd(dk[1][:, 0:T], bank(2), eps_rms, P, (m,))
            m_free = m = stt(yt[g][:, :], yt[g][:, :], col("ssm_norm_g", g), dk[1][:, 0:T], ALU.mult, ALU.mult, needs=(m,))
            m_y[0] = m_y[1] = m
            done["yc"] = split_y(4 + g, yt[g][:, :], (m,))
            yield

    def strand(*parts_):
        for g in parts_:
            yield from g

    def run(work, n=None):
        for _ in range(n if n is not None else 1 << 30):
            try:
                next(work)
            except StopIteration:
                return False
        return True

    vector.wait_ge(s_cst2, 16)
    tensor.wait_ge(s_cst2, 16)
    done["gs"] = None
    products = strand(inputs_a(), inputs_qkv(0, qk0, vv0))
    run(products)
    products = strand(inputs_qkv(1, qk1, vv1), inputs_c())
    mixer = stick()
    while run(mixer, 1):
        run(products, 1)
    run(products)
    after(vector, done["yb"], done["bc"])
    done["gs"] = done["yb"]
    done[0], done[1] = done["ya"], done["yb"]
    products = strand(merge(0, 0, True, False), merge(1, 1, False, False))
    mixer = moba()
    while run(mixer, 1):
        run(products, 1)
    mixer = mamba()
    while run(mixer, 1):
        run(products, 1)
    run(products)
    done[3], done[2] = done["yd"], done["yc"]
    run(merge(3, 3, False, False))
    after(scalar, done["yc"])
    run(merge(2, 2, False, True))

    m_mk = [done["m", f] for f in range(NT)]
    m_v = m_mk[-1]
    m = vop(vector.memset, s1[:, :], 0.0, needs=(m_v,))
    with loop("w_o", 2, chunks=4, banks_free=(bank_free[4], bank_free[5], bank_free[6], bank_free[7])) as lp:
        turns = Turns(lp, 4)
        for j in range(4):
            tn = turns.at(j)
            f = lp.i * 4 + j
            m = chunk(full(bank(j), m_hi, m_lo_), needs=(lp.back(f"res{j}"),), by_part=m_mk if j == 0 else None)
            m = tn.note("res", tt(tile(X, f), bank(j), tile(X, f), ALU.add, needs=(m,)))
            m_x = tn.note("s1", add_square(s1[:, :], tile(X, f), sqa[:, :], (m, tn.back("s1"))))

    p = Plan(area)
    f_hi, f_lo = p("f_hi", FFN_TILES * T, F32R), p("f_lo", FFN_TILES * T, F32R)
    fs = [p(f"fs{k}", T) for k in range(2)]
    rstd = at("rstd_b", T, area + 4 * T * 30)[:, :]
    nt_ = [at(f"nb{k}", T, area + 4 * T * (32 + k)) for k in range(3)]
    m_mm = Mark(chunk_mm, chunk_mm.n, None)
    after(scalar, m_x, m_mm)
    after(vector, m_mm)
    m = feature_sum(7, s1[:, :], T, (m_x,))
    m = rms_rstd(rstd, bank(7), eps_rms, D, (m,))
    m_hk = norm_split(X, T, rstd, lambda k: col("norm2_g", k), None, h_hi, h_lo, nt_, (m,))
    with loop("ffn_in", FFN_TILES // 2, chunks=4, banks_free=(m_x,)) as lp:
        for j in range(2):
            m_g = chunk(full(bank(2 * j), h_hi, h_lo), needs=(lp.back(f"up{j}"),), by_part=m_hk if j == 0 else None)
            m_u = chunk(full(bank(2 * j + 1), h_hi, h_lo))
            f = lp.i * 2 + j
            m = aop(fs[j][:, :], bank(2 * j), ACT.Silu, needs=(m_g, lp.back(f"flo{j}")))
            m = lp.note(f"up{j}", tt(fs[j][:, :], bank(2 * j + 1), fs[j][:, :], ALU.mult, needs=(m, m_u)))
            m = aop(tile(f_hi, f), fs[j][:, :], ACT.Copy, needs=(m,))
            m_f = lp.note(f"flo{j}", tt(tile(f_lo, f), fs[j][:, :], tile(f_hi, f).bitcast(F32), ALU.subtract, needs=(m,)))
    after(tensor, m_f)
    after(scalar, m_f)
    m_res, m_s = [None] * 4, None
    for f in range(NT):
        for k0, n in ((0, 8), (8, 8), (16, FFN_TILES - 16)):
            m = chunk([(bank(f % 4), [(k, tile(f_hi, k0 + k), tile(f_lo, k0 + k)) for k in range(n)], k0 == 0, k0 == 16)],
                      needs=(m_res[f % 4],) if k0 == 0 else ())
        m_res[f % 4] = tt(tile(X, f), bank(f % 4), tile(X, f), ALU.add, needs=(m,))
        m_s = add_square(s1[:, :], tile(X, f), sqa[:, :], (m_res[f % 4], m_s), first=f == 0)

    m = feature_sum(7, s1[:, :], T, (m_s,))
    rstd = fs[0][:, :]
    m = rms_rstd(rstd, bank(7), eps_rms, D, (m,))
    for k in range(NT):
        m_x = stt(tile(X, k), tile(X, k), col("final_g2", k), rstd, ALU.mult, ALU.mult, needs=(m,))
        if k % 2:
            nc.sync.wait_ge(v_done.sem, m_x.value())
            nc.sync.dma_start(out[:, (k - 1) * T:(k + 1) * T], X[:, (k - 1) * T:(k + 1) * T]).then_inc(s_out, 16)
    nc.sync.wait_ge(s_out, 16 * NT // 2)
    assert state["chunk"] == N_CHUNKS, state["chunk"]
    ctx.close()


def constants():
    c = np.zeros((P, NCONST), np.float32)
    r, q = np.arange(P)[:, None], np.arange(P)[None, :]
    c[:, CC["ident"]:CC["ident"] + P] = r == q
    c[:, CC["ones"]:CC["ones"] + P] = 1
    t = np.arange(ROW)
    for g in range(POOL_LEVELS):
        w = 2 << g
        cnt = np.clip(t + w // 2, 0, ROW) - np.clip(t - w // 2, 0, ROW)
        c[:, CC["inv_cnt"] + g * ROW:CC["inv_cnt"] + (g + 1) * ROW] = np.float32(1) / cnt.astype(np.float32)
    c[:, CC["tri_ones"]:CC["tri_ones"] + P] = r <= q
    c[:, CC["tri_ones"] + P:CC["tri_ones"] + 512] = 1
    c[:, CC["after"]:CC["after"] + P] = r > q
    c[:, CC["past"]:CC["past"] + P] = r < q
    c[:, CC["neg"]:CC["neg"] + P] = np.where(q <= r, 0, -1e30)
    return c


def tiles_of(w):
    k, n = w.shape
    return w.reshape(k // P, P, n // P, P).transpose(2, 1, 0, 3).reshape(n // P, P, k)


def lay_out(a):
    ev, od = a["ev_w_in"][0], a["od_w_in"][0]
    evt = tiles_of(ev)
    zero = np.zeros((P, CW - 4 * P), np.float32)
    gates = [np.concatenate([a["ev_w_r"][0, 0, h], a["ev_w_i"][0, 0, h], a["ev_w_r"][0, 1, h], a["ev_w_i"][0, 1, h], zero], 1)
             for h in range(8)]
    s = []
    for i in range(NT):
        s += [evt[24 + i], evt[8 + i], evt[i], gates[i]]
    cw = a["ev_conv_w"][0]
    diag = np.zeros((NT, 2, P, KC, P), np.float32)
    for j in range(2):
        for b in range(KC):
            diag[:, j, range(P), b, range(P)] = cw[KC * j + b].reshape(NT, P)
    diag = diag.reshape(NT, 2, P, CW)
    for i in range(NT):
        s += [evt[24 + i], evt[32 + i], gates[i], evt[16 + i], diag[i, 0], diag[i, 1]]
    wo = tiles_of(a["ev_w_out"][0])
    for half in range(2):
        s += [wo[4 * half + j][:, CW:] for j in range(4)] + [wo[4 * half + j][:, :CW] for j in range(4)]
    odt = tiles_of(od)
    for g in range(POOL_LEVELS):
        wg = tiles_of(a["od_w_grp"][0, g])
        s += list(odt[4 * g:4 * g + 4])
        for half in range(2):
            s += list(odt[16 + 4 * g + 2 * half:18 + 4 * g + 2 * half])
            s += [np.concatenate([wg[2 * half], wg[2 * half + 1]], 1)]
    wo = tiles_of(a["od_w_out"][0])
    for f in range(NT):
        s += [wo[f][:, :CW], wo[f][:, CW:]]
    w = a["w_in_2"][0]
    A = tiles_of(w[:, 0:768])
    for t in range(2):
        s += [A[t], A[4 + t], A[2 + t]]
    c0 = 768 + 768
    d0 = c0 + 772
    for base in (768, d0):
        s += list(tiles_of(w[:, base:base + 512]))
        v = w[:, base + 512:base + 768].reshape(2, 4, P, 256).transpose(0, 2, 1, 3).reshape(2, P, CW)
        s += [v[0], v[1]]
    s += list(tiles_of(w[:, c0:c0 + 768]))
    wdt = w[:, c0 + 768:c0 + 772]
    G = tiles_of(w[:, d0 + 768:])
    for b in (0, 1, 3, 2):
        br = tiles_of(a["w_branch_2"][0, b])
        for half in range(2):
            s += [G[b * NT + 4 * half + j] for j in range(4)]
            s.append(np.concatenate([br[4 * half + j] for j in range(4)], 1))
    s += list(tiles_of(a["w_o_2"][0]))
    gu = tiles_of(a["w_gate_up_2"][0])
    for f in range(FFN_TILES):
        s += [gu[f], gu[FFN_TILES + f]]
    wd = tiles_of(a["w_down_2"][0])
    for f in range(NT):
        last = np.concatenate([wd[f][:, 2 * CW:], np.zeros((P, 3 * CW - FFN_TILES * P), np.float32)], 1)
        s += [wd[f][:, :CW], wd[f][:, CW:2 * CW], last]
    weights = np.stack(s)
    assert weights.shape == (N_CHUNKS, P, CW), weights.shape
    modw = np.concatenate([tiles_of(a["mod_w"][0]), tiles_of(a["mod_w"][1])])

    f = lambda v: np.asarray(v).reshape(-1, P).T
    k_ = lambda v: v.reshape(v.shape[0], -1, P).transpose(2, 1, 0).reshape(P, -1)
    rep = lambda v: np.broadcast_to(np.tile(v, NB)[None, :], (P, NB * NH))
    vals = {
        "c": f(a["c"]), "c_ctx": f(a["c_ctx"]), "norm_g": f(a["norm_g"]), "mod_b": f(a["mod_b"]),
        "conv_w": k_(a["ev_conv_w"][0]), "conv_b": f(a["ev_conv_b"]), "ln_g": f(a["ev_ln_g"]), "ln_b": f(a["ev_ln_b"]),
        "sconv_w": k_(a["ev_sconv_w"][0]), "sconv_b": f(a["ev_sconv_b"]),
        "b_r": k_(a["ev_b_r"][0]), "b_i": k_(a["ev_b_i"][0]), "lam": k_(a["ev_lam"][0]),
        "od_scale": f(a["od_scale"]), "final_g": f(a["final_g"]), "norm1_g": f(a["norm1_g_2"]),
        "conv_a_w": k_(a["conv_a_w_2"][0]), "ssm_conv_w": k_(a["ssm_conv_w_2"][0]), "ssm_conv_b": f(a["ssm_conv_b_2"]),
        "dt_bias": rep(a["ssm_dt_bias_2"][0]), "a_log": rep(a["ssm_a_log_2"][0]),
        "ssm_d": f(np.repeat(a["ssm_d_2"][0], HD)), "ssm_norm_g": f(a["ssm_norm_g_2"]),
        "norm2_g": f(a["norm2_g_2"]), "final_g2": f(a["final_g_2"]),
        "w_dt": wdt.reshape(NT, P, NH).transpose(1, 0, 2).reshape(P, NT * NH),
    }
    order = sorted(VC, key=VC.get)
    vecs = np.ascontiguousarray(np.concatenate([vals[n] for n in order], 1))
    assert vecs.shape == (P, NVEC), vecs.shape
    xt = lambda x, t: np.ascontiguousarray(x[0].reshape(t, NT, P).transpose(2, 1, 0).reshape(P, NT * t))
    return {"weights": weights, "modw": np.ascontiguousarray(modw), "vecs": vecs, "consts": constants(),
            "x_in": xt(a["x"], T), "ctx_in": xt(a["ctx"], TC)}


def kernel(**inputs):
    import concourse.bacc as bacc
    from concourse.bass_utils import run_bass_kernel_spmd

    arrays = lay_out({k: np.asarray(v) for k, v in inputs.items()})
    nc = bacc.Bacc("TRN2", target_bir_lowering=False, num_devices=1)
    args = [nc.dram_tensor(n, v.shape, F32, kind="ExternalInput").ap() for n, v in arrays.items()]
    out = nc.dram_tensor("out", (P, NT * T), F32, kind="ExternalOutput").ap()
    program(nc, *args, out)
    r = run_bass_kernel_spmd(nc, [arrays], core_ids=[0])
    y = r.results[0]["out"]
    return y.reshape(P, NT, T).transpose(2, 1, 0).reshape(1, T, D)
```

```python
import numpy as np
import concourse.bass as bass
from concourse import mybir
from contextlib import ExitStack, contextmanager, nullcontext

P = 128
D = 1024
T = 512
TC = 256
NT = D // P
NB = T // P
MOD_RING = 2
RING = 4
AHEAD = 3
KC = 8
CW = KC * P
CONV_K, SCONV_K, SSM_K, SHORT_K = 31, 4, 4, 3
HALO = CONV_K // 2
EPS = 1e-6
PE_TAPS = 16
FFN_TILES = 22
HD = 64
NH = 4
ROW = 64
POOL_LEVELS = 4
F32, F32R = mybir.dt.float32, mybir.dt.float32r
ALU, ACT, AX = mybir.AluOpType, mybir.ActivationFunctionType, mybir.AxisListType

CAUSAL = NB * (NB + 1) // 2 * P
OFF = {0: 0, 1: 512, 3: 896, 2: 1024}


def vector_columns():
    at, cols = 0, {}
    for name, n in (
        ("c", NT), ("c_ctx", NT), ("norm_g", 2 * NT), ("mod_b", 2 * 3 * NT),
        ("conv_w", NT * CONV_K), ("conv_b", NT), ("ln_g", NT), ("ln_b", NT),
        ("sconv_w", NT * SCONV_K), ("sconv_b", NT), ("b_r", 2 * NT), ("b_i", 2 * NT), ("lam", 2 * NT),
        ("od_scale", 2 * NT), ("final_g", NT), ("norm1_g", NT), ("conv_a_w", 2 * SHORT_K),
        ("ssm_conv_w", 4 * SSM_K), ("ssm_conv_b", 4), ("dt_bias", NB * NH), ("a_log", NB * NH),
        ("ssm_d", 2), ("ssm_norm_g", 2), ("norm2_g", NT), ("final_g2", NT), ("w_dt", NT * NH),
    ):
        cols[name] = at
        at += n
    return cols, at


VC, NVEC = vector_columns()
LOOPS = {
    'va': {
        "per": {'v': 16, 'a': 15, 'mod': 1},
        "back": {'xp': ('a', 1), 'conv': ('v', 4), 'sig': ('a', 3), 'uu': ('v', 6), 'gates': ('mm', 4), 'gate_read': ('a', 10), 'th_read': ('v', 11), 'scans': ('v', 14)},
    },
    'heads': {
        "per": {'v': 72, 'a': 36, 'mod': 4},
        "back": {'xp0': ('a', 2), 'conv0': ('v', 8), 'sgb0': ('v', 12), 'gates0': ('mm', 4), 'sga0': ('v', 14), 'gate_read0': ('a', 12), 'conv_pe0': ('mm', 6), 'th_read0': ('v', 24), 'scans0': ('v', 30), 'taps0': ('v', 31), 'conv_sum0': ('v', 33), 'yb_lo0': ('v', 36), 'xp1': ('a', 20), 'conv1': ('v', 44), 'sgb1': ('v', 48), 'gates1': ('mm', 10), 'sga1': ('v', 50), 'gate_read1': ('a', 30), 'conv_pe1': ('mm', 12), 'th_read1': ('v', 60), 'scans1': ('v', 66), 'taps1': ('v', 67), 'conv_sum1': ('v', 69), 'yb_lo1': ('v', 72)},
    },
    'ev_out': {
        "per": {'v': 2},
        "back": {'res0': ('v', 1), 'res1': ('v', 2)},
    },
    'pool': {
        "per": {'v': 28, 'a': 8},
        "back": {'l0': ('a', 1), 'sub0': ('v', 6), 'l1': ('a', 3), 'sub1': ('v', 13), 'l2': ('a', 5), 'sub2': ('v', 20), 'l3': ('a', 7), 'sub3': ('v', 27)},
    },
    'group': {
        "per": {'v': 16, 'a': 16},
        "back": {'y0_0': ('v', 1), 'lo0_0': ('v', 2), 'y1_0': ('v', 3), 'lo1_0': ('v', 4), 'y2_0': ('v', 5), 'lo2_0': ('v', 6), 'y3_0': ('v', 7), 'lo3_0': ('v', 8), 'y0_1': ('v', 9), 'lo0_1': ('v', 10), 'y1_1': ('v', 11), 'lo1_1': ('v', 12), 'y2_1': ('v', 13), 'lo2_1': ('v', 14), 'y3_1': ('v', 15), 'lo3_1': ('v', 16)},
    },
    'od_out': {
        "per": {'v': 6, 'a': 4},
        "back": {'res0': ('v', 1), 's10': ('v', 2), 's20': ('v', 3), 'res1': ('v', 4), 's11': ('v', 5), 's21': ('v', 6)},
    },
    'merge': {
        "per": {'v': 32, 'a': 20},
        "back": {'sg0_0': ('a', 1), 'pr0_0': ('v', 1), 'sg0_1': ('a', 2), 'pr0_1': ('v', 3), 'sg0_2': ('a', 3), 'pr0_2': ('v', 5), 'sg0_3': ('a', 4), 'pr0_3': ('v', 7), 'lo0': ('v', 8), 'sg1_0': ('a', 6), 'pr1_0': ('v', 9), 'sg1_1': ('a', 7), 'pr1_1': ('v', 11), 'sg1_2': ('a', 8), 'pr1_2': ('v', 13), 'sg1_3': ('a', 9), 'pr1_3': ('v', 15), 'lo1': ('v', 16), 'sg2_0': ('a', 11), 'pr2_0': ('v', 17), 'sg2_1': ('a', 12), 'pr2_1': ('v', 19), 'sg2_2': ('a', 13), 'pr2_2': ('v', 21), 'sg2_3': ('a', 14), 'pr2_3': ('v', 23), 'lo2': ('v', 24), 'sg3_0': ('a', 16), 'pr3_0': ('v', 25), 'sg3_1': ('a', 17), 'pr3_1': ('v', 27), 'sg3_2': ('a', 18), 'pr3_2': ('v', 29), 'sg3_3': ('a', 19), 'pr3_3': ('v', 31), 'lo3': ('v', 32)},
    },
    'w_o': {
        "per": {'v': 16, 'a': 8},
        "back": {'res0': ('v', 1), 's10': ('v', 3), 'lo0': ('v', 4), 'res1': ('v', 5), 's11': ('v', 7), 'lo1': ('v', 8), 'res2': ('v', 9), 's12': ('v', 11), 'lo2': ('v', 12), 'res3': ('v', 13), 's13': ('v', 15), 'lo3': ('v', 16)},
    },
    'ffn_in': {
        "per": {'v': 8, 'a': 4},
        "back": {'up0': ('v', 2), 'flo0': ('v', 4), 'up1': ('v', 6), 'flo1': ('v', 8)},
    },
    'ffn_out': {
        "per": {'v': 4},
        "back": {'res0': ('v', 1), 'res1': ('v', 2), 'res2': ('v', 3), 'res3': ('v', 4)},
    },
    'odd': {
        "per": {'v': 68, 'a': 32},
        "back": {'l00': ('a', 1), 'l10': ('a', 3), 'dlo00': ('v', 9), 'sil00': ('a', 5), 'l20': ('a', 6), 'dlo10': ('v', 15), 'sil10': ('a', 8), 'l30': ('a', 9), 'dlo20': ('v', 21), 'sil20': ('a', 11), 'dlo30': ('v', 24), 'sil30': ('a', 12), 'y00': ('v', 25), 'ylo00': ('v', 26), 'y10': ('v', 27), 'ylo10': ('v', 28), 'y20': ('v', 29), 'ylo20': ('v', 30), 'y30': ('v', 31), 'ylo30': ('v', 32), 'grp0': ('mm', 10), 'l01': ('a', 17), 'l11': ('a', 19), 'dlo01': ('v', 43), 'sil01': ('a', 21), 'l21': ('a', 22), 'dlo11': ('v', 50), 'sil11': ('a', 24), 'l31': ('a', 25), 'dlo21': ('v', 57), 'sil21': ('a', 27), 'dlo31': ('v', 60), 'sil31': ('a', 28), 'y01': ('v', 61), 'ylo01': ('v', 62), 'y11': ('v', 63), 'ylo11': ('v', 64), 'y21': ('v', 65), 'ylo21': ('v', 66), 'y31': ('v', 67), 'ylo31': ('v', 68), 'grp1': ('mm', 20)},
    },
}
CC = {"ident": 0, "ones": 128, "inv_cnt": 256, "tri_ones": 512, "after": 1024, "past": 1152, "neg": 1280}
NCONST = 1408
N_CHUNKS = 32 + 48 + 16 + 40 + 16 + 24 + 40 + 8 + 44 + 24


class Counter:

    def __init__(self, sem):
        self.sem, self.n, self.loop = sem, 0, None

    def lead(self, engine, n):
        engine.sem_inc(self.sem, n)
        self.n += n

    def on(self, instruction):
        instruction.then_inc(self.sem, 1)
        self.n += 1
        return Mark(self, self.n, self.loop)


class Mark:
    def __init__(self, counter, n, loop):
        self.counter, self.n, self.loop = counter, n, loop

    def prev(self):
        return Mark(self.counter, self.n - self.loop.per[self.counter], self.loop)

    def value(self):
        if self.loop is None:
            return self.n
        per = self.loop.per[self.counter]
        if self.loop.done:
            return self.n + per * (self.loop.count - 1)
        return self.n + self.loop.i * per


class Turns:

    def __init__(self, loop, n):
        self.loop, self.n, self.e, self.last = loop, n, 0, {}

    def at(self, e):
        self.e = e
        return self

    def back(self, name):
        return self.loop.back(f"{name}{self.n - 1}") if self.e == 0 else self.last[name, self.e - 1]

    def note(self, name, mark):
        self.last[name, self.e] = mark
        return self.loop.note(f"{name}{self.e}", mark)


class Loop:

    def __init__(self, i, count, per, back, counters, starts):
        self.i, self.count, self.per, self.done = i, count, per, False
        self.back_at, self.counters, self.starts, self.noted = back, counters, starts, {}

    def back(self, name):
        if name not in self.back_at:
            return None
        which, k = self.back_at[name]
        c = self.counters[which]
        return Mark(c, self.starts[c] + k - self.per[c], self)

    def note(self, name, mark):
        which = next(k for k, c in self.counters.items() if c is mark.counter)
        self.noted[name] = (which, mark.n - self.starts[mark.counter])
        return mark


def program(nc, wts, modw, vecs, consts, x_in, ctx_in, out):
    ctx = ExitStack()
    base0 = (nc.sbuf_base + 31) // 32 * 32
    K = 1024

    def at(name, cols, off, dt=F32):
        return nc.alloc_sbuf_tensor_at(name, [P, cols], dt, offset=base0 + off)

    raw = at("raw", RING * CW, 0)
    w_hi = at("w_hi", RING * CW, 16 * K, F32R)
    w_lo = at("w_lo", RING * CW, 32 * K, F32R)
    X = at("X", NT * T, 48 * K)
    h_hi = at("h_hi", NT * T, 64 * K, F32R)
    h_lo = at("h_lo", NT * T, 80 * K, F32R)
    vec = at("vec", NVEC, 96 * K)
    o_small = 96 * K + (4 * NVEC + 31) // 32 * 32
    small = at("small", 392, o_small)
    o_cst = o_small + 4 * 392
    cst = at("cst", 512, o_cst)
    cst2 = at("cst2", NCONST - 512, o_cst + 2048)
    area = (o_cst + 2048 + 31) // 32 * 32
    area2 = area + 4 * (NCONST - 512)
    limit = nc.sbuf_usable_end - base0

    class Plan:

        def __init__(self, start):
            self.at = start

        def __call__(self, name, cols, dt=F32):
            t = at(name, cols, self.at, dt)
            self.at += (4 * cols + 31) // 32 * 32
            assert self.at <= limit, (name, self.at, limit)
            return t

    banks = ctx.enter_context(nc.psum_tensor("banks", [P, 8 * 512], F32))

    def bank(b, w=512, o=0):
        return banks[:, b * 512 + o:b * 512 + o + w]

    def sem(name):
        return ctx.enter_context(nc.semaphore(name))

    s_raw = [sem(f"s_raw{s}") for s in range(RING)]
    s_vec, s_x, s_ctx, s_cst = sem("s_vec"), sem("s_x"), sem("s_ctx"), sem("s_cst")
    s_cst2 = sem("s_cst2")
    s_mod0 = [sem(f"s_mod0_{j}") for j in range(4)]
    s_mraw = [sem(f"s_mraw{s}") for s in range(MOD_RING)]
    s_out = sem("s_out")
    chunk_hi = Counter(sem("s_hi"))
    chunk_lo = Counter(sem("s_lo"))
    chunk_mm = Counter(sem("s_mm"))
    mod_mm = Counter(sem("s_mod_mm"))
    pe_done = Counter(sem("s_pe"))
    v_done = Counter(sem("s_v"))
    a_done = Counter(sem("s_a"))
    v_side, a_side = Counter(sem("s_v_side")), Counter(sem("s_a_side"))
    counters = (chunk_hi, chunk_lo, chunk_mm, mod_mm, pe_done, v_done, a_done)

    chunk_mm.lead(nc.tensor, RING)
    mod_mm.lead(nc.tensor, 3)

    state = {"loop": None, "chunk": 0, "split": 0, "v": v_done, "a": a_done}

    def after(engine, *marks):
        for m in marks:
            if m is not None:
                engine.wait_ge(m.counter.sem, m.value())

    def V(ins):
        return state["v"].on(ins)

    def A(ins):
        return state["a"].on(ins)

    @contextmanager
    def beside():
        state["v"], state["a"] = v_side, a_side
        yield
        state["v"], state["a"] = v_done, a_done

    vector, scalar, tensor = nc.vector, nc.scalar, nc.tensor

    def vop(fn, *args, needs=(), **kw):
        after(vector, *needs)
        return V(fn(*args, **kw))

    def aop(out_ap, in_ap, func, needs=(), **kw):
        after(scalar, *needs)
        return A(scalar.activation(out_ap, in_ap, func, **kw))

    def tt(o, a, b, op, needs=()):
        return vop(vector.tensor_tensor, o, a, b, op, needs=needs)

    def ts(o, a, s1, s2, op0, op1=None, needs=()):
        if op1 is None:
            return vop(vector.tensor_scalar, o, a, s1, None, op0, needs=needs)
        return vop(vector.tensor_scalar, o, a, s1, s2, op0, op1, needs=needs)

    def stt(o, a, s, b, op0, op1, needs=()):
        return vop(vector.scalar_tensor_tensor, o, a, s, b, op0, op1, needs=needs)

    named = {"pe": pe_done, "v": v_done, "a": a_done, "mod": mod_mm, "mm": chunk_mm}

    @contextmanager
    def loop(name, count, chunks=0, banks_free=None):
        table = LOOPS.get(name, {"per": {}, "back": {}})
        rise = {c: 0 for c in counters}
        for c in (chunk_hi, chunk_lo, chunk_mm):
            rise[c] = chunks
        for k, n in table["per"].items():
            rise[named[k]] = n
        starts = {c: c.n for c in counters}
        c0, s0 = state["chunk"], state["split"]
        assert chunks % RING == 0
        v_all = [Mark(c, c.n, None) for c in (v_done, v_side) if c.n]
        a_all = [Mark(c, c.n, None) for c in (a_done, a_side) if c.n]
        after(tensor, *((*v_all, *a_all) if banks_free is None else banks_free))
        after(scalar, *v_all)
        after(vector, *a_all)
        with nc.Fori(0, count) as i:
            lp = Loop(i, count, rise, table["back"], named, starts)
            state["loop"] = lp
            for c in counters:
                c.loop = lp
            yield lp
        found = {k: c.n - starts[c] for k, c in named.items() if k != "mm" and c.n > starts[c]}
        found = {"per": found, "back": lp.noted}
        assert found == table, f"LOOPS[{name!r}] = {found}"
        assert state["chunk"] - c0 == chunks and state["split"] - s0 == chunks
        lp.done = True
        state["loop"] = None
        for c in counters:
            c.loop = None
            c.n = starts[c] + count * rise[c]
        state["chunk"] = c0 + count * chunks
        state["split"] = s0 + count * chunks

    def moving(n):
        lp = state["loop"]
        if lp is None or not lp.per[chunk_mm]:
            return n
        return n + lp.i * lp.per[chunk_mm]

    def split_next():
        c = state["split"]
        last = c >= N_CHUNKS
        state["split"] += 1
        if last:
            return
        s = c % RING
        lp = state["loop"]
        turn = 16 * (c // RING + 1)
        if lp is not None:
            turn = turn + lp.i * (16 * lp.per[chunk_mm] // RING)
        scalar.wait_ge(s_raw[s], turn)
        if c >= RING:
            scalar.wait_ge(chunk_mm.sem, moving(c + 1))
        chunk_hi.on(scalar.activation(w_hi[:, s * CW:(s + 1) * CW], raw[:, s * CW:(s + 1) * CW], ACT.Copy))
        vector.wait_ge(chunk_hi.sem, moving(c + 1))
        chunk_lo.on(vector.tensor_tensor(w_lo[:, s * CW:(s + 1) * CW], raw[:, s * CW:(s + 1) * CW],
                                         w_hi[:, s * CW:(s + 1) * CW].bitcast(F32), ALU.subtract))

    def chunk(groups, needs=(), swap=False, by_part=None, each=False):
        split_next()
        c = state["chunk"]
        state["chunk"] += 1
        s = c % RING
        tensor.wait_ge(chunk_lo.sem, moving(c + 1))
        after(tensor, *needs)
        last, marks = None, []
        for o, parts, start, stop in groups:
            for n, (b, r_hi, r_lo) in enumerate(parts):
                if by_part is not None and last is None or by_part is not None and o is groups[0][0]:
                    after(tensor, by_part[n])
                if swap:
                    hi = w_hi[:, s * CW + b * 256:s * CW + (b + 1) * 256]
                    lo = w_lo[:, s * CW + b * 256:s * CW + (b + 1) * 256]
                    passes = ((r_hi, hi), (r_hi, lo), (r_lo, hi))
                else:
                    hi = w_hi[:, s * CW + b * P:s * CW + (b + 1) * P]
                    lo = w_lo[:, s * CW + b * P:s * CW + (b + 1) * P]
                    passes = ((hi, r_hi), (hi, r_lo), (lo, r_hi))
                for j, (l, r) in enumerate(passes):
                    last = tensor.matmul(o, l, r, start=start and n == 0 and j == 0,
                                         stop=stop and n == len(parts) - 1 and j == 2)
            if each and o is not groups[-1][0]:
                marks.append(pe_done.on(last))
        m = chunk_mm.on(last)
        return [*marks, m] if each else m

    def parts(hi, lo, k0=0, n=KC, w=T, b0=0):
        return [(b0 + k, hi[:, (k0 + k) * w:(k0 + k + 1) * w], lo[:, (k0 + k) * w:(k0 + k + 1) * w]) for k in range(n)]

    def full(o, hi, lo, w=T):
        return [(o, parts(hi, lo, w=w), True, True)]

    def tile(t, f, w=T, stride=None, o=0):
        stride = w if stride is None else stride
        if isinstance(f, int):
            return t[:, f * stride + o:f * stride + o + w]
        return t[:, bass.ds(f * stride + o, w)]

    def col(name, k=0):
        k = VC[name] + k
        return vec[:, k:k + 1] if isinstance(k, int) else vec[:, bass.ds(k, 1)]

    ident, ones = cst[:, 0:P], cst[:, P:2 * P]

    nc.gpsimd.dma_start(vec[:, :], vecs).then_inc(s_vec, 16)
    nc.gpsimd.dma_start(cst[:, :], consts[:, 0:512]).then_inc(s_cst, 16)

    p = Plan(area)
    U = p("U", (NT + 1) * (T + 2 * HALO))
    o_sga = p.at
    hc_hi = p("hc_hi", NT * TC, F32R)
    hc_lo = p("hc_lo", NT * TC, F32R)
    sga = at("sga", NT * T, o_sga)
    yb_hi = p("yb_hi", NT * T, F32R)
    yb_lo = p("yb_lo", NT * T, F32R)
    mraw = p("mraw", MOD_RING * CW)
    us_hi = p("us_hi", T + 2 * HALO, F32R)
    us_lo = p("us_lo", T + 2 * HALO, F32R)
    csum = p("csum", T)
    u = p("u", T)
    u_hi = p("u_hi", T, F32R)
    u_lo = p("u_lo", T, F32R)
    o_tr = p.at
    tr = [p(f"tr{k}", T) for k in range(2)]
    ti = [p(f"ti{k}", T) for k in range(2)]
    aa = [p(f"aa{k}", T) for k in range(2)]
    xp = p("xp", T + SCONV_K)
    th = [xp[:, SCONV_K // 2:SCONV_K // 2 + T], p("th1", T)]
    tg = p("tg", T)
    mod0 = at("mod0", 16 * CW, o_sga)
    ctx_x = at("ctx_x", NT * TC, o_tr)
    sq, sq2, rstd, rstd_c, ssum = aa[0], aa[1], th[0], th[1], tg
    rows0 = at("rows0", 4 * T, area + 8 * K)
    n_t = [at(f"n_t{k}", T, area + 2 * K * k) for k in range(3)]
    assert o_sga + 64 * K <= o_tr

    csil = small[:, 0:2 * NT]
    modv0 = small[:, 16:64]
    modv1 = small[:, 64:88]
    g0, g0c, g1 = small[:, 88:96], small[:, 96:104], small[:, 104:112]
    sp4, nsp4 = small[:, 112:128], small[:, 128:144]
    hb_r, hb_i = small[:, 144:160], small[:, 160:176]
    ctx_state = small[:, 176:192]
    tmp16 = [small[:, 192 + 16 * j:208 + 16 * j] for j in range(6)]
    wdt_hi = at("wdt_hi", NT * NH, o_small + 4 * 288, F32R)
    wdt_lo = at("wdt_lo", NT * NH, o_small + 4 * 320, F32R)
    eps_rms, eps_ln = small[:, 352:353], small[:, 353:354]
    eps_sq = small[:, 387:388]
    cb2, gn, nsp8 = small[:, 354:362], small[:, 362:370], small[:, 370:386]

    for j in range(4):
        scalar.dma_start(mod0[:, j * 4 * CW:(j + 1) * 4 * CW].rearrange("p (a n) -> p a n", a=4),
                         modw[4 * j:4 * j + 4, :, :].rearrange("a p n -> p a n")).then_inc(s_mod0[j], 16)
        if j == 0:
            scalar.dma_start(X[:, :], x_in).then_inc(s_x, 16)
        if j == 1:
            scalar.dma_start(ctx_x[:, :], ctx_in).then_inc(s_ctx, 16)

    nc.sync.wait_ge(s_mod0[1], 16)
    for s in range(RING):
        nc.sync.dma_start(raw[:, s * CW:(s + 1) * CW], wts[s, :, :]).then_inc(s_raw[s], 16)
    with nc.sync.Fori(0, N_CHUNKS // RING - 1) as it:
        for s in range(RING):
            nc.sync.wait_ge(chunk_lo.sem, it * RING + s + 1)
            nc.sync.dma_start(raw[:, s * CW:(s + 1) * CW],
                              wts[bass.ds(it * RING + s + RING, 1), :, :].rearrange("a p n -> p (a n)")).then_inc(s_raw[s], 16)

    m_z = vop(vector.memset, small[:, :], 0.0)
    m_e = vop(vector.memset, eps_rms, EPS, needs=(m_z,))
    m_e = vop(vector.memset, eps_ln, 4e-5, needs=(m_e,))
    m_e = vop(vector.memset, eps_sq, EPS * EPS, needs=(m_e,))
    scalar.wait_ge(s_vec, 16)
    vector.wait_ge(s_vec, 16)
    cs3 = csil.rearrange("p (k two) -> p k two", two=2)
    aop(cs3[:, :, 0:1], vec[:, VC["c"]:VC["c"] + NT].rearrange("p (k a) -> p k a", a=1), ACT.Silu, needs=(m_z,))
    m_c = aop(cs3[:, :, 1:2], vec[:, VC["c_ctx"]:VC["c_ctx"] + NT].rearrange("p (k a) -> p k a", a=1), ACT.Silu)

    def softplus16(dst, src, negate, needs):
        z, e, s, s2, acc, t = tmp16
        m = ts(z, src, -1.0 if negate else 1.0, None, ALU.mult, needs=needs)
        m = aop(e, z, ACT.Abs, needs=(m,))
        m_x = aop(e, e, ACT.Exp, scale=-1.0, needs=(m,))
        m = ts(t, e, 2.0, None, ALU.add, needs=(m_x,))
        m = vop(vector.reciprocal, t, t, needs=(m,))
        m = tt(s, e, t, ALU.mult, needs=(m,))
        m = tt(s2, s, s, ALU.mult, needs=(m,))
        m = ts(acc, s2, 1.0 / 15, None, ALU.mult, needs=(m,))
        for k in (13, 11, 9, 7, 5, 3):
            m = stt(acc, acc, 1.0 / k, s2, ALU.add, ALU.mult, needs=(m,))
        m = stt(acc, acc, 1.0, s, ALU.add, ALU.mult, needs=(m,))
        m = ts(z, z, 0.0, None, ALU.max, needs=(m,))
        return stt(dst, acc, 2.0, z, ALU.mult, ALU.add, needs=(m,))

    lam = vec[:, VC["lam"]:VC["lam"] + 16]
    m = softplus16(sp4, lam, True, (m_e,))
    m = ts(nsp4, sp4, -4.0, None, ALU.mult, needs=(m,))
    m = ts(sp4, sp4, 4.0, None, ALU.mult, needs=(m,))
    ts(hb_r, vec[:, VC["b_r"]:VC["b_r"] + 16], 0.5, None, ALU.mult)
    ts(cb2, vec[:, VC["conv_b"]:VC["conv_b"] + NT], 2.0, None, ALU.mult)
    tt(gn, vec[:, VC["final_g"]:VC["final_g"] + NT], vec[:, VC["norm1_g"]:VC["norm1_g"] + NT], ALU.mult)
    ts(nsp8, nsp4, 2.0, None, ALU.mult, needs=(m,))
    m_small = ts(hb_i, vec[:, VC["b_i"]:VC["b_i"] + 16], 0.5, None, ALU.mult, needs=(m,))
    wdt = vec[:, VC["w_dt"]:VC["w_dt"] + NT * NH]
    m = aop(wdt_hi[:, :], wdt, ACT.Copy)
    tt(wdt_lo[:, :], wdt, wdt_hi[:, :].bitcast(F32), ALU.subtract, needs=(m,))

    def add_square(total, src, tmp, needs, gain=1.0, first=False):
        if first:
            return aop(total, src, ACT.Square, scale=gain, needs=needs)
        m = aop(tmp, src, ACT.Square, scale=gain, needs=needs)
        return tt(total, total, tmp, ALU.add, needs=(m,))

    def feature_sum(b, total, w, needs):
        after(tensor, *needs)
        return pe_done.on(tensor.matmul(bank(b, w), ones, total, start=True, stop=True))

    table = [None]

    def load_sqrt():
        table[0] = aop(small[:, 386:387], eps_rms, ACT.Sqrt, needs=table)

    read = [None]

    def rms_rstd(dst, src, eps, n, needs):
        m = aop(dst, src, ACT.Sqrt, bias=eps, scale=1.0 / n, needs=needs)
        read[0] = m
        return vop(vector.reciprocal, dst, dst, needs=(m,))

    def mod_rows(j):
        tensor.wait_ge(s_mod0[j], 16)
        for t in range(4):
            for k in range(KC):
                w = mod0[:, (4 * j + t) * CW + k * P:(4 * j + t) * CW + (k + 1) * P]
                last = tensor.matmul(bank(2 + j)[0:2, t * P:(t + 1) * P], csil[:, 2 * k:2 * k + 2], w,
                                     start=k == 0, stop=k == KC - 1)
        return pe_done.on(last)

    def copy_rows(j, m):
        return aop(rows0[0:2, j * T:(j + 1) * T], bank(2 + j)[0:2, :], ACT.Copy, needs=(m,))

    def mod_columns(j, m):
        after(tensor, m)
        for t in range(4 * j, 4 * j + 4):
            last = tensor.transpose(bank(6, 2, 2 * t), rows0[0:2, t * P:(t + 1) * P], ident[0:2, 0:2])
        return pe_done.on(last)

    after(tensor, m_c)
    scalar.wait_ge(s_x, 16)
    vector.wait_ge(s_x, 16)
    m = m_e
    for k in range(NT):
        m = add_square(ssum[:, :], tile(X, k), (sq, sq2)[k % 2][:, :], (m,) if k < 2 else (m2, m), first=k == 0)
        m2 = m
    m_r = [mod_rows(0), mod_rows(1)]
    tensor.wait_ge(s_cst, 16)
    m = feature_sum(0, ssum[:, :], T, (m,))
    m_rx = rms_rstd(rstd[:, :], bank(0), eps_rms, D, (m,))
    scalar.wait_ge(s_ctx, 16)
    vector.wait_ge(s_ctx, 16)
    for k in range(NT):
        m = add_square(ssum[:, 0:TC], tile(ctx_x, k, TC), (sq, sq2)[k % 2][:, 0:TC], (m,), first=k == 0)
    m_r.append(mod_rows(2))
    m_c = [copy_rows(j, m_r[j]) for j in range(2)]
    m = feature_sum(1, ssum[:, 0:TC], TC, (m,))
    m_rc = rms_rstd(rstd_c[:, 0:TC], bank(1, TC), eps_rms, D, (m,))
    mod_columns(0, m_c[0])
    mod_columns(1, m_c[1])
    for _ in range(AHEAD):
        split_next()
    m2 = copy_rows(2, m_r[2])
    m_r.append(mod_rows(3))
    m3 = copy_rows(3, m_r[3])
    mod_columns(2, m2)
    m = mod_columns(3, m3)

    def bias_mod0(t0, t1, b, needs):
        mb = vec[:, VC["mod_b"] + t0:VC["mod_b"] + t1].rearrange("p (k a) -> p k a", a=1)
        for j in range(2):
            d = modv0[:, 2 * t0:2 * t1].rearrange("p (k a) -> p k a", a=2)[:, :, j:j + 1]
            s = bank(b, 2 * (t1 - t0)).rearrange("p (k a) -> p k a", a=2)[:, :, j:j + 1]
            m = tt(d, s, mb, ALU.add, needs=needs)
        return m

    m = bias_mod0(0, 16, 6, (m, m_small))
    mv0 = modv0.rearrange("p (k two) -> p k two", two=2)
    ng = lambda l: vec[:, VC["norm_g"] + NT * l:VC["norm_g"] + NT * (l + 1)].rearrange("p (k a) -> p k a", a=1)
    stt(g0.rearrange("p (k a) -> p k a", a=1), mv0[:, 8:16, 0:1], 1.0, ng(0), ALU.add, ALU.mult, needs=(m,))
    m_g0 = stt(g0c.rearrange("p (k a) -> p k a", a=1), mv0[:, 8:16, 1:2], 1.0, ng(0), ALU.add, ALU.mult)

    def norm_split(src, w, r, gain, shift, hi, lo, tmps, needs, n=NT, also=None):
        marks, pend = [], None
        used = [None] * len(tmps)

        def finish(k, t, m2):
            if shift is None:
                m = tt(tile(lo, k, w), t, tile(hi, k, w).bitcast(F32), ALU.subtract, needs=(m2,))
            else:
                m = stt(tile(lo, k, w), t, shift(k), tile(hi, k, w).bitcast(F32), ALU.add, ALU.subtract, needs=(m2,))
            used[k % len(tmps)] = m
            marks.append(m)

        with beside():
            for k in range(n):
                t = tmps[k % len(tmps)][:, 0:w]
                m1 = stt(t, tile(src, k, w), gain(k), r, ALU.mult, ALU.mult, needs=(*needs, used[k % len(tmps)]))
                if shift is None:
                    m2 = aop(tile(hi, k, w), t, ACT.Copy, needs=(m1,))
                else:
                    m2 = aop(tile(hi, k, w), t, ACT.Identity, bias=shift(k), needs=(m1,))
                if also is not None:
                    also(k, m1)
                if pend is not None:
                    finish(*pend)
                pend = (k, t, m2)
            finish(*pend)
        return marks

    m_hc = norm_split(ctx_x, TC, rstd_c[:, 0:TC], lambda k: g0c[:, k:k + 1], lambda k: modv0[:, 2 * k + 1:2 * k + 2],
                      hc_hi, hc_lo, n_t, (m_g0, m_rc))
    m_h = norm_split(X, T, rstd[:, :], lambda k: g0[:, k:k + 1], lambda k: modv0[:, 2 * k:2 * k + 1],
                     h_hi, h_lo, n_t, (m_rx, m_hc[-1]))

    UW = T + 2 * HALO
    u3 = U[:, :].rearrange("p (f w) -> p f w", w=UW)
    vop(vector.memset, u3[:, :, 0:HALO], 0.0, needs=(m_h[-1],))
    vop(vector.memset, u3[:, :, HALO + T:UW], 0.0)
    vop(vector.memset, xp[:, :], 0.0)
    vop(vector.memset, ctx_state, 0.0)

    def mod_chunk(slot, turn, o, needs=()):
        tensor.wait_ge(s_mraw[slot], turn)
        after(tensor, *needs)
        for k in range(KC):
            last = tensor.matmul(o, mraw[:, slot * CW + k * P:slot * CW + (k + 1) * P],
                                 csil[:, 2 * k:2 * k + 2], start=k == 0, stop=k == KC - 1)
        return mod_mm.on(last)

    def head_input(i, w, xb_bank, m_xb, lp, u_read=None, between=lambda: None):
        m_xp = lp.note("xp", aop(xp[:, 2:2 + w], xb_bank, ACT.Copy, needs=(m_xb, lp.back("conv"), lp.back("th_read"))))
        sw = lambda k: col("sconv_w", i * SCONV_K + k)
        m = ts(u[:, 0:w], xp[:, 0:w], sw(0), col("sconv_b", i), ALU.mult, ALU.add, needs=(m_xp, u_read))
        for k in range(1, SCONV_K):
            between()
            m = stt(u[:, 0:w], xp[:, k:k + w], sw(k), u[:, 0:w], ALU.mult, ALU.add, needs=(m,))
        lp.note("conv", m)
        m = aop(u_hi[:, 0:w], u[:, 0:w], ACT.Copy, needs=(m, lp.back("gates")))
        between()
        return tt(u_lo[:, 0:w], u[:, 0:w], u_hi[:, 0:w].bitcast(F32), ALU.subtract, needs=(m,))

    last_gate = [None]

    def head_scan(i, w, m_gates, gates, init, lp, part=None, got=None, between=lambda: None):
        m_t, m_iu, res = [], [], []
        if part == 1:
            return head_scan_end(w, got, init, lp, between)
        for k in range(2):
            c = i * 2 + k
            at_c = lambda o: small[:, bass.ds(o + c, 1)]
            m_r = aop(tr[k][:, 0:w], gates[2 * k], ACT.Tanh, bias=at_c(144), scale=0.5, needs=(m_gates, lp.back("scans")))
            m_i = aop(ti[k][:, 0:w], gates[2 * k + 1], ACT.Tanh, bias=at_c(160), scale=0.5)
            aop(aa[k][:, 0:w], tr[k][:, 0:w], ACT.Exp, bias=at_c(128), scale=at_c(128), needs=(m_r,))
            m_h = aop(th[k][:, 0:w], tr[k][:, 0:w], ACT.Tanh, bias=at_c(112), scale=at_c(112))
            m_2 = aop(tr[k][:, 0:w], tr[k][:, 0:w], ACT.Exp, bias=at_c(370), scale=at_c(370))
            m_t.append((m_i, m_2))
        last_gate[0] = lp.note("gate_read", m_i)
        for k in range(2):
            m_i, m_h = m_t[k]
            m_v = stt(th[k][:, 0:w], tr[k][:, 0:w], 1.0, th[k][:, 0:w], ALU.add, ALU.mult, needs=(m_h,))
            between()
            m = stt(ti[k][:, 0:w], ti[k][:, 0:w], 1.0, u[:, 0:w], ALU.add, ALU.mult)
            between()
            m_iu.append((m_v, m))
        return m_iu if part == 0 else head_scan_end(w, m_iu, init, lp, between)

    def head_scan_end(w, m_iu, init, lp, between):
        res = []
        for k in range(2):
            m_s = aop(th[k][:, 0:w], th[k][:, 0:w], ACT.Sqrt, scale=0.25, needs=(m_iu[k][0],))
            m = tt(ti[k][:, 0:w], ti[k][:, 0:w], th[k][:, 0:w], ALU.mult, needs=(m_s, m_iu[k][1]))
            if k == 0:
                lp.note("th_read", m)
            between()
            o, d0, d1 = (t[:, 0:w] if k == 0 else t[:, 0:w][:, ::-1] for t in (tr[k], aa[k], ti[k]))
            res.append(vop(vector.tensor_tensor_scan, o, d0, d1, init(k), ALU.mult, ALU.add, needs=(m,)))
            between()
        lp.note("scans", res[-1])
        return res

    nc.gpsimd.wait_ge(pe_done.sem, pe_done.n)
    nc.gpsimd.wait_ge(v_done.sem, v_done.n)
    with loop("va", NT, chunks=4, banks_free=(m_e,)) as lp:
        i = lp.i
        nc.gpsimd.wait_ge(mod_mm.sem, i + 3)
        nc.gpsimd.dma_start(mraw[:, 0:CW], modw[bass.ds(i + 16, 1), :, :].rearrange("a p n -> p (a n)")).then_inc(s_mraw[0], 16)
        m_xb = chunk(full(bank(4, TC), hc_hi, hc_lo, w=TC), needs=(lp.back("xp"),), by_part=m_hc)
        m_u = head_input(i, TC, bank(4, TC), m_xb, lp)
        m_vg = chunk(full(bank(1), h_hi, h_lo), needs=(lp.back("sig"),), by_part=m_h)
        m_sig = lp.note("sig", aop(tg[:, :], bank(1), ACT.Tanh, scale=0.5, needs=(m_vg, lp.back("uu"))))
        m_va = chunk(full(bank(0), h_hi, h_lo), needs=(lp.back("uu"),))
        m_uu = lp.note("uu", stt(tile(U, i, T, UW, UW + HALO), tg[:, :], 1.0, bank(0), ALU.add, ALU.mult, needs=(m_va, m_sig)))
        mod_chunk(0, 16 * (i + 1), banks[:, bass.ds(2 * 512 + 2 * i, 2)])
        gates = [bank(5, TC), bank(5, TC, TC), bank(6, TC), bank(6, TC, TC)]
        m_gt = lp.note("gates", chunk([(o, [(b, u_hi[:, 0:TC], u_lo[:, 0:TC])], True, True) for b, o in enumerate(gates)],
                                      needs=(m_u, lp.back("gate_read"))))
        res = head_scan(i, TC, m_gt, gates, lambda k: 0.0, lp)
        for k in range(2):
            vop(vector.tensor_copy, small[:, bass.ds(176 + i * 2 + k, 1)], tr[k][:, (TC - 1, 0)[k]:(TC, 1)[k]], needs=(res[k],))

    m_gr = last_gate[0]
    m = vop(vector.memset, xp[:, :], 0.0)
    after(scalar, m)
    vop(vector.memset, csum[:, :], 0.0)
    nc.gpsimd.wait_ge(mod_mm.sem, NT + 3)
    with loop("heads", NT // 2, chunks=12, banks_free=(m_uu,)) as lp:
        turns = Turns(lp, 2)
        for e in range(2):
            i, tn = lp.i * 2 + e, turns.at(e)
            for n in (2 * e, 2 * e + 1):
                nc.gpsimd.wait_ge(mod_mm.sem, lp.i * 4 + n + NT + 3 + 1 - MOD_RING)
                nc.gpsimd.dma_start(mraw[:, n % 2 * CW:(n % 2 + 1) * CW],
                                    modw[bass.ds(lp.i * 4 + n + 24, 1), :, :].rearrange("a p n -> p (a n)")).then_inc(s_mraw[n % 2], 16)

            tap_at, tap_m = [PE_TAPS], [tn.back("taps")]

            def tap():
                k, acc = tap_at[0], tile(U, i, T, UW)
                src, w = tile(U, i, T, UW, UW + k), col("conv_w", i * CONV_K + k)
                if k == PE_TAPS:
                    tap_m[0] = ts(acc, src, w, small[:, bass.ds(354 + i, 1)], ALU.mult, ALU.add, needs=tap_m)
                else:
                    tap_m[0] = stt(acc, src, w, acc, ALU.mult, ALU.add, needs=tap_m)
                tap_at[0] = k + 1

            def mod(j):
                n = 2 * e + j
                return mod_chunk(j, lp.i * 32 + 16 * ((NT if j == 0 else 0) + n // 2 + 1),
                                 banks[:, bass.ds(2 * 512 + 16 + 8 * lp.i + 2 * n, 2)])

            m_xb = chunk(full(bank(0), h_hi, h_lo), needs=(tn.back("sga"),))
            mod(0)
            m = aop(us_hi[:, :], tile(U, i, UW, UW, UW), ACT.Copy, needs=(tn.back("conv_pe"),))
            m_us = tt(us_lo[:, :], tile(U, i, UW, UW, UW), us_hi[:, :].bitcast(F32), ALU.subtract, needs=(m,))
            m_u = head_input(i, T, bank(0), m_xb, tn, tn.back("yb_lo"), tap)
            m_gb = chunk(full(bank(1), h_hi, h_lo), needs=(tn.back("sgb"),))
            mod(1)
            m = aop(tg[:, :], bank(1), ACT.Tanh, scale=0.5, needs=(m_gb, tn.back("yb_lo")))
            tap()
            m_sgb = tn.note("sgb", stt(tg[:, :], tg[:, :], 1.0, bank(1), ALU.add, ALU.mult, needs=(m,)))
            tap()
            gates = [bank(4), bank(5), bank(6), bank(7)]
            m_ga = chunk(full(bank(0), h_hi, h_lo), needs=(tn.last["xp", e],))
            m_gt = tn.note("gates", chunk([(o, [(b, u_hi[:, :], u_lo[:, :])], True, True) for b, o in enumerate(gates)],
                                          needs=(m_u, tn.back("gate_read"), m_gr if e == 0 else None)))
            m = aop(tile(sga, i), bank(0), ACT.Tanh, scale=0.5, needs=(m_ga,))
            tn.note("sga", stt(tile(sga, i), tile(sga, i), 1.0, bank(0), ALU.add, ALU.mult, needs=(m,)))
            res_v = head_scan(i, T, m_gt, gates, lambda k: small[:, bass.ds(176 + i * 2 + k, 1)], tn, part=0, between=tap)
            for half in range(2):
                m_cv = chunk([(bank(3), [(b, us_hi[:, 8 * half + b:8 * half + b + T], us_lo[:, 8 * half + b:8 * half + b + T])
                                         for b in range(KC)], half == 0, half == 1)],
                             needs=(m_us, tn.back("conv_sum")) if half == 0 else ())
            tn.note("conv_pe", m_cv)
            tap()
            res = head_scan(i, T, m_gt, gates, lambda k: small[:, bass.ds(176 + i * 2 + k, 1)], tn, part=1, got=res_v, between=tap)
            assert tap_at[0] == CONV_K
            m = tt(u[:, :], tr[0][:, :], tr[1][:, :], ALU.add, needs=res)
            m_1 = tn.note("conv_sum", tt(tile(U, i, T, UW), bank(3), tile(U, i, T, UW), ALU.add,
                                         needs=(tn.note("taps", tap_m[0]), m_cv)))
            m = stt(u[:, :], u[:, :], 0.5, tg[:, :], ALU.mult, ALU.mult, needs=(m, m_sgb))
            m_taps = tt(csum[:, :], csum[:, :], tile(U, i, T, UW), ALU.add, needs=(m_1,))
            m = aop(tile(yb_hi, i), u[:, :], ACT.Copy, needs=(m,))
            m_yb = tn.note("yb_lo", tt(tile(yb_lo, i), u[:, :], tile(yb_hi, i).bitcast(F32), ALU.subtract, needs=(m,)))

    for n in range(NT):
        nc.gpsimd.wait_ge(mod_mm.sem, 3 + 3 * NT + n + 1 - MOD_RING)
        nc.gpsimd.dma_start(mraw[:, n % 2 * CW:(n % 2 + 1) * CW], modw[40 + n, :, :]).then_inc(s_mraw[n % 2], 16)

    def gate_chunk(n, b, needs=()):
        return mod_chunk(n % 2, 16 * ((NT if n % 2 == 0 else 0) + NT + n // 2 + 1), bank(b, 2, 16 + 2 * (2 * NT + n)), needs)

    for n in range(NT // 2):
        m = gate_chunk(n, 2)

    def bias_mod1(t0, t1, b, needs):
        mb = vec[:, VC["mod_b"] + 24 + t0:VC["mod_b"] + 24 + t1].rearrange("p (k a) -> p k a", a=1)
        return tt(modv1[:, t0:t1].rearrange("p (k a) -> p k a", a=1),
                  bank(b, 2 * (t1 - t0), 16 + 2 * t0).rearrange("p (k two) -> p k two", two=2)[:, :, 0:1], mb, ALU.add, needs=needs)

    m = bias_mod1(0, 20, 2, (m,))
    bias_mod0(16, 24, 2, ())
    m_mod = Mark(v_done, v_done.n, None)
    m = stt(g1, modv1[:, 8:16], 1.0, vec[:, VC["norm_g"] + NT:VC["norm_g"] + 2 * NT], ALU.add, ALU.mult, needs=(m,))
    mu, rs, s_a, ssq = aa[0], aa[1], (tr[0], tr[1]), ti[0]
    s_b, s_c = (th[0], th[1], u), (ti[1], tg, tr[0])
    m_sum = feature_sum(0, csum[:, :], T, (m_taps, m))
    BANK_OF = (4, 5, 6, 7, 3, 2, 0, 1)

    def yb_chunk(f, needs=()):
        chunk([(bank(BANK_OF[f]), parts(yb_hi, yb_lo), True, False)], needs=needs, by_part=[None] * 7 + [m_yb])

    m_mu = ts(mu[:, :], bank(0), 1.0 / D, None, ALU.mult, needs=(m_sum,))
    pend, m_sq = None, [None, None]
    for k in range(NT + 1):
        if k < NT:
            m1 = tt(tile(U, k, T, UW), tile(U, k, T, UW), mu[:, :], ALU.subtract, needs=(m_mu,))
            m1 = aop(ssq[:, :] if k == 0 else s_a[k % 2][:, :], tile(U, k, T, UW), ACT.Square, needs=(m1, m_sq[k % 2]))
        if k % 3 == 1:
            yb_chunk(k // 3)
        if k > 1:
            m_sq[(k - 1) % 2] = m = tt(ssq[:, :], ssq[:, :], s_a[(k - 1) % 2][:, :], ALU.add, needs=(pend, m_sq[k % 2]))
        pend = m1
    load_sqrt()
    m = feature_sum(1, ssq[:, :], T, (m,))
    m_rs = rms_rstd(rs[:, :], bank(1), eps_ln, D, (m,))
    m_sq1 = read[0]
    m_ya, pend1, pend2, m_hi2, used = [], None, None, None, [None] * 3
    for k in range(NT + 2):
        if k % 2 == 0:
            f = 3 + k // 2
            yb_chunk(f, needs=({5: m_mod, 6: m_mu, 7: m_sq1}.get(f),))
        if k < NT:
            m = stt(s_b[k % 3][:, :], tile(U, k, T, UW), col("ln_g", k), rs[:, :], ALU.mult, ALU.mult, needs=(m_rs, used[k % 3]))
            m_si = aop(s_c[k % 3][:, :], s_b[k % 3][:, :], ACT.Silu, bias=col("ln_b", k), needs=(m,))
        if 0 < k <= NT:
            j = k - 1
            m = stt(s_b[j % 3][:, :], s_c[j % 3][:, :], 0.5, tile(sga, j), ALU.mult, ALU.mult, needs=(pend1,))
            m_hi2 = aop(tile(h_hi, j), s_b[j % 3][:, :], ACT.Copy, needs=(m,))
        if k > 1:
            j = k - 2
            m = used[j % 3] = tt(tile(h_lo, j), s_b[j % 3][:, :], tile(h_hi, j).bitcast(F32), ALU.subtract, needs=(pend2,))
            m_ya.append(m)
        pend1, pend2 = m_si, m_hi2

    s1, s2, sqa, sqb = (at(f"s_{n}", T, limit // 32 * 32 - 2 * K * (n + 1)) for n in range(4))
    after(scalar, m_ya[-1])
    after(vector, m_ya[-1])

    m_sqf, m_fr = None, [None] * NT
    for f in range(NT):
        o = BANK_OF[f]
        m = chunk([(bank(o), parts(h_hi, h_lo), False, True)], by_part=m_ya if f == 0 else None)
        m_fr[f] = m_res = stt(tile(X, f), bank(o), modv0[:, 32 + 2 * f:33 + 2 * f], tile(X, f), ALU.mult, ALU.add, needs=(m,))
        m_sqf = add_square(s1[:, :], tile(X, f), sqa[:, :], (m_res, m_sqf), first=f == 0)
    m_x = m_sqf

    p = Plan(area)
    y1_hi = p("y1_hi", 2 * NT * T, F32R)
    y1_lo = p("y1_lo", 2 * NT * T, F32R)
    d_hi = p("d_hi", 4 * T, F32R)
    d_lo = p("d_lo", 4 * T, F32R)
    LW = 88
    lev0 = [p(f"lev0_{k}", 8 * LW) for k in range(2)]
    lev = p("lev", POOL_LEVELS * 8 * LW)
    sg = [p(f"sg{k}", T) for k in range(4)]
    rstd, nt_ = lev0[0][:, 0:T], [lev[:, T * k:T * (k + 1)] for k in range(3)]

    m_free = Mark(chunk_mm, chunk_mm.n, None)
    after(scalar, m_free)
    after(vector, m_free)
    load_sqrt()
    for n in (4, 5):
        gate_chunk(n, BANK_OF[0], (m_fr[0],))
    m = feature_sum(7, s1[:, :], T, (m_x,))
    for n in (6, 7):
        m_g = gate_chunk(n, BANK_OF[0])
    m = rms_rstd(rstd, bank(7), eps_rms, D, (m,))
    m_hk = norm_split(X, T, rstd, lambda k: g1[:, k:k + 1], lambda k: modv1[:, k:k + 1], h_hi, h_lo, nt_, (m,))
    bias_mod1(20, 24, BANK_OF[0], (m_g,))
    after(scalar, m_g)
    m = vop(vector.memset, lev0[0][:, :], 0.0, needs=(m_hk[-1],))
    vop(vector.memset, lev0[1][:, :], 0.0)
    vop(vector.memset, lev[:, :], 0.0)

    rows = lambda ap, w: ap.rearrange("p (r w) -> p r w", w=w)
    PADL = 8
    with loop("odd", 2, chunks=20, banks_free=(m_x,)) as lp:
        turns = Turns(lp, 2)
        for gg in range(2):
            tn, group = turns.at(gg), lp.i * 2 + gg
            m_l, m_sub, m_dhi, m_dlo = [], [], [], []

            def d_low(j):
                c = rows(lev0[j % 2][:, :], LW)[:, :, PADL:PADL + ROW]
                m_dlo.append(tn.note(f"dlo{j}", tt(rows(tile(d_lo, j), ROW), c, rows(tile(d_hi, j).bitcast(F32), ROW),
                                                   ALU.subtract, needs=(m_dhi[j],))))

            def d_high():
                j = len(m_dhi)
                if j < len(m_sub):
                    c = rows(lev0[j % 2][:, :], LW)[:, :, PADL:PADL + ROW]
                    m_dhi.append(aop(rows(tile(d_hi, j), ROW), c, ACT.Copy, needs=(m_sub[j], tn.back("grp"))))

            def pooled(j):
                m = chunk(full(bank(j % 2), h_hi, h_lo), needs=(m_l[j - 2] if j > 1 else tn.back(f"l{j + 2}"),),
                          by_part=m_hk if gg == 0 and j == 0 else None)
                d_high()
                l0 = rows(lev0[j % 2][:, :], LW)
                c0 = l0[:, :, PADL:PADL + ROW]
                m_l.append(tn.note(f"l{j}", aop(c0, rows(bank(j % 2), ROW), ACT.Copy,
                                                needs=(m, m_dlo[j - 2] if j > 1 else tn.back(f"dlo{j + 2}")))))
                below, m, shift0 = l0, m_l[j], 0
                for g in range(POOL_LEVELS - 1 + gg):
                    w = 2 << g
                    n = PADL + ROW + PADL - w + 1
                    here = rows(lev[:, g * 8 * LW:(g + 1) * 8 * LW], LW)
                    m = tt(here[:, :, w // 2:w // 2 + n], below[:, :, shift0:shift0 + n],
                           below[:, :, shift0 + w // 2:shift0 + w // 2 + n], ALU.add, needs=(m,))
                    below, shift0 = here, w // 2
                if j:
                    d_low(j - 1)
                sums = rows(lev[:, bass.ds(group * (8 * LW), 8 * LW)], LW)[:, :, PADL:PADL + ROW]
                inv = cst[:, bass.ds(group * ROW + 2 * P, ROW)].rearrange("p (a w) -> p a w", a=1).to_broadcast([P, 8, ROW])
                m = tt(sums, sums, inv, ALU.mult, needs=(m,))
                m = tt(c0, sums, c0, ALU.subtract, needs=(m,))
                m_sub.append(m)

            m_s = []

            def gate(t):
                m = chunk(full(bank(2 + t % 2), h_hi, h_lo), needs=(m_s[t - 2] if t > 1 else tn.back(f"sil{t + 2}"),))
                d_high()
                m_s.append(tn.note(f"sil{t}", aop(sg[t][:, :], bank(2 + t % 2), ACT.Silu, needs=(m, tn.back(f"ylo{t}")))))

            pooled(0)
            pooled(1)
            gate(0)
            pooled(2)
            gate(1)
            pooled(3)
            gate(2)
            d_low(3)
            gate(3)
            for half in range(2):
                dp = [[(4 * e + k, tile(d_hi, k), tile(d_lo, k)) for k in range(4)] for e in range(2)]
                m_g = chunk([(bank(4 + 2 * half + e), dp[e], True, True) for e in range(2)],
                            needs=(m_dlo[3], tn.back(f"y{2 * half + 1}")))
                for e in range(2):
                    t = 2 * half + e
                    f = group * 4 + t
                    m = tn.note(f"y{t}", stt(sg[t][:, :], bank(4 + t), col("od_scale", f), sg[t][:, :], ALU.mult, ALU.mult,
                                             needs=(m_g, m_s[t])))
                    m = aop(tile(y1_hi, f), sg[t][:, :], ACT.Copy, needs=(m,))
                    m_ylo = tn.note(f"ylo{t}", tt(tile(y1_lo, f), sg[t][:, :], tile(y1_hi, f).bitcast(F32), ALU.subtract, needs=(m,)))
            tn.note("grp", m_g)

    m = vop(vector.memset, s1[:, :], 0.0, needs=(m_ylo,))
    m = vop(vector.memset, s2[:, :], 0.0)
    with loop("od_out", NT // 2, chunks=4, banks_free=(m_l[2], m_l[3])) as lp:
        turns = Turns(lp, 2)
        for j in range(2):
            tn = turns.at(j)
            f = lp.i * 2 + j
            chunk([(bank(j), parts(y1_hi, y1_lo), True, False)], needs=(lp.back(f"res{j}"),))
            m = chunk([(bank(j), [(k, tile(y1_hi, KC + k), tile(y1_lo, KC + k)) for k in range(KC)], False, True)],
                      needs=(m_ylo,) if j == 0 else ())
            m_x = tn.note("res", stt(tile(X, f), bank(j), small[:, bass.ds(64 + 16 + f, 1)], tile(X, f), ALU.mult, ALU.add, needs=(m,)))
            tn.note("s1", add_square(s1[:, :], tile(X, f), sqa[:, :], (m_x, tn.back("s1"))))
            m_s2 = tn.note("s2", add_square(s2[:, :], tile(X, f), sqb[:, :], (m_x, tn.back("s2")), gain=col("final_g", f)))

    p = Plan(area2)
    y_hi = p("y_hi", 8 * T, F32R)
    y_lo = p("y_lo", 8 * T, F32R)
    o_m = p.at
    qk0 = p("qk0", 4 * T)
    vv0 = p("vv0", NB * 256)
    XW = T + SSM_K
    cpad = [p(f"cpad{k}", XW) for k in range(2)]
    ct = [p(f"ct{k}", T) for k in range(2)]
    M = at("M", NT * T, o_m)
    gs = [at("gs0", T, o_m + 16 * K), at("gs1", T, o_m + 18 * K)]
    assert o_m + 20 * K <= p.at
    o_2 = p.at
    qk1 = p("qk1", 4 * T)
    vv1 = p("vv1", NB * 256)
    zs = p("zs", 2 * T)
    bc = p("bc", 4 * T)
    ew = [p(f"ew{k}", CAUSAL) for k in range(3)]
    xd = p("xd", NB * 256)
    abc = p("abc", T)
    dtv, av, acs, mx, nl = p("dtv", 16), p("av", 16), p("acs", 16), p("mx", NB), p("nl", NB)
    gs += [p("gs2", T), p("gs3", T)]
    m_hi = at("m_hi", NT * T, o_2, F32R)
    m_lo_ = at("m_lo", NT * T, o_2 + 16 * K, F32R)
    yt = [at(f"yt{k}", T, o_2 + 2 * K * k) for k in range(2)]

    rstd, r2, nt_ = zs[:, 0:T], zs[:, T:2 * T], [bc[:, T * k:T * (k + 1)] for k in range(3)]
    m_mm = Mark(chunk_mm, chunk_mm.n, None)
    after(vector, m_mm, m_s2)
    after(scalar, m_mm, m_s2)
    after(nc.gpsimd, m_s2, m_mm)
    nc.gpsimd.dma_start(cst2[:, :], consts[:, 512:NCONST]).then_inc(s_cst2, 16)
    tri_ones, after_m = cst2[:, 0:512], cst2[:, 512:640]
    past, neg = cst2[:, 640:768], cst2[:, 768:896]
    tri = tri_ones[:, 0:P]

    load_sqrt()
    m = stt(s2[:, :], s1[:, :], EPS, s2[:, :], ALU.mult, ALU.add, needs=(m_s2,))
    m = feature_sum(7, s2[:, :], T, (m,))
    m_q = feature_sum(6, s1[:, :], T, ())
    m = aop(r2, bank(7), ACT.Sqrt, bias=eps_sq, scale=1.0 / D, needs=(m,))
    m_r = aop(rstd, bank(6), ACT.Sqrt, bias=eps_rms, scale=1.0 / D, needs=(m_q,))
    m = vop(vector.reciprocal, r2, r2, needs=(m,))
    m_hk = norm_split(X, T, r2, lambda k: gn[:, k:k + 1], None, h_hi, h_lo, nt_, (m,))
    m_q = vop(vector.reciprocal, rstd, rstd, needs=(m_r, m_hk[-1]))
    for k in range(NT):
        m_h = stt(tile(X, k), tile(X, k), col("final_g", k), rstd, ALU.mult, ALU.mult, needs=(m_q,))

    after(scalar, m_h)
    vop(vector.memset, cpad[0][:, :], 0.0)
    m_pad = vop(vector.memset, cpad[1][:, :], 0.0)
    bank_free = {b: m_r for b in range(4, 8)}
    turn_b = [0]

    def next_bank():
        turn_b[0] = (turn_b[0] + 1) % 4
        return 4 + turn_b[0]

    def split_y(f, src, needs):
        m = aop(tile(y_hi, f), src, ACT.Copy, needs=needs)
        return tt(tile(y_lo, f), src, tile(y_hi, f).bitcast(F32), ALU.subtract, needs=(m,))

    done = {}

    def taps_of(dst, src, name, t, n, first, needs):
        for k in range(n):
            a, w = src[:, first + k:first + k + T], col(name, t * n + k)
            if k == 0:
                m = ts(dst, a, w, None, ALU.mult, needs=needs)
            else:
                m = stt(dst, a, w, dst, ALU.mult, ALU.add, needs=(m,))
        return m

    def inputs_a():
        m_y = None
        for t in range(2):
            marks, bs = [], []
            for n in range(3):
                b = next_bank()
                bs.append(b)
                marks.append(chunk(full(bank(b), h_hi, h_lo), needs=(bank_free[b],), ))
                if n == 0:
                    bank_free[b] = m = aop(ct[t][:, :], bank(b), ACT.Copy, needs=(marks[0], m_pad))
                if n == 1:
                    bank_free[b] = m = tt(cpad[t][:, SSM_K - 1:SSM_K - 1 + T], bank(b), ct[t][:, :], ALU.mult, needs=(m, marks[1]))
                    m = taps_of(ct[t][:, :], cpad[t], "conv_a_w", t, SHORT_K, 1, (m,))
                if n == 2:
                    bank_free[b] = m = tt(ct[t][:, :], bank(b), ct[t][:, :], ALU.mult, needs=(m, marks[2]))
                    done["ya"] = split_y(t, ct[t][:, :], (m,))
                yield

    def inputs_qkv(n, qk, vv):
        for t in range(4):
            b = next_bank()
            m = chunk(full(bank(b), h_hi, h_lo), needs=(bank_free[b],), by_part=m_hk if t == n == 0 else None)
            bank_free[b] = done["qk", n] = aop(tile(qk, t), bank(b), ACT.Copy, needs=(m,))
            yield
        for half in range(2):
            groups = []
            for tb in range(NB):
                pr = [(k, h_hi[:, (4 * half + k) * T + tb * P:(4 * half + k) * T + (tb + 1) * P],
                       h_lo[:, (4 * half + k) * T + tb * P:(4 * half + k) * T + (tb + 1) * P]) for k in range(4)]
                groups.append((bank(4 + tb, 256), pr, half == 0, half == 1))
            m = chunk(groups, needs=[bank_free[4 + tb] for tb in range(NB)] if half == 0 else (), swap=True)
            if half == 0:
                yield
        for tb in range(NB):
            bank_free[4 + tb] = done["v", n] = aop(vv[:, tb * 256:(tb + 1) * 256], bank(4 + tb, 256), ACT.Copy, needs=(m,))
        yield

    def inputs_c():
        for t in range(2):
            b = next_bank()
            m = chunk(full(bank(b), h_hi, h_lo), needs=(bank_free[b],))
            bank_free[b] = aop(tile(zs, t), bank(b), ACT.Silu, needs=(m,))
            yield
        m_tap, m_act = [done["ya"]] * 2, [None, None]
        for t in range(4):
            b = next_bank()
            m = chunk(full(bank(b), h_hi, h_lo), needs=(bank_free[b],))
            bank_free[b] = m = aop(cpad[t % 2][:, SSM_K - 1:SSM_K - 1 + T], bank(b), ACT.Copy, needs=(m, m_tap[t % 2]))
            m_tap[t % 2] = m = taps_of(ct[t % 2][:, :], cpad[t % 2], "ssm_conv_w", t, SSM_K, 0, (m, m_act[t % 2]))
            done["bc"] = m_act[t % 2] = aop(tile(bc, t), ct[t % 2][:, :], ACT.Silu, bias=col("ssm_conv_b", t), needs=(m,))
            if t == 3:
                b = next_bank()
                after(tensor, bank_free[b])
                for k in range(NT):
                    wh, wl = (w[:, k * NH:(k + 1) * NH] for w in (wdt_hi, wdt_lo))
                    for j, (l, r) in enumerate(((wh, tile(h_hi, k)), (wl, tile(h_hi, k)), (wh, tile(h_lo, k)))):
                        last = tensor.matmul(bank(b)[0:NH, :], l, r, start=k == 0 and j == 0, stop=k == NT - 1 and j == 2)
                m = pe_done.on(last)
                bank_free[b] = m = aop(abc[0:NH, :], bank(b)[0:NH, :], ACT.Copy, needs=(m,))
                yield
                b = next_bank()
                after(tensor, m, bank_free[b])
                for tb in range(NB):
                    last = tensor.transpose(bank(b, NH, tb * NH), abc[0:NH, tb * P:(tb + 1) * P], ident[0:NH, 0:NH])
                m = pe_done.on(last)
                bank_free[b] = m = tt(av[:, :], bank(b, 16), vec[:, VC["dt_bias"]:VC["dt_bias"] + 16], ALU.add, needs=(m,))
                m = softplus16(dtv[:, :], av[:, :], False, (m,))
                m_e = aop(av[:, :], vec[:, VC["a_log"]:VC["a_log"] + 16], ACT.Exp, needs=(m,))
                done["a"] = stt(av[:, :], av[:, :], -1.0, dtv[:, :], ALU.mult, ALU.mult, needs=(m_e,))
            yield

    m_gs = [None] * 4

    def merge(n, br, first, last):
        for half in range(2):
            bs, m_s = [], []
            for j in range(4):
                b = 4 + j
                m = chunk(full(bank(b), h_hi, h_lo), needs=(bank_free[b],))
                bank_free[b] = m = aop(gs[j][:, :], bank(b), ACT.Sigmoid, needs=(m, m_gs[j], done["gs"]))
                m_s.append(m)
                yield
            m = chunk([(bank(4 + j), [(2 * j + k, tile(y_hi, 2 * br + k), tile(y_lo, 2 * br + k)) for k in range(2)], True, True)
                       for j in range(4)], needs=(*m_s, done[n]), each=True)
            with beside() if last else nullcontext():
                m_p, m_t = [None] * 4, [None] * 4
                for j in range(4 + 2):
                    if j < 4:
                        dst = tile(M, 4 * half + j) if first else gs[j][:, :]
                        m_p[j] = bank_free[4 + j] = m_gs[j] = tt(dst, bank(4 + j), gs[j][:, :], ALU.mult, needs=(m[j], m_s[j]))
                    if first:
                        continue
                    if 0 < j <= 4:
                        f = 4 * half + j - 1
                        m_t[j - 1] = m_gs[j - 1] = tt(tile(M, f), gs[j - 1][:, :], tile(M, f), ALU.add, needs=(m_p[j - 1],))
                        if last:
                            m_t[j - 1] = aop(tile(m_hi, f), tile(M, f), ACT.Copy, needs=(m_t[j - 1],))
                    if j > 1 and last:
                        f = 4 * half + j - 2
                        done["m", f] = tt(tile(m_lo_, f), tile(M, f), tile(m_hi, f).bitcast(F32), ALU.subtract, needs=(m_t[j - 2],))
            yield

    def blk(t, n, w=None):
        return t[:, OFF[n]:OFF[n] + (T - P * n if w is None else w)]

    def pblk(b, n, w=None, o=0):
        s = b * 512 + OFF[n] + o
        return banks[:, s:s + (T - P * n if w is None else w)]

    wide = lambda b: banks[:, b * 512:b * 512 + CAUSAL]
    scale = HD ** -0.5
    OUT = 3

    def weighted_values(h, vv, w):
        p0 = HD * (h % 2)
        for n in range(NB):
            last = tensor.matmul(banks[p0:p0 + HD, OUT * 512 + n * P:(OUT + 1) * 512],
                                 vv[:, n * 256 + h * HD:n * 256 + (h + 1) * HD], blk(w, n), start=n == 0, stop=n == NB - 1)
        return pe_done.on(last)

    def stick():
        sp_, zz, ww = ew
        after(tensor, done["qk", 0], done["v", 0])
        m_zb = m_pv = m_out = None
        for h in range(NH):
            t, p0 = h // 2, HD * (h % 2)
            q = qk0[p0:p0 + HD, t * T:(t + 1) * T]
            kk = qk0[p0:p0 + HD, (2 + t) * T:(3 + t) * T]
            after(tensor, m_zb)
            for n in range(NB):
                last = tensor.matmul(pblk(0, n), kk[:, n * P:(n + 1) * P], q[:, n * P:T], start=True, stop=True)
            m = pe_done.on(last)
            m_abs = aop(ww[:, :], wide(0), ACT.Abs, scale=scale, needs=(m, m_pv, m_out))
            m_1 = aop(zz[:, :], ww[:, :], ACT.Exp, scale=-1.0, needs=(m_abs, m_zb))
            m_1 = aop(ww[:, :], zz[:, :], ACT.Ln, bias=1.0, needs=(m_1,))
            m = ts(sp_[:, :], wide(0), scale, 0.0, ALU.mult, ALU.max, needs=(m_abs,))
            m = tt(sp_[:, :], sp_[:, :], ww[:, :], ALU.add, needs=(m, m_1))
            m_z = stt(zz[:, :], wide(0), scale, sp_[:, :], ALU.mult, ALU.subtract, needs=(m,))
            for n in range(NB):
                m = tt(blk(sp_, n, P), blk(sp_, n, P), past, ALU.mult, needs=(m_z,))
            yield
            after(tensor, m)
            for n in range(NB):
                for k in range(n, NB):
                    last = tensor.matmul(pblk(0, n, T - P * k, P * (k - n)), after_m if k == n else ones, blk(sp_, k),
                                         start=k == n, stop=k == NB - 1)
            m = pe_done.on(last)
            m_zb = m = tt(zz[:, :], zz[:, :], wide(0), ALU.subtract, needs=(m,))
            m_w = aop(ww[:, :], zz[:, :], ACT.Exp, needs=(m,))
            for n in range(NB):
                m = tt(blk(ww, n, P), blk(ww, n, P), past, ALU.mult, needs=(m_w,))
            yield
            after(tensor, m, m_out)
            m_pv = weighted_values(h, vv0, ww)
            if h % 2:
                m = aop(sp_[:, 0:T], bank(OUT), ACT.Copy, needs=(m_pv,))
                m_out = done["yb"] = split_y(2 + t, sp_[:, 0:T], (m,))
            yield

    def moba():
        pm, pT, o = ew
        after(tensor, done["qk", 1], done["v", 1], done["yb"])
        after(scalar, done["yb"])
        m_pt = m_pv = m_out = m_cp = None
        for h in range(NH):
            t, p0 = h // 2, HD * (h % 2)
            q = qk1[p0:p0 + HD, t * T:(t + 1) * T]
            kk = qk1[p0:p0 + HD, (2 + t) * T:(3 + t) * T]
            after(tensor, m_cp)
            for b in range(NB):
                last = tensor.matmul(pblk(0, NB - 1 - b, (b + 1) * P), q[:, b * P:(b + 1) * P], kk[:, 0:(b + 1) * P], start=True, stop=True)
            m = pe_done.on(last)
            yield
            for b in range(NB):
                dg = pblk(0, NB - 1 - b, P, b * P)
                m_1 = tt(dg, dg, neg, ALU.add, needs=(m,))
                m_1 = vop(vector.reduce_max, mx[:, b:b + 1], pblk(0, NB - 1 - b, (b + 1) * P), AX.X, needs=(m_1,))
            m_1 = ts(mx[:, :], mx[:, :], -scale, None, ALU.mult, needs=(m_1,))
            for b in range(NB):
                m_p = aop(blk(pm, NB - 1 - b, (b + 1) * P), pblk(0, NB - 1 - b, (b + 1) * P), ACT.Exp, bias=mx[:, b:b + 1],
                          scale=scale, accum_out=nl[:, b:b + 1], needs=(m_1, m_pt))
            m = vop(vector.reciprocal, nl[:, :], nl[:, :], needs=(m_p,))
            for b in range(NB):
                m_n = ts(blk(pm, NB - 1 - b, (b + 1) * P), blk(pm, NB - 1 - b, (b + 1) * P), nl[:, b:b + 1], None, ALU.mult, needs=(m,))
            yield
            after(tensor, m_n)
            for b in range(NB):
                for k in range(b + 1):
                    src = pm[:, OFF[NB - 1 - b] + k * P:OFF[NB - 1 - b] + (k + 1) * P]
                    last = tensor.transpose(pblk(0, k, P, (b - k) * P), src, ident)
            m_pt = pe_done.on(last)
            m_cp = m = aop(pT[:, :], wide(0), ACT.Copy, needs=(m_pt, m_pv))
            yield
            after(tensor, m, m_out)
            m_pv = weighted_values(h, vv1, pT)
            if h % 2:
                m = aop(o[:, t * T:(t + 1) * T], bank(OUT), ACT.Copy, needs=(m_pv,))
                m_out = done["yd"] = split_y(6 + t, o[:, t * T:(t + 1) * T], (m,))
            yield

    def mamba():
        gm, dk = ew[0], (ew[1], ew[2])
        after(tensor, done["a"], done["bc"], done["yd"])
        after(vector, done["yd"])
        for n in range(NB):
            for k in range(n + 1):
                last = tensor.matmul(bank(OUT, NH, n * NH), tri if k == n else ones, av[:, k * NH:(k + 1) * NH], start=k == 0, stop=k == n)
        m = pe_done.on(last)
        m_acs = vop(vector.tensor_copy, acs[:, :], bank(OUT, 16), needs=(m, done["a"]))
        for t in range(2):
            for n in range(NB):
                last = tensor.transpose(banks[:, n * 256 + t * P:n * 256 + (t + 1) * P],
                                        bc[:, t * T + n * P:t * T + (n + 1) * P], ident)
        m = pe_done.on(last)
        m_free = tt(xd[:, :].rearrange("p (n d) -> p n d", d=HD), banks[:, 0:2 * 512].rearrange("p (n d) -> p n d", d=HD),
                           dtv[:, :].rearrange("p (n a) -> p n a", a=1).to_broadcast([P, 16, HD]), ALU.mult, needs=(m,))
        yield
        m_row, m_y, m_used = None, [None, None], None
        for g in range(2):
            bm = bc[g * HD:(g + 1) * HD, 2 * T:3 * T]
            cm = bc[g * HD:(g + 1) * HD, 3 * T:4 * T]
            after(tensor, m_free)
            for n in range(NB):
                last = tensor.matmul(pblk(0, n), bm[:, n * P:(n + 1) * P], cm[:, n * P:T], start=True, stop=True)
            m = pe_done.on(last)
            m_cp = aop(gm[:, :], wide(0), ACT.Copy, needs=(m, m_used))
            for n in range(NB):
                m_gm = tt(blk(gm, n, P), blk(gm, n, P), tri, ALU.mult, needs=(m_cp,))
            yield
            for e in range(2):
                h, p0, d_ = 2 * g + e, HD * e, dk[e]
                m = vop(vector.tensor_copy, abc[:, :].rearrange("p (n c) -> p n c", c=P),
                        av[:, :].rearrange("p (n h) -> p n h", h=NH)[:, :, h:h + 1].to_broadcast([P, NB, P]), needs=(m_row,))
                after(tensor, m, m_gm)
                for n in range(NB):
                    last = tensor.matmul(bank(e, T - P * n, P * n), abc[:, n * P:(n + 1) * P], tri_ones[:, 0:T - P * n],
                                         start=n == 0, stop=n == NB - 1)
                m_row = pe_done.on(last)
                for n in range(NB):
                    m = ts(blk(d_, n), bank(e, T - P * n, P * n), acs[:, n * NH + h:n * NH + h + 1], 0.0, ALU.subtract, ALU.min,
                           needs=(m_row, m_y[e], m_acs))
                m_free = m
                m = aop(d_[:, :], d_[:, :], ACT.Exp, needs=(m,))
                m_used = m = tt(d_[:, :], d_[:, :], gm[:, :], ALU.mult, needs=(m,))
                yield
                after(tensor, m, done.get("yc"))
                m_y[e] = weighted_values(h, xd, d_)
                yield
            m = m_y[1]
            m = stt(yt[g][:, :], tile(bc, g), col("ssm_d", g), bank(OUT), ALU.mult, ALU.add, needs=(m,))
            m = tt(yt[g][:, :], yt[g][:, :], tile(zs, g), ALU.mult, needs=(m,))
            m_s = aop(dk[0][:, 0:T], yt[g][:, :], ACT.Square, needs=(m,))
            m = feature_sum(2, dk[0][:, 0:T], T, (m_s, m_free))
            m_y[0] = m_y[1] = m = rms_rstd(dk[1][:, 0:T], bank(2), eps_rms, P, (m,))
            m_free = m = stt(yt[g][:, :], yt[g][:, :], col("ssm_norm_g", g), dk[1][:, 0:T], ALU.mult, ALU.mult, needs=(m,))
            m_y[0] = m_y[1] = m
            done["yc"] = split_y(4 + g, yt[g][:, :], (m,))
            yield

    def strand(*parts_):
        for g in parts_:
            yield from g

    def run(work, n=None):
        for _ in range(n if n is not None else 1 << 30):
            try:
                next(work)
            except StopIteration:
                return False
        return True

    def alternate(mixer, products, steps=(2, 1, 1)):
        n = 0
        while run(mixer, 1):
            run(products, steps[n % len(steps)])
            n += 1

    vector.wait_ge(s_cst2, 16)
    tensor.wait_ge(s_cst2, 16)
    done["gs"] = None
    run(inputs_qkv(0, qk0, vv0))
    products = strand(inputs_a(), inputs_qkv(1, qk1, vv1), inputs_c())
    alternate(stick(), products)
    run(products)
    after(vector, done["yb"], done["bc"])
    done["gs"] = done["yb"]
    done[0], done[1] = done["ya"], done["yb"]
    products = strand(merge(0, 0, True, False), merge(1, 1, False, False), merge(3, 3, False, False))
    alternate(moba(), products, (1, 1, 1, 1))
    done[3] = done["yd"]
    alternate(mamba(), products, (1,))
    run(products)
    done[2] = done["yc"]
    after(scalar, done["yc"])
    run(merge(2, 2, False, True))

    m_mk = [done["m", f] for f in range(NT)]
    m = vop(vector.memset, s1[:, :], 0.0)
    m_hx = []
    with loop("w_o", 2, chunks=4, banks_free=(bank_free[4], bank_free[5], bank_free[6], bank_free[7])) as lp:
        turns = Turns(lp, 4)
        for j in range(4):
            tn = turns.at(j)
            f = lp.i * 4 + j
            m = chunk(full(bank(j), m_hi, m_lo_), needs=(lp.back(f"res{j}"),), by_part=m_mk if j == 0 else None)
            m_x = tn.note("res", tt(tile(X, f), bank(j), tile(X, f), ALU.add, needs=(m,)))
            xg = (sqb, s2)[j % 2][:, :]
            m = ts(xg, tile(X, f), col("norm2_g", f), None, ALU.mult, needs=(m_x, tn.back("lo"), m_hx[j - 2] if j > 1 else None))
            m_sq = aop(sqa[:, :], tile(X, f), ACT.Square, needs=(m_x, tn.back("s1")))
            m = aop(tile(h_hi, f), xg, ACT.Copy, needs=(m,))
            m_x = tn.note("s1", tt(s1[:, :], s1[:, :], sqa[:, :], ALU.add, needs=(m_sq,)))
            m_hx.append(tn.note("lo", tt(tile(h_lo, f), xg, tile(h_hi, f).bitcast(F32), ALU.subtract, needs=(m,))))
    m_hx = [m.prev() for m in m_hx] + m_hx

    p = Plan(area)
    f_hi, f_lo = p("f_hi", FFN_TILES * T, F32R), p("f_lo", FFN_TILES * T, F32R)
    fs = [p(f"fs{k}", T) for k in range(2)]
    rstd = at("rstd_b", T, limit // 32 * 32 - 2 * K * 5)[:, :]
    assert p.at <= limit // 32 * 32 - 2 * K * 5
    m_mm = Mark(chunk_mm, chunk_mm.n, None)
    after(scalar, m_x, m_mm)
    after(vector, m_mm)
    load_sqrt()
    m = feature_sum(0, s1[:, :], T, (m_x,))
    m_r = rms_rstd(rstd, bank(0), eps_rms, D, (m,))
    with loop("ffn_in", FFN_TILES // 2, chunks=4, banks_free=()) as lp:
        for j in range(2):
            b = 4 + 2 * j
            m_g = chunk(full(bank(b), h_hi, h_lo), needs=(lp.back(f"up{j}"),), by_part=m_hx if j == 0 else None)
            m_u = chunk(full(bank(b + 1), h_hi, h_lo))
            f = lp.i * 2 + j
            m = tt(fs[j][:, :], bank(b), rstd, ALU.mult, needs=(m_g, m_r, lp.back(f"flo{j}")))
            m = aop(fs[j][:, :], fs[j][:, :], ACT.Silu, needs=(m,))
            m = lp.note(f"up{j}", tt(fs[j][:, :], bank(b + 1), fs[j][:, :], ALU.mult, needs=(m, m_u)))
            m = tt(fs[j][:, :], fs[j][:, :], rstd, ALU.mult, needs=(m,))
            m = aop(tile(f_hi, f), fs[j][:, :], ACT.Copy, needs=(m,))
            m_f = lp.note(f"flo{j}", tt(tile(f_lo, f), fs[j][:, :], tile(f_hi, f).bitcast(F32), ALU.subtract, needs=(m,)))
    after(scalar, m_f)
    m_res, m_s = [None] * 4, None
    for f in range(NT):
        for k0, n in ((0, 8), (8, 8), (16, FFN_TILES - 16)):
            m = chunk([(bank(f % 4), [(k, tile(f_hi, k0 + k), tile(f_lo, k0 + k)) for k in range(n)], k0 == 0, k0 == 16)],
                      needs=((m_f.prev() if f == 0 else m_res[f % 4]) if k0 == 0 else m_f if k0 == 16 and f == 0 else None,))
        m_res[f % 4] = tt(tile(X, f), bank(f % 4), tile(X, f), ALU.add, needs=(m,))
        m_s = add_square(s1[:, :], tile(X, f), sqa[:, :], (m_res[f % 4], m_s), first=f == 0)

    load_sqrt()
    m = feature_sum(7, s1[:, :], T, (m_s,))
    rstd = fs[0][:, :]
    m = rms_rstd(rstd, bank(7), eps_rms, D, (m,))
    for k in range(NT):
        m_x = stt(tile(X, k), tile(X, k), col("final_g2", k), rstd, ALU.mult, ALU.mult, needs=(m,))
        if k % 2:
            nc.sync.wait_ge(v_done.sem, m_x.value())
            nc.sync.dma_start(out[:, (k - 1) * T:(k + 1) * T], X[:, (k - 1) * T:(k + 1) * T]).then_inc(s_out, 16)
    nc.sync.wait_ge(s_out, 16 * NT // 2)
    assert state["chunk"] == N_CHUNKS, state["chunk"]
    ctx.close()


def constants():
    c = np.zeros((P, NCONST), np.float32)
    r, q = np.arange(P)[:, None], np.arange(P)[None, :]
    c[:, CC["ident"]:CC["ident"] + P] = r == q
    c[:, CC["ones"]:CC["ones"] + P] = 1
    t = np.arange(ROW)
    for g in range(POOL_LEVELS):
        w = 2 << g
        cnt = np.clip(t + w // 2, 0, ROW) - np.clip(t - w // 2, 0, ROW)
        c[:, CC["inv_cnt"] + g * ROW:CC["inv_cnt"] + (g + 1) * ROW] = np.float32(1) / cnt.astype(np.float32)
    c[:, CC["tri_ones"]:CC["tri_ones"] + P] = r <= q
    c[:, CC["tri_ones"] + P:CC["tri_ones"] + 512] = 1
    c[:, CC["after"]:CC["after"] + P] = r > q
    c[:, CC["past"]:CC["past"] + P] = r < q
    c[:, CC["neg"]:CC["neg"] + P] = np.where(q <= r, 0, -1e30)
    return c


def tiles_of(w):
    k, n = w.shape
    return w.reshape(k // P, P, n // P, P).transpose(2, 1, 0, 3).reshape(n // P, P, k)


def lay_out(a):
    ev, od = a["ev_w_in"][0], a["od_w_in"][0]
    evt = tiles_of(ev)
    zero = np.zeros((P, CW - 4 * P), np.float32)
    gates = [np.concatenate([a["ev_w_r"][0, 0, h], a["ev_w_i"][0, 0, h], a["ev_w_r"][0, 1, h], a["ev_w_i"][0, 1, h], zero], 1)
             for h in range(8)]
    s = []
    for i in range(NT):
        s += [evt[24 + i], evt[8 + i], evt[i], gates[i]]
    cw = a["ev_conv_w"][0]
    diag = np.zeros((NT, 2, P, KC, P), np.float32)
    for j in range(2):
        for b in range(KC):
            diag[:, j, range(P), b, range(P)] = cw[KC * j + b].reshape(NT, P)
    diag = diag.reshape(NT, 2, P, CW)
    for i in range(NT):
        s += [evt[24 + i], evt[32 + i], evt[16 + i], gates[i], diag[i, 0], diag[i, 1]]
    wo = tiles_of(a["ev_w_out"][0])
    s += [wo[f][:, CW:] for f in range(NT)] + [wo[f][:, :CW] for f in range(NT)]
    odt = tiles_of(od)
    for g in range(POOL_LEVELS):
        wg = tiles_of(a["od_w_grp"][0, g])
        s += [odt[4 * g + t if n == "u" else 16 + 4 * g + t] for n, t in (
            ("u", 0), ("u", 1), ("g", 0), ("u", 2), ("g", 1), ("u", 3), ("g", 2), ("g", 3))]
        for half in range(2):
            s += [np.concatenate([wg[2 * half], wg[2 * half + 1]], 1)]
    wo = tiles_of(a["od_w_out"][0])
    for f in range(NT):
        s += [wo[f][:, :CW], wo[f][:, CW:]]
    w = a["w_in_2"][0]
    A = tiles_of(w[:, 0:768])
    c0 = 768 + 768
    d0 = c0 + 772
    for base in (768, d0):
        s += list(tiles_of(w[:, base:base + 512]))
        v = w[:, base + 512:base + 768].reshape(2, 4, P, 256).transpose(0, 2, 1, 3).reshape(2, P, CW)
        s += [v[0], v[1]]
        if base == 768:
            for t in range(2):
                s += [A[t], A[4 + t], A[2 + t]]
    s += list(tiles_of(w[:, c0:c0 + 768]))
    wdt = w[:, c0 + 768:c0 + 772]
    G = tiles_of(w[:, d0 + 768:])
    for b in (0, 1, 3, 2):
        br = tiles_of(a["w_branch_2"][0, b])
        for half in range(2):
            s += [G[b * NT + 4 * half + j] for j in range(4)]
            s.append(np.concatenate([br[4 * half + j] for j in range(4)], 1))
    s += list(tiles_of(a["w_o_2"][0]))
    gu = tiles_of(a["w_gate_up_2"][0])
    for f in range(FFN_TILES):
        s += [gu[f], gu[FFN_TILES + f]]
    wd = tiles_of(a["w_down_2"][0])
    for f in range(NT):
        last = np.concatenate([wd[f][:, 2 * CW:], np.zeros((P, 3 * CW - FFN_TILES * P), np.float32)], 1)
        s += [wd[f][:, :CW], wd[f][:, CW:2 * CW], last]
    weights = np.stack(s)
    assert weights.shape == (N_CHUNKS, P, CW), weights.shape
    modw = np.concatenate([tiles_of(a["mod_w"][0]), tiles_of(a["mod_w"][1])])

    f = lambda v: np.asarray(v).reshape(-1, P).T
    k_ = lambda v: v.reshape(v.shape[0], -1, P).transpose(2, 1, 0).reshape(P, -1)
    rep = lambda v: np.broadcast_to(np.tile(v, NB)[None, :], (P, NB * NH))
    vals = {
        "c": f(a["c"]), "c_ctx": f(a["c_ctx"]), "norm_g": f(a["norm_g"]), "mod_b": f(a["mod_b"]),
        "conv_w": k_(a["ev_conv_w"][0]), "conv_b": f(a["ev_conv_b"]), "ln_g": f(a["ev_ln_g"]), "ln_b": f(a["ev_ln_b"]),
        "sconv_w": k_(a["ev_sconv_w"][0]), "sconv_b": f(a["ev_sconv_b"]),
        "b_r": k_(a["ev_b_r"][0]), "b_i": k_(a["ev_b_i"][0]), "lam": k_(a["ev_lam"][0]),
        "od_scale": f(a["od_scale"]), "final_g": f(a["final_g"]), "norm1_g": f(a["norm1_g_2"]),
        "conv_a_w": k_(a["conv_a_w_2"][0]), "ssm_conv_w": k_(a["ssm_conv_w_2"][0]), "ssm_conv_b": f(a["ssm_conv_b_2"]),
        "dt_bias": rep(a["ssm_dt_bias_2"][0]), "a_log": rep(a["ssm_a_log_2"][0]),
        "ssm_d": f(np.repeat(a["ssm_d_2"][0], HD)), "ssm_norm_g": f(a["ssm_norm_g_2"]),
        "norm2_g": f(a["norm2_g_2"]), "final_g2": f(a["final_g_2"]),
        "w_dt": wdt.reshape(NT, P, NH).transpose(1, 0, 2).reshape(P, NT * NH),
    }
    order = sorted(VC, key=VC.get)
    vecs = np.ascontiguousarray(np.concatenate([vals[n] for n in order], 1))
    assert vecs.shape == (P, NVEC), vecs.shape
    xt = lambda x, t: np.ascontiguousarray(x[0].reshape(t, NT, P).transpose(2, 1, 0).reshape(P, NT * t))
    return {"weights": weights, "modw": np.ascontiguousarray(modw), "vecs": vecs, "consts": constants(),
            "x_in": xt(a["x"], T), "ctx_in": xt(a["ctx"], TC)}


def kernel(**inputs):
    import concourse.bacc as bacc
    from concourse.bass_utils import run_bass_kernel_spmd

    arrays = lay_out({k: np.asarray(v) for k, v in inputs.items()})
    nc = bacc.Bacc("TRN2", target_bir_lowering=False, num_devices=1)
    args = [nc.dram_tensor(n, v.shape, F32, kind="ExternalInput").ap() for n, v in arrays.items()]
    out = nc.dram_tensor("out", (P, NT * T), F32, kind="ExternalOutput").ap()
    program(nc, *args, out)
    r = run_bass_kernel_spmd(nc, [arrays], core_ids=[0])
    y = r.results[0]["out"]
    return y.reshape(P, NT, T).transpose(2, 1, 0).reshape(1, T, D)
```
